# Optimizing a Trainium2 kernel written in Bass

```python
import jax, jax.numpy as jnp
from jax import lax
import numpy as np

D_MODEL = 1024
BATCH = 1
SEQ = 2048
DEPTH = 1
DEC_BATCH = 8
DEC_SEQ = 4
PAST_LEN = 4096
PAGE_SIZE = 128

N_HEADS = 8
N_KV_HEADS = 2
HEAD_DIM = 64
GROUP = N_HEADS // N_KV_HEADS
ATTN_W = N_HEADS * HEAD_DIM
KV_W = N_KV_HEADS * HEAD_DIM
WINDOW = 128
LRU_W = D_MODEL // 2
LRU_BLOCKS = 8
LRU_BW = LRU_W // LRU_BLOCKS
CONV_W = 4
LRU_C = 8.0
MIX_W = ATTN_W + LRU_W
IN_W = ATTN_W + 2 * KV_W + 2 * LRU_W
Q_END = ATTN_W
K_END = Q_END + KV_W
V_END = K_END + KV_W
X_END = V_END + LRU_W
D_FF = -(-8 * D_MODEL // (3 * 256)) * 256
EPS = 1e-6
NEG = -1e30

kernel_name = "hymba_swa_sink_rglru_decoder_step"

def _rmsnorm(x, g):
    xf = x.astype(jnp.float32)
    y = xf * lax.rsqrt(jnp.mean(xf * xf, axis=-1, keepdims=True) + EPS) * g.astype(jnp.float32)
    return y.astype(x.dtype)

def _alibi_slopes():
    return jnp.exp2(-8.0 * jnp.arange(1, N_HEADS + 1, dtype=jnp.float32) / N_HEADS)

def _sink_attend(q, kb, vb, dist, sinks):
    s = jnp.einsum('bnqkgd,bnskd->bnkgqs', q, kb).astype(jnp.float32) * (HEAD_DIM ** -0.5)
    slopes = _alibi_slopes().reshape(N_KV_HEADS, GROUP, 1, 1)
    valid = ((dist >= 0) & (dist < WINDOW))[None, :, None, None]
    distf = dist.astype(jnp.float32)[None, :, None, None]
    s = jnp.where(valid, s - slopes * distf, NEG)
    sink = sinks.astype(jnp.float32).reshape(N_KV_HEADS, GROUP, 1, 1)
    m = jnp.maximum(jnp.max(s, axis=-1, keepdims=True), sink)
    p = jnp.exp(s - m)
    p = p / (jnp.sum(p, axis=-1, keepdims=True) + jnp.exp(sink - m))
    out = jnp.einsum('bnkgqs,bnskd->bnqkgd', p.astype(vb.dtype), vb)
    B, n, Tq = out.shape[:3]
    return out.reshape(B, n * Tq, ATTN_W)

def _attn_prompt(q, k, v, sinks):
    B, T = q.shape[:2]
    nb = T // WINDOW
    qb = q.reshape(B, nb, WINDOW, N_KV_HEADS, GROUP, HEAD_DIM)

    def band(t):
        tb = t.reshape(B, nb, WINDOW, N_KV_HEADS, HEAD_DIM)
        prev = jnp.pad(tb[:, :-1], ((0, 0), (1, 0), (0, 0), (0, 0), (0, 0)))
        return jnp.concatenate([prev, tb], axis=2)

    i = jnp.arange(WINDOW)[:, None]
    j = jnp.arange(2 * WINDOW)[None, :]
    d = WINDOW + i - j
    first = (jnp.arange(nb)[:, None, None] == 0) & (j[None] < WINDOW)
    dist = jnp.where(first, -1, d[None])
    out = _sink_attend(qb, band(k), band(v), dist, sinks)
    return out, k[:, -WINDOW:], v[:, -WINDOW:]

def _attn_sample(q, k, v, ck, cv, sinks):
    T = q.shape[1]
    kall = jnp.concatenate([ck.astype(k.dtype), k], axis=1)
    vall = jnp.concatenate([cv.astype(v.dtype), v], axis=1)
    i = jnp.arange(T)[:, None]
    j = jnp.arange(WINDOW + T)[None, :]
    dist = (WINDOW + i - j)[None]
    out = _sink_attend(q[:, None], kall[:, None], vall[:, None], dist, sinks)
    return out, kall[:, -WINDOW:], vall[:, -WINDOW:]

def _causal_conv(x, prefix, w, b):
    T = x.shape[1]
    xp = jnp.concatenate([prefix.astype(x.dtype), x], axis=1)
    out = b + w[0] * xp[:, 0:T]
    for kk in range(1, CONV_W):
        out = out + w[kk] * xp[:, kk:kk + T]
    return out, xp[:, T:]

def _block_diag(x, w, b):
    B, T = x.shape[:2]
    xr = x.reshape(B, T, LRU_BLOCKS, LRU_BW)
    return jnp.einsum('btnd,nde->btne', xr, w).reshape(B, T, LRU_W) + b

def _rg_lru(x, h0, w_a, b_a, w_i, b_i, lam):
    xf = x.astype(jnp.float32)
    r = jax.nn.sigmoid(_block_diag(x, w_a, b_a).astype(jnp.float32))
    ig = jax.nn.sigmoid(_block_diag(x, w_i, b_i).astype(jnp.float32))
    log_a = -LRU_C * r * jax.nn.softplus(-lam.astype(jnp.float32))
    a = jnp.exp(log_a)
    bterm = jnp.sqrt(-jnp.expm1(2.0 * log_a)) * (ig * xf)

    def step(h, ab):
        a_t, b_t = ab
        h = a_t * h + b_t
        return h, h

    h_last, hs = lax.scan(step, h0.astype(jnp.float32), (jnp.swapaxes(a, 0, 1), jnp.swapaxes(bterm, 0, 1)))
    return jnp.swapaxes(hs, 0, 1).astype(x.dtype), h_last

def _layer(x, mode, ck, cv, conv_prefix, h0, g_mix, w_in, b_in, attn_sinks, conv_w, conv_b,
           w_a, b_a, w_i, b_i, lam, w_out, b_out, g_ffn, w_ffn_in, w_ffn_out):
    B, T, _ = x.shape
    u = _rmsnorm(x, g_mix)
    z = u @ w_in + b_in
    q, k, v, xb, yb = jnp.split(z, [Q_END, K_END, V_END, X_END], axis=-1)
    q = q.reshape(B, T, N_KV_HEADS, GROUP, HEAD_DIM)
    k = k.reshape(B, T, N_KV_HEADS, HEAD_DIM)
    v = v.reshape(B, T, N_KV_HEADS, HEAD_DIM)
    if mode == 'prompt':
        attn, nk, nv = _attn_prompt(q, k, v, attn_sinks)
    else:
        attn, nk, nv = _attn_sample(q, k, v, ck, cv, attn_sinks)
    xc, nconv = _causal_conv(xb, conv_prefix, conv_w, conv_b)
    lru, nh = _rg_lru(xc, h0, w_a, b_a, w_i, b_i, lam)
    mix = jnp.concatenate([attn, lru * jax.nn.gelu(yb)], axis=-1)
    h = x + mix @ w_out + b_out
    gate, up = jnp.split(_rmsnorm(h, g_ffn) @ w_ffn_in, [D_FF], axis=-1)
    y = h + (jax.nn.silu(gate) * up) @ w_ffn_out
    return y, nk, nv, nconv, nh

def setup_inputs(seed: int = 0) -> dict:
    key = jax.random.key(seed)
    ks = jax.random.split(key, 23)

    def nrm(k, shape, scale):
        return jax.random.normal(k, shape, jnp.float32) * scale

    u = jax.random.uniform(ks[16], (DEPTH, LRU_W), jnp.float32, minval=0.9, maxval=0.999)
    return {
        'x_prompt': nrm(ks[0], (BATCH, SEQ, D_MODEL), 1.0),
        'x_sample': nrm(ks[1], (DEC_BATCH, DEC_SEQ, D_MODEL), 1.0),
        'cache_k': nrm(ks[2], (DEPTH, DEC_BATCH, WINDOW, N_KV_HEADS, HEAD_DIM), 1.0),
        'cache_v': nrm(ks[3], (DEPTH, DEC_BATCH, WINDOW, N_KV_HEADS, HEAD_DIM), 1.0),
        'state_conv': nrm(ks[4], (DEPTH, DEC_BATCH, CONV_W - 1, LRU_W), 1.0),
        'state_h': nrm(ks[5], (DEPTH, DEC_BATCH, LRU_W), 0.5),
        'g_mix': 1.0 + nrm(ks[6], (DEPTH, D_MODEL), 0.02),
        'w_in': nrm(ks[7], (DEPTH, D_MODEL, IN_W), D_MODEL ** -0.5),
        'b_in': nrm(ks[8], (DEPTH, IN_W), 0.02),
        'attn_sinks': nrm(ks[9], (DEPTH, N_HEADS), 0.5),
        'conv_w': nrm(ks[10], (DEPTH, CONV_W, LRU_W), CONV_W ** -0.5),
        'conv_b': nrm(ks[11], (DEPTH, LRU_W), 0.02),
        'w_a': nrm(ks[12], (DEPTH, LRU_BLOCKS, LRU_BW, LRU_BW), LRU_BW ** -0.5),
        'b_a': nrm(ks[13], (DEPTH, LRU_W), 0.02),
        'w_i': nrm(ks[14], (DEPTH, LRU_BLOCKS, LRU_BW, LRU_BW), LRU_BW ** -0.5),
        'b_i': nrm(ks[15], (DEPTH, LRU_W), 0.02),
        'lam': jnp.log(u) - jnp.log1p(-u),
        'w_out': nrm(ks[17], (DEPTH, MIX_W, D_MODEL), MIX_W ** -0.5),
        'b_out': nrm(ks[18], (DEPTH, D_MODEL), 0.02),
        'g_ffn': 1.0 + nrm(ks[19], (DEPTH, D_MODEL), 0.02),
        'w_ffn_in': nrm(ks[20], (DEPTH, D_MODEL, 2 * D_FF), D_MODEL ** -0.5),
        'w_ffn_out': nrm(ks[21], (DEPTH, D_FF, D_MODEL), D_FF ** -0.5),
        'g_final': 1.0 + nrm(ks[22], (D_MODEL,), 0.02),
    }

def reference(x_prompt, x_sample, cache_k, cache_v, state_conv, state_h, g_mix, w_in, b_in,
              attn_sinks, conv_w, conv_b, w_a, b_a, w_i, b_i, lam, w_out, b_out, g_ffn,
              w_ffn_in, w_ffn_out, g_final):
    yp, ys = x_prompt, x_sample
    pk, pv, pc, ph, sk, sv, sc, sh = [], [], [], [], [], [], [], []
    conv0 = jnp.zeros((x_prompt.shape[0], CONV_W - 1, LRU_W), x_prompt.dtype)
    h_zero = jnp.zeros((x_prompt.shape[0], LRU_W), jnp.float32)
    for l in range(DEPTH):
        lp = (g_mix[l], w_in[l], b_in[l], attn_sinks[l], conv_w[l], conv_b[l], w_a[l], b_a[l],
              w_i[l], b_i[l], lam[l], w_out[l], b_out[l], g_ffn[l], w_ffn_in[l], w_ffn_out[l])
        yp, k1, v1, c1, h1 = _layer(yp, 'prompt', None, None, conv0, h_zero, *lp)
        ys, k2, v2, c2, h2 = _layer(ys, 'sample', cache_k[l], cache_v[l], state_conv[l], state_h[l], *lp)
        pk.append(k1); pv.append(v1); pc.append(c1); ph.append(h1)
        sk.append(k2); sv.append(v2); sc.append(c2); sh.append(h2)
    y_prompt = _rmsnorm(yp, g_final)
    y_sample = _rmsnorm(ys, g_final)
    return (y_prompt, y_sample,
            jnp.stack(pk), jnp.stack(pv), jnp.stack(pc), jnp.stack(ph),
            jnp.stack(sk), jnp.stack(sv), jnp.stack(sc), jnp.stack(sh))


_drawn_inputs = setup_inputs


def setup_inputs(seed=0):
    import zlib

    import numpy as np

    out = dict(_drawn_inputs(seed))
    spreads = {}
    factors = {'attn_sinks': 3.665,
     'b_a': 8.0,
     'b_i': 7.953,
     'b_out': 2.689,
     'g_ffn': 3.973,
     'g_final': 2.824}
    for name, (base, spread) in spreads.items():
        noise = np.random.default_rng([zlib.crc32(name.encode()), seed]).standard_normal(out[name].shape)
        drawn = base * np.exp(spread * noise) if base else spread * noise
        out[name] = __import__('jax').numpy.asarray(drawn.astype(out[name].dtype))
    for name, factor in factors.items():
        out[name] = (out[name] * factor).astype(out[name].dtype)
    return out
```

```python
import concourse.bass as bass
from concourse import mybir
from contextlib import ExitStack

F32 = mybir.dt.float32
F32R = mybir.dt.float32r
ALU = mybir.AluOpType
ACT = mybir.ActivationFunctionType

P = 128
WINDOW = 128
HEAD = 64
EPS = 1e-6
GELU_K = 0.7978845608028654
GELU_C = 0.044715
CONV_W = 4
RING = 3


class Signal:

    def __init__(self, sem, per_block, step=1, primed=True):
        self.sem, self.per, self.step, self.primed = sem, per_block, step, primed

    def prime(self, eng):
        eng.sem_inc(self.sem, self.per * self.step)

    def wait(self, eng, b, k):
        eng.wait_ge(self.sem, (b * self.per + (self.per if self.primed else 0) + k) * self.step)

    def by(self, ins):
        ins.then_inc(self.sem, self.step)


class Chain:

    def __init__(self, eng, sem):
        self.eng, self.sem, self.n = eng, sem, 0

    def link(self, ins):
        ins.then_inc(self.sem, 1)
        self.n += 1
        self.eng.wait_ge(self.sem, self.n)

    def restart(self):
        if self.n:
            self.eng.sem_clear(self.sem)
            self.n = 0


def hymba_layer(nc, x_p, x_s, cache_k, cache_v, conv_in, h_in, units, vecs, w_a, w_i, sinks_p, sinks_s,
                g_fin, ident_in, dist_in, dist_s_in, per_row,
                y_p, y_s, nk_p, nv_p, nc_p, nh_p, nk_s, nv_s, nc_s, nh_s, d_ff):
    SEQ, DM = x_p.shape[1], x_p.shape[2]
    DB, DT = x_s.shape[0], x_s.shape[1]
    NS = DB * DT
    T = 512
    NB = SEQ // T
    W = T + NS
    QB = T // WINDOW
    KT = DM // P
    NKV = 2
    LC = conv_in.shape[3] // P
    NH = sinks_p.shape[1]
    JT = NH // NKV
    NF = d_ff // P
    FCH = []
    n = -(-NF // KT)
    for i in range(n):
        FCH.append(NF // n + (i < NF % n))
    HALF = T

    U_K, U_V = 0, 1
    U_Q = [2 + j for j in range(JT)]
    U_X = [2 + JT + 2 * c for c in range(LC)]
    U_Y = [3 + JT + 2 * c for c in range(LC)]
    U_O = [2 + JT + 2 * LC + m for m in range(KT)]
    U_IN, U_OUT, at = [], [], 2 + JT + 2 * LC + KT
    for nf in FCH:
        U_IN.append([(at + 2 * f, at + 2 * f + 1) for f in range(nf)])
        U_OUT.append([at + 2 * nf + m for m in range(KT)])
        at += 2 * nf + KT
    NU = at
    assert NU % RING == 0, (NU, NF, FCH)
    kt_of = [KT] * NU
    for nf, outs in zip(FCH, U_OUT):
        for u in outs:
            kt_of[u] = nf

    def chunks(last):
        return [(0, W // 2), (W // 2, W)] if last else [(0, T)]

    def job(u, c, last):
        return u * len(chunks(last)) + c

    by_act = [U_V] + U_X + U_Y
    def freed(u, c, last):
        act = u in by_act
        before = sum((v in by_act) == act for v in range(u))
        return act, before * len(chunks(last)) + c + 1

    ctx = ExitStack()
    with ctx:
        ctx.enter_context(nc.allow_non_contiguous_dma("small state vectors"))

        top = [-(-nc.sbuf_base // 64) * 64]

        def place(name, shape, dt=F32, at=None):
            size = 4
            for s in shape[1:]:
                size *= s
            size = -(-size // 64) * 64
            where = top[0] if at is None else at[0]
            t = nc.alloc_sbuf_tensor_at(name, list(shape), dt, offset=where)
            if at is None:
                top[0] += size
            else:
                at[0] += size
            return t

        w_raw = place("w_raw", [P, RING, KT * P])
        w_hi = place("w_hi", [P, RING, KT * P], F32R)
        w_lo = place("w_lo", [P, RING, KT * P], F32R)
        hT = place("hT", [P, KT, W])
        a_at = [top[0]]
        a_hi = place("a_hi", [P, KT, W], F32R)
        a_lo = place("a_lo", [P, KT, W], F32R)
        x_hi = place("x_hi", [P, KT, W], F32R)
        x_lo = place("x_lo", [P, KT, W], F32R)
        qT = place("qT", [P, JT, W])
        kT = place("kT", [P, WINDOW + W])
        vT = place("vT", [P, W])
        v_tok = place("v_tok", [P, 1 + QB, P])
        ident = place("ident", [P, P])
        ones = place("ones", [P, P])
        dist = place("dist", [P, 2 * WINDOW])
        dist_b = place("dist_b", [P, 2 * WINDOW])
        sinks = place("sinks", [P, NH])
        gates_w = place("gates_w", [P, 2, LC, P])
        gfin = place("gfin", [P, DM])
        vec = place("vec", [P, vecs.shape[1]])
        rows = place("rows", [P, 4])
        sink_s = place("sink_s", [P, NKV])
        lru_c = place("lru_c", [P, 3, LC])
        set_t = place("set_t", [P, 6, LC])
        eps_t = place("eps_t", [P, 1])
        x_prev = place("x_prev", [P, LC, CONV_W - 1])
        h_prev = place("h_prev", [P, LC])
        ssum = place("ssum", [P, W])
        std = place("std", [P, W])
        rinv = place("rinv", [P, W])
        mx = place("mx", [P, 2, NH // 2])
        nm = place("nm", [P, 2, NH // 2])
        sd = place("sd", [P, 2, NH // 2])
        rs = place("rs", [P, 2, NH // 2])
        es = place("es", [P, 2, NH // 2])
        rec = place("rec", [P, 2, NH])
        std_t = place("std_t", [P, QB + 1])
        rstd_t = place("rstd_t", [P, QB + 1])
        a_tok = place("a_tok", [P, NH * HEAD])
        xs_b = place("xs_b", [P, LC, (CONV_W - 1) * DB + NS])
        ys_b = place("ys_b", [P, LC, NS])
        HH = NH // 2

        r = top[0]
        x_tok = place("x_tok", [P, QB, DM])
        a2 = [r]
        s_p = place("s_p", [P, 2, HH, 2 * WINDOW], at=a2)
        pT = place("pT", [P, 2, HH * 2, P], at=a2)
        top[0] = max(top[0], a2[0])
        r = top[0]
        xb = place("xb", [P, 2, CONV_W - 1 + W])
        yb = place("yb", [P, 2, W])
        xc = place("xc", [P, 2, T])
        a2 = [r]
        sq = place("sq", [P, 2, W], at=a2)
        un = place("un", [P, 3, W], at=a2)
        a3 = [r]
        th = place("th", [P, 2, W], at=a3)
        gt = place("gt", [P, 2, W], at=a3)
        a32 = place("a32", [P, 2, W], at=a3)
        top[0] = max(top[0], a2[0], a3[0])
        r = top[0]
        gl = place("gl", [P, 2, T])
        ra = place("ra", [P, T])
        ii = place("ii", [P, T])
        qq = place("qq", [P, T])
        om = place("om", [P, T])
        a2 = [r]
        y_tok = place("y_tok", [P, 2, DM], at=a2)
        top[0] = max(top[0], a2[0])
        xs_tok = place("xs_tok", [NS, DM], at=[r])
        assert top[0] <= nc.sbuf_usable_end, top[0]

        SC = WINDOW + NS
        q_d = place("q_d", [P, DB, P], at=a_at)
        kc_tok = place("kc_tok", [P, DB, P], at=a_at)
        kc_T = place("kc_T", [P, DB, P], at=a_at)
        vc_tok = place("vc_tok", [P, DB, P], at=a_at)
        dist_s = place("dist_s", [P, SC], at=a_at)
        s_s = place("s_s", [P, NKV, SC], at=a_at)
        mx_s = place("mx_s", [P, 6, NKV], at=a_at)
        pcT = place("pcT", [P, NKV, P], at=a_at)
        pnT = place("pnT", [NS, NKV, P], at=a_at)
        q_r = place("q_r", [P, P], at=a_at)
        vs_tok = place("vs_tok", [NS, P], at=a_at)
        mixs = place("mixs", [P, KT, NS], at=a_at)
        xc_s = place("xc_s", [P, LC, NS], at=a_at)
        hs0 = place("hs0", [P, LC, DB], at=a_at)
        st_s = place("st_s", [(CONV_W - 1) * DB + DB, LC * P], at=a_at)
        l_s = [place(f"l_s{i}", [P, LC, NS], at=a_at) for i in range(6)]
        SCOLS = (DT - 1) * DB + DB + CONV_W - 1 + 1
        outc = place("outc", [P, LC, SCOLS], at=a_at)
        outr = place("outr", [SCOLS, LC * P], at=a_at)
        k_out = place("k_out", [P, P], at=a_at)
        ks_out = place("ks_out", [NS, P], at=a_at)

        bank = [ctx.enter_context(nc.psum_tensor(f"bank{i}", [P, 512], F32)) for i in range(8)]
        G = bank[0:3]
        S = bank[3:5]
        TB = bank[5:7]
        V = bank[7]

        def sem(name):
            return ctx.enter_context(nc.semaphore(name))

        raw_in = [Signal(sem(f"raw_in{i}"), NU // RING, 16) for i in range(RING)]
        w_hi_ready = Signal(sem("w_hi_ready"), NU)
        w_ready = Signal(sem("w_ready"), NU)
        gemm_done = Signal(sem("gemm_done"), NU)
        dve_freed = Signal(sem("dve_freed"), NU - len(by_act))
        act_freed = Signal(sem("act_freed"), len(by_act))
        x_in = Signal(sem("x_in"), QB, 16, primed=False)
        xT_done = Signal(sem("xT_done"), KT)
        sq_ready = Signal(sem("sq_ready"), 3 * KT)
        sq_added = Signal(sem("sq_added"), 3 * KT)
        stat_done = Signal(sem("stat_done"), 3)
        std_ready = Signal(sem("std_ready"), 3)
        un_ready = Signal(sem("un_ready"), 2 * KT)
        nhi_ready = Signal(sem("nhi_ready"), 2 * KT)
        norm_ready = Signal(sem("norm_ready"), 2 * KT)
        vT_done = Signal(sem("vT_done"), 1)
        v_ready = Signal(sem("v_ready"), 1)
        NUN = 2 * QB
        sc_done = Signal(sem("sc_done"), NUN)
        sc_read = Signal(sem("sc_read"), NUN)
        p_ready = Signal(sem("p_ready"), NUN)
        pT_done = Signal(sem("pT_done"), NUN)
        pTa_ready = Signal(sem("pTa_ready"), NUN)
        pTb_ready = Signal(sem("pTb_ready"), NUN)
        av_done = Signal(sem("av_done"), NUN)
        atok_ready = Signal(sem("atok_ready"), QB)
        attnT_done = Signal(sem("attnT_done"), QB)
        amix_hi = Signal(sem("amix_hi"), QB)
        amix_ready = Signal(sem("amix_ready"), QB)
        xc_ready = Signal(sem("xc_ready"), LC)
        gates_done = Signal(sem("gates_done"), LC)
        gates_read = Signal(sem("gates_read"), LC)
        gelu_in = Signal(sem("gelu_in"), LC)
        gelu_th = Signal(sem("gelu_th"), LC)
        lru_sqrt = Signal(sem("lru_sqrt"), LC)
        lmix_f = Signal(sem("lmix_f"), LC)
        lmix_hi = Signal(sem("lmix_hi"), LC)
        lmix_ready = Signal(sem("lmix_ready"), LC)
        gate_tanh = Signal(sem("gate_tanh"), NF)
        act_f = Signal(sem("act_f"), NF)
        act_hi = Signal(sem("act_hi"), NF)
        act_ready = Signal(sem("act_ready"), NF)
        yT_done = Signal(sem("yT_done"), QB)
        y_ready = Signal(sem("y_ready"), QB)
        y_out = [Signal(sem(f"y_out{i}"), QB // 2, 16) for i in range(2)]
        state_moved = Signal(sem("state_moved"), 1)
        const_in = sem("const_in")
        zeroed = sem("zeroed")
        setup_act = sem("setup_act")
        setup_done = sem("setup_done")
        xs_in = sem("xs_in")
        smp_in = sem("smp_in")
        smp_out = sem("smp_out")
        smp_pe = sem("smp_pe")
        smp_act = sem("smp_act")
        smp_dve = sem("smp_dve")
        dve_chain = sem("dve_chain")
        act_chain = sem("act_chain")

        VB = 0
        VG1 = VB + U_O[0]
        VBO = VG1 + KT
        VG2 = VBO + KT
        VCW = VG2 + KT
        VCB = VCW + CONV_W * LC
        VBA = VCB + LC
        VBI = VBA + LC
        VLAM = VBI + LC
        VQS = VLAM + LC

        def v(i):
            return vec[:, i:i + 1]

        N_CONST = 12

        def done(eng, b, u, c, last):
            gemm_done.wait(eng, b, u + 1 if u < 0 else job(u, c, last) + 1)

        block = ctx.enter_context(nc.Block())

        @block.sync
        def _(sp):
            for s in raw_in:
                s.prime(sp)

            def load_unit(b, u):
                w_ready.wait(sp, b, u - RING + 1)
                n = kt_of[u % NU] * P
                raw_in[u % RING].by(sp.dma_start(w_raw[:, u % RING, 0:n], units[u % NU, :, 0:n]))

            w_ready.wait(sp, 0, 0)
            for u in range(RING):
                load_unit(0, u)
            with sp.Fori(0, NB - 1) as b:
                for u in range(RING, NU + RING):
                    load_unit(b, u)
            for u in range(RING, NU):
                load_unit(NB - 1, u)

        @block.gpsimd
        def _(pool):
            nc.gpsimd.memset(gates_w[:, :, :, :], 0.0).then_inc(zeroed, 1)
            nc.gpsimd.memset(kT[:, :], 0.0).then_inc(zeroed, 1)
            nc.gpsimd.memset(v_tok[:, :, :], 0.0).then_inc(zeroed, 1)
            nc.gpsimd.memset(x_prev[:, :, :], 0.0).then_inc(zeroed, 1)
            nc.gpsimd.memset(h_prev[:, :], 0.0).then_inc(zeroed, 1)
            nc.gpsimd.memset(ones[:, :], 1.0).then_inc(zeroed, 1)
            nc.gpsimd.memset(eps_t[:, :], EPS).then_inc(zeroed, 1)

            def load_x(b):
                for m in range(QB):
                    x_in.by(pool.dma_start(x_tok[:, m, :], x_p[0, bass.ds(b * T + m * P, P), :]))

            load_x(0)
            for dst, src in ((ident[:, :], ident_in), (vec[:, :], vecs), (dist[:, :], dist_in[0]),
                             (dist_b[:, :], dist_in[1]), (sinks[:, :], sinks_p), (gfin[:, :], g_fin),
                             (rows[:, :], per_row), (sink_s[:, :], sinks_s)):
                pool.dma_start(dst, src).then_inc(const_in, 16)
            pool.wait_ge(zeroed, 1)
            for n, w in enumerate((w_a, w_i)):
                for half in range(2):
                    lo = half * HEAD
                    pool.dma_start(gates_w[lo:lo + HEAD, n, :, lo:lo + HEAD],
                                   w[0, half::2].rearrange("n d e -> d n e")).then_inc(const_in, 16)

            with pool.Fori(0, NB - 1) as b:
                amix_ready.wait(pool, b, QB)
                xT_done.wait(pool, b, KT)
                load_x(b + 1)
            b = NB - 1
            for o in y_out:
                o.wait(pool, b, 0)
            for t in range(DT):
                pool.dma_start(xs_tok[t * DB:(t + 1) * DB, :], x_s[:, t, :]).then_inc(xs_in, 16)
            done(pool, b, U_O[0] - 1, 1, True)
            for dst, src in ((kc_tok[:, :, :], cache_k[0].rearrange("b s g d -> s b (g d)")),
                             (vc_tok[:, :, :], cache_v[0].rearrange("b s g d -> s b (g d)")),
                             (dist_s[:, :], dist_s_in)):
                pool.dma_start(dst, src).then_inc(smp_in, 16)
            for t in range(CONV_W - 1):
                pool.dma_start(st_s[t * DB:(t + 1) * DB, :], conv_in[0, :, t, :]).then_inc(smp_in, 16)
            pool.dma_start(st_s[(CONV_W - 1) * DB:CONV_W * DB, :], h_in[0]).then_inc(smp_in, 16)
            for o, c in ((nk_s, cache_k), (nv_s, cache_v)):
                pool.dma_start(o[0, :, 0:WINDOW - DT].rearrange("b s g d -> b (s g d)"),
                               c[0, :, DT:WINDOW].rearrange("b s g d -> b (s g d)")).then_inc(smp_out, 16)
            n_out = 2
            pool.wait_ge(smp_dve, SMP_DVE_OUT)
            pool.dma_start(nv_p[0, 0].rearrange("s g d -> s (g d)"), v_tok[:, QB, :]).then_inc(smp_out, 16)
            pool.dma_start(nk_p[0, 0].rearrange("s g d -> s (g d)"), k_out[:, :]).then_inc(smp_out, 16)
            n_out += 2
            for t in range(DT):
                r0 = t * DB
                pool.dma_start(nk_s[0, :, WINDOW - DT + t].rearrange("b g d -> b (g d)"),
                               ks_out[r0:r0 + DB, :]).then_inc(smp_out, 16)
                pool.dma_start(nv_s[0, :, WINDOW - DT + t].rearrange("b g d -> b (g d)"),
                               vs_tok[r0:r0 + DB, :]).then_inc(smp_out, 16)
                n_out += 2
            r0 = 0
            for t in range(CONV_W - 1):
                pool.dma_start(nc_s[0, :, t], outr[r0:r0 + DB, :]).then_inc(smp_out, 16)
                r0 += DB
            pool.dma_start(nh_s[0], outr[r0:r0 + DB, :]).then_inc(smp_out, 16)
            r0 += DB
            pool.dma_start(nc_p[0, 0], outr[r0:r0 + CONV_W - 1, :]).then_inc(smp_out, 16)
            r0 += CONV_W - 1
            pool.dma_start(nh_p[0], outr[r0:r0 + 1, :]).then_inc(smp_out, 16)
            n_out += CONV_W - 1 + 3
            pool.wait_ge(smp_dve, SMP_DVE_Y)
            for t in range(DT):
                pool.dma_start(y_s[:, t, :], y_tok[t * DB:(t + 1) * DB, 0, :]).then_inc(smp_out, 16)
            n_out += DT
            pool.wait_ge(smp_out, 16 * n_out)
            for o in y_out:
                o.wait(pool, b, QB // 2)

        @block.tensor
        def _(pe):
            for s in (gemm_done, xT_done, stat_done, vT_done, sc_done, pT_done, av_done, attnT_done,
                      gates_done, yT_done):
                s.prime(pe)
            pe.wait_ge(const_in, 16 * N_CONST)
            pe.wait_ge(zeroed, 7)
            smp = [0]

            def smp_by(ins):
                smp[0] += 1
                ins.then_inc(smp_pe, 1)

            def gemm(b, last, u, hi, lo, tile_ready=None):
                w_ready.wait(pe, b, u + 1)
                for c, (c0, c1) in enumerate(chunks(last)):
                    j = job(u, c, last)
                    if j >= 3:
                        n = len(chunks(last))
                        act, k = freed((j - 3) // n, (j - 3) % n, last)
                    else:
                        act, k = freed(NU + j - 3, 0, False)
                        k -= act_freed.per if act else dve_freed.per
                    (act_freed if act else dve_freed).wait(pe, b, k)
                    out = G[j % 3][:, 0:c1 - c0]
                    for kt in range(kt_of[u]):
                        if tile_ready and c == 0:
                            tile_ready(kt)
                        h = w_hi[:, u % RING, kt * P:(kt + 1) * P]
                        l = w_lo[:, u % RING, kt * P:(kt + 1) * P]
                        nc.tensor.matmul(out, h, hi[:, kt, c0:c1], start=(kt == 0), stop=False)
                        nc.tensor.matmul(out, h, lo[:, kt, c0:c1], start=False, stop=False)
                        mm = nc.tensor.matmul(out, l, hi[:, kt, c0:c1], start=False, stop=(kt == kt_of[u] - 1))
                    gemm_done.by(mm)

            def stat_sum(b, last, which):
                sq_added.wait(pe, b, (which + 1) * KT)
                if which == 0:
                    std_ready.wait(pe, b, 0)
                else:
                    amix_ready.wait(pe, b, QB)
                cs = chunks(last)
                if last:
                    if which == 0:
                        sq_ready.wait(pe, b, KT)
                    else:
                        pe.wait_ge(smp_dve, SMP_DVE_OUT)
                for c, (c0, c1) in enumerate(cs):
                    mm = nc.tensor.matmul((V, TB[0])[c][:, 0:c1 - c0], ones[:, :], ssum[:, c0:c1],
                                          start=True, stop=True)
                stat_done.by(mm)

            def front(b, last):
                x_in.wait(pe, b, QB)
                xbank = [S[0], S[1], TB[0], TB[1]]
                if last:
                    pe.wait_ge(xs_in, 16 * DT)
                    std_ready.wait(pe, b, 0)
                    for kt in range(KT):
                        mm = nc.tensor.transpose(V[:, kt * NS:(kt + 1) * NS], xs_tok[:, kt * P:(kt + 1) * P],
                                                 ident[0:NS, 0:NS])
                    smp_by(mm)
                for kt in range(KT):
                    if kt < 4:
                        y_ready.wait(pe, b, 0)
                    else:
                        sq_ready.wait(pe, b, kt - 3)
                    for m in range(QB):
                        mm = nc.tensor.transpose(xbank[kt % 4][:, m * P:(m + 1) * P],
                                                 x_tok[:, m, kt * P:(kt + 1) * P], ident[:, :])
                    xT_done.by(mm)
                stat_sum(b, last, 0)

                gemm(b, last, U_K, a_hi, a_lo, lambda kt: norm_ready.wait(pe, b, kt + 1))
                for u in [U_V] + U_Q:
                    gemm(b, last, u, a_hi, a_lo)

                act, k = freed(U_V, len(chunks(last)) - 1, last)
                act_freed.wait(pe, b, k)
                sq_ready.wait(pe, b, KT)
                for m in range(QB):
                    mm = nc.tensor.transpose(TB[0][:, m * P:(m + 1) * P], vT[:, m * P:(m + 1) * P], ident[:, :])
                vT_done.by(mm)

                def scores(s):
                    qb, jp = s // 2, s % 2
                    if s == 0:
                        act, k = freed(U_Q[-1], len(chunks(last)) - 1, last)
                        dve_freed.wait(pe, b, k)
                        sq_ready.wait(pe, b, KT)
                    elif s % 2 == 0:
                        gates_read.wait(pe, b, s // 2)
                    else:
                        sc_read.wait(pe, b, s)
                    for g in range(NKV):
                        r = slice(g * HEAD, (g + 1) * HEAD)
                        for jj in range(2):
                            mm = nc.tensor.matmul(S[g][:, jj * 256:(jj + 1) * 256],
                                                  qT[r, 2 * jp + jj, qb * P:(qb + 1) * P],
                                                  kT[r, qb * P:qb * P + 2 * WINDOW], start=True, stop=True)
                    sc_done.by(mm)

                def probs_T(s):
                    p_ready.wait(pe, b, s + 1)
                    if s == 0:
                        v_ready.wait(pe, b, 1)
                    else:
                        pTa_ready.wait(pe, b, s)
                        pTb_ready.wait(pe, b, s)
                    for n in range(2 * HH):
                        mm = nc.tensor.transpose(TB[n // 4][:, n % 4 * P:(n % 4 + 1) * P],
                                                 s_p[:, s % 2, n // 2, n % 2 * P:(n % 2 + 1) * P], ident[:, :])
                    pT_done.by(mm)

                def attend(s):
                    qb, jp = s // 2, s % 2
                    pTa_ready.wait(pe, b, s + 1)
                    pTb_ready.wait(pe, b, s + 1)
                    if s == 0:
                        std_ready.wait(pe, b, 1)
                    elif jp == 0:
                        amix_ready.wait(pe, b, qb)
                    for hh in range(HH):
                        g, jj = hh // 2, hh % 2
                        head = g * JT + 2 * jp + jj
                        for half in range(2):
                            mm = nc.tensor.matmul(V[:, head * HEAD:(head + 1) * HEAD],
                                                  pT[:, s % 2, 2 * hh + half, :],
                                                  v_tok[:, qb + half, g * HEAD:(g + 1) * HEAD],
                                                  start=(half == 0), stop=(half == 1))
                    av_done.by(mm)

                def attn_T(qb):
                    atok_ready.wait(pe, b, qb + 1)
                    for c in range(4):
                        mm = nc.tensor.transpose(V[:, c * P:(c + 1) * P], a_tok[:, c * P:(c + 1) * P], ident[:, :])
                    attnT_done.by(mm)

                def gates(c):
                    xc_ready.wait(pe, b, c + 1)
                    sc_read.wait(pe, b, 2 * c + 2)
                    for n in range(2):
                        mm = nc.tensor.matmul(S[n][:, :], gates_w[:, n, c, :], xc[:, c % 2, :],
                                              start=True, stop=True)
                    gates_done.by(mm)

                for s in range(NUN + 3):
                    if s >= 4 and s % 2 == 0:
                        attn_T((s - 4) // 2)
                    if s < NUN:
                        gemm(b, last, U_X[0] + s, a_hi, a_lo)
                        scores(s)
                    if 1 <= s <= NUN:
                        probs_T(s - 1)
                    if 2 <= s <= NUN + 1:
                        attend(s - 2)
                    if s % 2 == 1 and s < NUN:
                        gates(s // 2)

                if last:
                    sample_pe(b)

                def mix_ready(kt):
                    if kt == 0:
                        amix_ready.wait(pe, b, QB)
                        if last:
                            pe.wait_ge(smp_dve, SMP_DVE_MIX)
                    if kt >= KT - LC:
                        lmix_ready.wait(pe, b, kt - (KT - LC) + 1)

                gemm(b, last, U_O[0], x_hi, x_lo, mix_ready)
                for u in U_O[1:]:
                    gemm(b, last, u, x_hi, x_lo)

            def sample_pe(b):
                pe.wait_ge(smp_in, 16 * 7)
                gates_read.wait(pe, b, LC)
                R = CONV_W * DB
                for c in range(LC):
                    mm = nc.tensor.transpose(S[0][:, c * R:(c + 1) * R], st_s[:, c * P:(c + 1) * P], ident[0:R, 0:R])
                smp_by(mm)
                pTa_ready.wait(pe, b, NUN)
                pTb_ready.wait(pe, b, NUN)
                for bb in range(DB):
                    mm = nc.tensor.transpose(TB[bb // 4][:, bb % 4 * P:(bb % 4 + 1) * P], kc_tok[:, bb, :], ident[:, :])
                smp_by(mm)
                amix_ready.wait(pe, b, QB)
                nc.tensor.transpose(V[0:NS, 0:P], vT[:, T:W], ident[:, :])
                nc.tensor.transpose(V[0:NS, P:2 * P], kT[:, WINDOW + T:WINDOW + W], ident[:, :])
                smp_by(nc.tensor.transpose(V[:, 2 * P:3 * P], kT[:, T:T + WINDOW], ident[:, :]))
                pe.wait_ge(smp_dve, SMP_DVE_Q)
                for g in range(NKV):
                    r = slice(g * HEAD, (g + 1) * HEAD)
                    for bb in range(DB):
                        nc.tensor.matmul(S[g][:, 0:WINDOW], q_d[r, bb, :], kc_T[r, bb, :],
                                         start=(bb == 0), stop=(bb == DB - 1))
                    mm = nc.tensor.matmul(S[g][:, WINDOW:SC], q_r[r, :], kT[r, WINDOW + T:WINDOW + W],
                                          start=False, stop=True, skip_group_check=True)
                smp_by(mm)
                pe.wait_ge(smp_dve, SMP_DVE_P)
                for g in range(NKV):
                    nc.tensor.transpose(TB[0][:, g * P:(g + 1) * P], s_s[:, g, 0:WINDOW], ident[:, :])
                    mm = nc.tensor.transpose(TB[1][0:NS, g * P:(g + 1) * P], s_s[:, g, WINDOW:SC], ident[:, :])
                smp_by(mm)
                pe.wait_ge(smp_dve, SMP_DVE_PT)
                for g in range(NKV):
                    d = slice(g * HEAD, (g + 1) * HEAD)
                    o = (V, TB[0])[g]
                    for bb in range(DB):
                        rr = slice(bb * DT * JT, (bb + 1) * DT * JT)
                        nc.tensor.matmul(o[0:HEAD, rr], vc_tok[:, bb, d], pcT[:, g, rr],
                                         start=(bb == 0), stop=(bb == DB - 1), skip_group_check=True)
                    mm = nc.tensor.matmul(o[0:HEAD, 0:P], vs_tok[:, d], pnT[:, g, :], start=False, stop=True,
                                          skip_group_check=True)
                smp_by(mm)
                pe.wait_ge(smp_dve, SMP_DVE_XC)
                for n in range(2):
                    for c in range(LC):
                        mm = nc.tensor.matmul(S[n][:, c * NS:(c + 1) * NS], gates_w[:, n, c, :], xc_s[:, c, :],
                                              start=True, stop=True)
                smp_by(mm)
                pe.wait_ge(smp_dve, SMP_DVE_OUTC)
                for c in range(LC):
                    mm = nc.tensor.transpose(TB[1][0:SCOLS, c * P:(c + 1) * P], outc[:, c, :], ident[:, :])
                smp_by(mm)

            def back(b, last):
                stat_sum(b, last, 1)
                f0 = 0
                for ci, nf in enumerate(FCH):
                    for f, (ug, uu) in enumerate(U_IN[ci]):
                        first = ci == 0 and f == 0
                        gemm(b, last, ug, x_hi, x_lo,
                             (lambda kt: norm_ready.wait(pe, b, KT + kt + 1)) if first else None)
                        gemm(b, last, uu, x_hi, x_lo)
                    for m, u in enumerate(U_OUT[ci]):
                        gemm(b, last, u, a_hi, a_lo,
                             (lambda kt, f0=f0: act_ready.wait(pe, b, f0 + kt + 1)) if m == 0 else None)
                    f0 += nf
                sq_added.wait(pe, b, 3 * KT)
                std_ready.wait(pe, b, 2)
                for m in range(QB):
                    mm = nc.tensor.matmul(V[:, m:m + 1], ssum[:, m * P:(m + 1) * P], ones[:, 0:1], start=True, stop=True)
                if last:
                    mm = nc.tensor.matmul(V[0:NS, QB:QB + 1], ssum[:, T:W], ones[:, 0:1], start=True, stop=True)
                stat_done.by(mm)
                for m in range(QB):
                    if m >= 2:
                        y_ready.wait(pe, b, m - 1)
                    o = (S, TB)[m % 2]
                    for kt in range(KT):
                        mm = nc.tensor.transpose(o[kt // 4][:, kt % 4 * P:(kt % 4 + 1) * P],
                                                 hT[:, kt, m * P:(m + 1) * P], ident[:, :])
                    yT_done.by(mm)
                if last:
                    y_ready.wait(pe, b, 3)
                    for kt in range(KT):
                        mm = nc.tensor.transpose(S[kt // 4][0:NS, kt % 4 * P:(kt % 4 + 1) * P],
                                                 hT[:, kt, T:W], ident[:, :])
                    smp_by(mm)

            with pe.Fori(0, NB - 1) as b:
                front(b, False)
                back(b, False)
            front(NB - 1, True)
            back(NB - 1, True)

        @block.scalar
        def _(act):
            for s in (w_hi_ready, act_freed, sq_ready, std_ready, nhi_ready, p_ready, pTa_ready, amix_hi,
                      gates_read, gelu_th, lru_sqrt, lmix_hi, gate_tanh, act_hi, *y_out):
                s.prime(act)
            chain = Chain(act, act_chain)
            smp = [0]

            def smp_by(ins):
                smp[0] += 1
                ins.then_inc(smp_act, 1)

            A = nc.scalar.activation
            act.wait_ge(const_in, 16 * N_CONST)
            act.wait_ge(zeroed, 7)
            act.wait_ge(setup_done, 1)
            A(set_t[:, 1, :], set_t[:, 0, :], ACT.Exp, scale=-1.0).then_inc(setup_act, 1)
            act.wait_ge(setup_done, 2)

            def split(b, last, u, end=False):
                if end and u >= NU:
                    return
                raw_in[u % RING].wait(act, b, u // RING + 1)
                nch = len(chunks(last))
                done(act, b, u - RING, nch - 1, last)
                n = kt_of[u % NU] * P
                w_hi_ready.by(A(w_hi[:, u % RING, 0:n], w_raw[:, u % RING, 0:n], ACT.Copy))

            def turn(b, last, u):
                done(act, b, u, len(chunks(last)) - 1, last)
                split(b, last, u + RING, last)

            def squares(b, last, which, hT_ready=None):
                w = W if last else T
                for kt in range(KT):
                    if hT_ready:
                        hT_ready(kt)
                    sq_added.wait(act, b, which * KT + kt - 1)
                    sq_ready.by(A(sq[:, kt % 2, 0:w], hT[:, kt, 0:w], ACT.Square))

            def norm_std(b, last, which):
                stat_done.wait(act, b, which + 1)
                for c, (c0, c1) in enumerate(chunks(last)):
                    ins = A(std[:, c0:c1], (V, TB[0])[c][:, 0:c1 - c0], ACT.Sqrt, bias=eps_t[:, 0:1], scale=1.0 / DM)
                std_ready.by(ins)

            def norm_hi(b, last, which, dst, g0):
                w = W if last else T
                for kt in range(KT):
                    un_ready.wait(act, b, which * KT + kt + 1)
                    nhi_ready.by(A(dst[:, kt, 0:w], un[:, kt % 3, 0:w], ACT.Copy, scale=v(g0 + kt)))

            def front(b, last):
                xbank = [S[0], S[1], TB[0], TB[1]]
                if last:
                    act.wait_ge(smp_pe, 1)
                    chain.link(A(hT[:, :, T:W], V[:, 0:KT * NS].rearrange("p (k n) -> p k n", k=KT), ACT.Copy))
                for kt in range(KT):
                    xT_done.wait(act, b, kt + 1)
                    chain.link(A(hT[:, kt, 0:T], xbank[kt % 4][:, :], ACT.Copy))
                    sq_added.wait(act, b, kt - 1)
                    w = W if last else T
                    sq_ready.by(A(sq[:, kt % 2, 0:w], hT[:, kt, 0:w], ACT.Square))
                norm_std(b, last, 0)
                norm_hi(b, last, 0, a_hi, VG1)
                for o in y_out:
                    o.wait(act, b, 0)
                for u in [U_K, U_V] + U_Q:
                    if u == U_V:
                        for c, (c0, c1) in enumerate(chunks(last)):
                            done(act, b, u, c, last)
                            act_freed.by(A(vT[:, c0:c1], G[job(u, c, last) % 3][:, 0:c1 - c0], ACT.Identity,
                                           bias=v(VB + u)))
                    turn(b, last, u)

                def exps(s):
                    sc_read.wait(act, b, s + 1)
                    for hh in range(HH):
                        A(s_p[:, s % 2, hh, :], s_p[:, s % 2, hh, :], ACT.Exp, bias=nm[:, s % 2, hh:hh + 1],
                          accum_out=rs[:, s % 2, hh:hh + 1])
                    p_ready.by(A(es[:, s % 2, :], sd[:, s % 2, :], ACT.Exp))

                def probs_T(s):
                    pT_done.wait(act, b, s + 1)
                    av_done.wait(act, b, s - 1)
                    pTa_ready.by(A(pT[:, s % 2, 0:4, :], TB[0][:, :].rearrange("p (n q) -> p n q", n=4), ACT.Copy))

                def lru_1(c):
                    gelu_in.wait(act, b, c + 1)
                    gelu_th.by(A(gl[:, c % 2, :], gl[:, c % 2, :], ACT.Tanh))
                    gates_done.wait(act, b, c + 1)
                    lmix_f.wait(act, b, c)
                    chain.link(A(ra[:, :], S[0][:, :], ACT.Tanh, bias=lru_c[:, 0, c:c + 1], scale=0.5))
                    gates_read.by(A(ii[:, :], S[1][:, :], ACT.Tanh, bias=lru_c[:, 1, c:c + 1], scale=0.5))
                    chain.link(A(ra[:, :], ra[:, :], ACT.Tanh, bias=lru_c[:, 2, c:c + 1], scale=lru_c[:, 2, c:c + 1]))
                    lru_sqrt.by(A(qq[:, :], ra[:, :], ACT.Sqrt, scale=-1.0))

                def lru_2(c):
                    lmix_f.wait(act, b, c + 1)
                    lmix_hi.by(A(x_hi[:, KT - LC + c, 0:T], gl[:, c % 2, :], ACT.Copy))

                for s in range(NUN + 3):
                    if s >= 4 and s % 2 == 0:
                        qb = (s - 4) // 2
                        attnT_done.wait(act, b, qb + 1)
                        amix_hi.by(A(x_hi[:, 0:4, qb * P:(qb + 1) * P],
                                     V[:, :].rearrange("p (c q) -> p c q", c=4), ACT.Copy))
                    if s < NUN:
                        u, c = U_X[0] + s, s // 2
                        for n, (c0, c1) in enumerate(chunks(last)):
                            done(act, b, u, n, last)
                            src = G[job(u, n, last) % 3][:, 0:c1 - c0]
                            if s % 2 == 0:
                                xc_ready.wait(act, b, c - 1)
                                act_freed.by(A(xb[:, c % 2, CONV_W - 1 + c0:CONV_W - 1 + c1], src, ACT.Identity,
                                               bias=v(VB + u)))
                            else:
                                lmix_ready.wait(act, b, c - 1)
                                A(yb[:, c % 2, c0:c1], src, ACT.Identity, bias=v(VB + u))
                                c2 = min(c1, T)
                                act_freed.by(A(gl[:, c % 2, c0:c2], src[:, 0:c2 - c0], ACT.Square, bias=v(VB + u)))
                        turn(b, last, u)
                    if 2 <= s and s % 2 == 0 and s // 2 - 1 < LC:
                        lru_1(s // 2 - 1)
                    if s < NUN:
                        exps(s)
                    if 1 <= s <= NUN:
                        probs_T(s - 1)
                    if s >= 3 and s % 2 == 1 and (s - 3) // 2 < LC:
                        lru_2((s - 3) // 2)
                if last:
                    sample_act(b)
                for u in U_O:
                    turn(b, last, u)

            def sample_act(b):
                act.wait_ge(smp_dve, SMP_DVE_S)
                for g in range(NKV):
                    A(s_s[:, g, :], s_s[:, g, :], ACT.Exp, bias=mx_s[:, 1, g:g + 1], accum_out=mx_s[:, 2, g:g + 1])
                smp_by(A(mx_s[:, 3, :], mx_s[:, 4, :], ACT.Exp))
                act.wait_ge(smp_pe, 8)
                for n in range(2):
                    for c in range(LC):
                        ins = A(l_s[n][:, c, :], S[n][:, c * NS:(c + 1) * NS], ACT.Tanh,
                                bias=lru_c[:, n, c:c + 1], scale=0.5)
                chain.link(ins)
                for c in range(LC):
                    ins = A(l_s[0][:, c, :], l_s[0][:, c, :], ACT.Tanh, bias=lru_c[:, 2, c:c + 1],
                            scale=lru_c[:, 2, c:c + 1])
                chain.link(ins)
                act.wait_ge(smp_dve, SMP_DVE_GI)
                A(l_s[4][:, :, :], l_s[4][:, :, :], ACT.Tanh)
                smp_by(A(l_s[2][:, :, :], l_s[0][:, :, :], ACT.Sqrt, scale=-1.0))
                act.wait_ge(smp_dve, SMP_DVE_MIXF)
                smp_by(A(x_hi[:, :, T:W], mixs[:, :, :], ACT.Copy))

            def back(b, last):
                nch = len(chunks(last))

                def h_ready(kt):
                    act_, k = freed(U_O[kt], nch - 1, last)
                    dve_freed.wait(act, b, k)
                squares(b, last, 1, h_ready)
                norm_std(b, last, 1)
                norm_hi(b, last, 1, x_hi, VG2)
                w = W if last else T
                f0 = 0
                for ci, nf in enumerate(FCH):
                    for f, (ug, uu) in enumerate(U_IN[ci]):
                        n = f0 + f
                        act_ready.wait(act, b, n - 1)
                        for c, (c0, c1) in enumerate(chunks(last)):
                            done(act, b, ug, c, last)
                            ins = A(th[:, n % 2, c0:c1], G[job(ug, c, last) % 3][:, 0:c1 - c0], ACT.Tanh, scale=0.5)
                            if c == nch - 1:
                                gate_tanh.by(ins)
                            else:
                                chain.link(ins)
                        split(b, last, ug + RING, last)
                        turn(b, last, uu)
                        act_f.wait(act, b, n + 1)
                        act_hi.by(A(a_hi[:, f, 0:w], a32[:, n % 2, 0:w], ACT.Copy))
                    for u in U_OUT[ci]:
                        turn(b, last, u)
                    f0 += nf

                def y_in(kt):
                    act_, k = freed(U_OUT[-1][kt], nch - 1, last)
                    dve_freed.wait(act, b, k)
                squares(b, last, 2, y_in)
                stat_done.wait(act, b, 3)
                if last:
                    A(std_t[0:NS, QB:QB + 1], V[0:NS, QB:QB + 1], ACT.Sqrt, bias=eps_t[0:NS, 0:1], scale=1.0 / DM)
                std_ready.by(A(std_t[:, 0:QB], V[:, 0:QB], ACT.Sqrt, bias=eps_t[:, 0:1], scale=1.0 / DM))
                for m in range(QB):
                    y_ready.wait(act, b, m + 1)
                    y_out[m % 2].by(act.dma_start(y_p[0, bass.ds(b * T + m * P, P), :], y_tok[:, m % 2, :]))

            for u in range(RING):
                split(0, False, u)
            with act.Fori(0, NB - 1) as b:
                chain.restart()
                front(b, False)
                back(b, False)
                chain_n = chain.n
                act.sem_clear(act_chain)
                chain.n = 0
            front(NB - 1, True)
            back(NB - 1, True)

        @block.vector
        def _(dve):
            for s in (w_ready, dve_freed, sq_added, un_ready, norm_ready, v_ready, sc_read, pTb_ready,
                      atok_ready, amix_ready, xc_ready, gelu_in, lmix_f, lmix_ready, act_f, act_ready,
                      y_ready, state_moved):
                s.prime(dve)
            chain = Chain(dve, dve_chain)
            link = chain.link
            TT = nc.vector.tensor_tensor
            TS = nc.vector.tensor_scalar
            STT = nc.vector.scalar_tensor_tensor
            dve.wait_ge(const_in, 16 * N_CONST)
            dve.wait_ge(zeroed, 7)

            lam = vec[:, VLAM:VLAM + LC]
            link(TS(set_t[:, 5, :], lam, -1.0, None, ALU.mult))
            TT(set_t[:, 0, :], set_t[:, 5, :], lam, ALU.max).then_inc(setup_done, 1)
            dve.wait_ge(setup_act, 1)
            e = set_t[:, 1, :]
            link(TS(set_t[:, 2, :], e, 2.0, None, ALU.add))
            link(nc.vector.reciprocal(set_t[:, 2, :], set_t[:, 2, :]))
            link(TT(set_t[:, 2, :], set_t[:, 2, :], e, ALU.mult))
            link(TT(set_t[:, 3, :], set_t[:, 2, :], set_t[:, 2, :], ALU.mult))
            link(TS(set_t[:, 4, :], set_t[:, 3, :], 1.0 / 19, None, ALU.mult))
            for k in (17, 15, 13, 11, 9, 7, 5, 3):
                link(STT(out=set_t[:, 4, :], in0=set_t[:, 4, :], scalar=1.0 / k, in1=set_t[:, 3, :],
                         op0=ALU.add, op1=ALU.mult))
            link(STT(out=set_t[:, 4, :], in0=set_t[:, 4, :], scalar=1.0, in1=set_t[:, 2, :],
                     op0=ALU.add, op1=ALU.mult))
            link(TS(set_t[:, 4, :], set_t[:, 4, :], -4.0, None, ALU.mult))
            link(TS(set_t[:, 5, :], set_t[:, 5, :], 0.0, -2.0, ALU.max, ALU.mult))
            link(TT(lru_c[:, 2, :], set_t[:, 4, :], set_t[:, 5, :], ALU.add))
            TS(lru_c[:, 0, :], vec[:, VBA:VBA + LC], 0.5, None, ALU.mult)
            TS(lru_c[:, 1, :], vec[:, VBI:VBI + LC], 0.5, None, ALU.mult).then_inc(setup_done, 1)

            def split(b, u, end=False):
                if end and u >= NU:
                    return
                w_hi_ready.wait(dve, b, u + 1)
                n = kt_of[u % NU] * P
                w_ready.by(TT(w_lo[:, u % RING, 0:n], w_raw[:, u % RING, 0:n], w_hi[:, u % RING, 0:n], ALU.subtract))

            def turn(b, last, u, evac=None):
                for c, (c0, c1) in enumerate(chunks(last)):
                    done(dve, b, u, c, last)
                    if evac:
                        dve_freed.by(evac(G[job(u, c, last) % 3][:, 0:c1 - c0], c0, c1))
                split(b, u + RING, last)

            def add_squares(b, last, which):
                w = W if last else T
                for kt in range(KT):
                    sq_ready.wait(dve, b, which * KT + kt + 1)
                    if kt == 0:
                        ins = nc.vector.tensor_copy(ssum[:, 0:w], sq[:, 0, 0:w])
                    else:
                        sq_added.wait(dve, b, which * KT + kt)
                        ins = TT(ssum[:, 0:w], ssum[:, 0:w], sq[:, kt % 2, 0:w], ALU.add)
                    sq_added.by(ins)

            def norm(b, last, which, hi, lo, g0):
                w = W if last else T
                std_ready.wait(dve, b, which + 1)
                link(nc.vector.reciprocal(rinv[:, 0:w], std[:, 0:w]))

                def scaled(kt):
                    if kt >= 3:
                        norm_ready.wait(dve, b, which * KT + kt - 2)
                    un_ready.by(TT(un[:, kt % 3, 0:w], hT[:, kt, 0:w], rinv[:, 0:w], ALU.mult))

                scaled(0)
                for kt in range(KT):
                    if kt + 1 < KT:
                        scaled(kt + 1)
                    nhi_ready.wait(dve, b, which * KT + kt + 1)
                    norm_ready.by(STT(out=lo[:, kt, 0:w], in0=un[:, kt % 3, 0:w], scalar=v(g0 + kt),
                                      in1=hi[:, kt, 0:w], op0=ALU.mult, op1=ALU.subtract))

            def front(b, last):
                add_squares(b, last, 0)
                norm(b, last, 0, a_hi, a_lo, VG1)
                link(nc.vector.tensor_copy(kT[:, 0:WINDOW], kT[:, T:T + WINDOW]))
                link(nc.vector.tensor_copy(v_tok[:, 0, :], v_tok[:, QB, :]))
                turn(b, last, U_K, lambda src, c0, c1: TS(kT[:, WINDOW + c0:WINDOW + c1], src, v(VB + U_K), None,
                                                          ALU.add))
                turn(b, last, U_V)
                for j in range(JT):
                    turn(b, last, U_Q[j], lambda src, c0, c1: TS(qT[:, j, c0:c1], src, v(VB + U_Q[j]),
                                                                 v(VQS + j), ALU.add, ALU.mult))
                vT_done.wait(dve, b, 1)
                v_ready.by(nc.vector.tensor_copy(v_tok[:, 1:1 + QB, :],
                                                 TB[0][:, :].rearrange("p (m q) -> p m q", m=QB)))

                def softmax_1(s):
                    qb, jp = s // 2, s % 2
                    sc_done.wait(dve, b, s + 1)
                    pT_done.wait(dve, b, s - 1)
                    link(nc.vector.memset(mx[:, s % 2, :], 0.0))
                    for hh in range(HH):
                        g, jj = hh // 2, hh % 2
                        head = g * JT + 2 * jp + jj
                        d = dist_b if qb == 0 else dist
                        ins = nc.vector.tensor_tensor_reduce(
                            s_p[:, s % 2, hh, :], S[g][:, jj * 256:(jj + 1) * 256], d[:, :], 2.0 ** -(head + 1),
                            sinks[:, head:head + 1], ALU.add, ALU.max, mx[:, s % 2, hh:hh + 1])
                    link(ins)
                    link(TS(nm[:, s % 2, :], mx[:, s % 2, :], -1.0, None, ALU.mult))
                    sk = sinks[:, :].rearrange("p (g j) -> p g j", g=NKV)[:, :, 2 * jp:2 * jp + 2]
                    sc_read.by(TT(sd[:, s % 2, :].rearrange("p (g j) -> p g j", g=NKV), sk,
                                  nm[:, s % 2, :].rearrange("p (g j) -> p g j", g=NKV), ALU.add))

                def softmax_2(s):
                    qb, jp = s // 2, s % 2
                    p_ready.wait(dve, b, s + 1)
                    link(TT(es[:, s % 2, :], es[:, s % 2, :], rs[:, s % 2, :], ALU.add))
                    ro = rec[:, qb % 2, :].rearrange("p (g j) -> p g j", g=NKV)[:, :, 2 * jp:2 * jp + 2]
                    link(nc.vector.reciprocal(ro, es[:, s % 2, :].rearrange("p (g j) -> p g j", g=NKV)))

                def probs_T(s):
                    pT_done.wait(dve, b, s + 1)
                    av_done.wait(dve, b, s - 1)
                    pTb_ready.by(nc.vector.tensor_copy(pT[:, s % 2, 4:8, :],
                                                       TB[1][:, :].rearrange("p (n q) -> p n q", n=4)))

                def attn_out(qb):
                    av_done.wait(dve, b, 2 * qb + 2)
                    attnT_done.wait(dve, b, qb)
                    bc = rec[:, qb % 2, :].rearrange("p (h o) -> p h o", o=1).to_broadcast([P, NH, HEAD])
                    atok_ready.by(TT(a_tok[:, :].rearrange("p (h d) -> p h d", h=NH),
                                     V[:, :].rearrange("p (h d) -> p h d", h=NH), bc, ALU.mult))

                def conv(c):
                    act_, k = freed(U_X[c], len(chunks(last)) - 1, last)
                    act_freed.wait(dve, b, k)
                    xi = xb[:, c % 2, :]
                    link(nc.vector.tensor_copy(xi[:, 0:CONV_W - 1], x_prev[:, c, :]))
                    nc.vector.tensor_copy(x_prev[:, c, :], xi[:, T:T + CONV_W - 1])
                    o = xc[:, c % 2, :]
                    lmix_f.wait(dve, b, c - 1)
                    link(TS(o, xi[:, 0:T], v(VCW + c), v(VCB + c), ALU.mult, ALU.add))
                    for k in range(1, CONV_W):
                        ins = STT(out=o, in0=xi[:, k:k + T], scalar=v(VCW + k * LC + c), in1=o,
                                  op0=ALU.mult, op1=ALU.add)
                        if k < CONV_W - 1:
                            link(ins)
                    if last:
                        link(ins)
                        ins = nc.vector.tensor_copy(xs_b[:, c, (CONV_W - 1) * DB:], xi[:, CONV_W - 1 + T:])
                    xc_ready.by(ins)

                def gelu_arg(c):
                    act_, k = freed(U_Y[c], len(chunks(last)) - 1, last)
                    act_freed.wait(dve, b, k)
                    g = gl[:, c % 2, :]
                    if last:
                        link(nc.vector.tensor_copy(ys_b[:, c, :], yb[:, c % 2, T:W]))
                    link(TS(g, g, GELU_K * GELU_C, GELU_K, ALU.mult, ALU.add))
                    gelu_in.by(TT(g, g, yb[:, c % 2, 0:T], ALU.mult))

                def lru(c):
                    g = gl[:, c % 2, :]
                    lru_sqrt.wait(dve, b, c + 1)
                    link(TS(om[:, :], ra[:, :], -1.0, 1.0, ALU.mult, ALU.add))
                    STT(out=ii[:, :], in0=ii[:, :], scalar=1.0, in1=xc[:, c % 2, :], op0=ALU.add, op1=ALU.mult)
                    link(nc.vector.reciprocal(om[:, :], om[:, :]))
                    link(TT(qq[:, :], qq[:, :], om[:, :], ALU.mult))
                    link(STT(out=ra[:, :], in0=ra[:, :], scalar=1.0, in1=om[:, :], op0=ALU.add, op1=ALU.mult))
                    link(TT(ii[:, :], ii[:, :], qq[:, :], ALU.mult))
                    link(nc.vector.tensor_tensor_scan(om[:, :], ra[:, :], ii[:, :], h_prev[:, c:c + 1],
                                                      ALU.mult, ALU.add))
                    nc.vector.tensor_copy(h_prev[:, c:c + 1], om[:, T - 1:T])
                    gelu_th.wait(dve, b, c + 1)
                    link(STT(out=g, in0=g, scalar=1.0, in1=yb[:, c % 2, 0:T], op0=ALU.add, op1=ALU.mult))
                    lmix_f.by(STT(out=g, in0=g, scalar=0.5, in1=om[:, :], op0=ALU.mult, op1=ALU.mult))

                def lru_lo(c):
                    lmix_hi.wait(dve, b, c + 1)
                    lmix_ready.by(TT(x_lo[:, KT - LC + c, 0:T], gl[:, c % 2, :], x_hi[:, KT - LC + c, 0:T],
                                     ALU.subtract))

                for s in range(NUN + 3):
                    if s >= 4 and s % 2 == 0:
                        qb = (s - 4) // 2
                        amix_hi.wait(dve, b, qb + 1)
                        amix_ready.by(TT(x_lo[:, 0:4, qb * P:(qb + 1) * P],
                                         V[:, :].rearrange("p (c q) -> p c q", c=4),
                                         x_hi[:, 0:4, qb * P:(qb + 1) * P], ALU.subtract))
                    if s < NUN:
                        turn(b, last, U_X[0] + s)
                        softmax_1(s)
                        if s % 2 == 0:
                            conv(s // 2)
                        else:
                            gelu_arg(s // 2)
                    if 1 <= s <= NUN:
                        probs_T(s - 1)
                    if s < NUN:
                        softmax_2(s)
                    if s >= 3 and s % 2 == 1:
                        attn_out((s - 3) // 2) if (s - 3) // 2 < QB else None
                    if 2 <= s and s % 2 == 0 and s // 2 - 1 < LC:
                        lru(s // 2 - 1)
                    if s >= 3 and s % 2 == 1 and (s - 3) // 2 < LC:
                        lru_lo((s - 3) // 2)
                if last:
                    sample_dve(b)
                else:
                    link(nc.vector.tensor_copy(dist_b[:, :], dist[:, :]))
                for m, u in enumerate(U_O):
                    turn(b, last, u, lambda src, c0, c1: STT(out=hT[:, m, c0:c1], in0=src, scalar=v(VBO + m),
                                                             in1=hT[:, m, c0:c1], op0=ALU.add, op1=ALU.add))

            def sample_dve(b):
                n = [0]

                def by(ins, want=None):
                    n[0] += 1
                    ins.then_inc(smp_dve, 1)
                    dve.wait_ge(smp_dve, n[0])
                    assert want is None or want == n[0], (want, n[0])

                D3 = (CONV_W - 1) * DB
                by(nc.vector.memset(q_d[:, :, :], 0.0))
                R = DT * JT
                for bb in range(DB):
                    src = qT[:, :, T + bb:W:DB]
                    nc.vector.tensor_copy(q_d[:, bb, bb * R:(bb + 1) * R].rearrange("p (j t) -> p j t", j=JT), src)
                    ins = nc.vector.tensor_copy(q_r[:, bb * R:(bb + 1) * R].rearrange("p (j t) -> p j t", j=JT), src)
                link(ins)
                dve.wait_ge(smp_pe, 2)
                sv = S[0][:, 0:LC * CONV_W * DB].rearrange("p (c r) -> p c r", c=LC)
                nc.vector.tensor_copy(xs_b[:, :, 0:D3], sv[:, :, 0:D3])
                link(nc.vector.tensor_copy(hs0[:, :, :], sv[:, :, D3:D3 + DB]))
                dve.wait_ge(smp_pe, 3)
                nc.vector.tensor_copy(kc_T[:, 0:4, :], TB[0][:, :].rearrange("p (n q) -> p n q", n=4))
                by(nc.vector.tensor_copy(kc_T[:, 4:8, :], TB[1][:, :].rearrange("p (n q) -> p n q", n=4)), SMP_DVE_Q)
                dve.wait_ge(smp_pe, 4)
                nc.vector.tensor_copy(vs_tok[:, :], V[0:NS, 0:P])
                nc.vector.tensor_copy(ks_out[:, :], V[0:NS, P:2 * P])
                link(nc.vector.tensor_copy(k_out[:, :], V[:, 2 * P:3 * P]))
                for c in range(LC):
                    ins = TS(xc_s[:, c, :], xs_b[:, c, 0:NS], v(VCW + c), v(VCB + c), ALU.mult, ALU.add)
                link(ins)
                for k in range(1, CONV_W):
                    for c in range(LC):
                        ins = STT(out=xc_s[:, c, :], in0=xs_b[:, c, k * DB:k * DB + NS], scalar=v(VCW + k * LC + c),
                                  in1=xc_s[:, c, :], op0=ALU.mult, op1=ALU.add)
                    link(ins)
                dve.wait_ge(smp_pe, 5)
                dve.wait_ge(smp_in, 16 * 7)
                for g in range(NKV):
                    ins = nc.vector.tensor_tensor_reduce(s_s[:, g, :], S[g][:, 0:SC], dist_s[:, :], rows[:, g:g + 1],
                                                         sink_s[:, g:g + 1], ALU.add, ALU.max, mx_s[:, 0, g:g + 1])
                link(ins)
                link(TS(mx_s[:, 1, :], mx_s[:, 0, :], -1.0, None, ALU.mult))
                by(TT(mx_s[:, 4, :], sink_s[:, :], mx_s[:, 1, :], ALU.add), SMP_DVE_S)
                link(TT(l_s[4][:, :, :], ys_b[:, :, :], ys_b[:, :, :], ALU.mult))
                link(TS(l_s[4][:, :, :], l_s[4][:, :, :], GELU_K * GELU_C, GELU_K, ALU.mult, ALU.add))
                by(TT(l_s[4][:, :, :], l_s[4][:, :, :], ys_b[:, :, :], ALU.mult), SMP_DVE_GI)
                dve.wait_ge(smp_act, 1)
                link(TT(mx_s[:, 3, :], mx_s[:, 3, :], mx_s[:, 2, :], ALU.add))
                link(nc.vector.reciprocal(mx_s[:, 5, :], mx_s[:, 3, :]))
                for g in range(NKV):
                    ins = TS(s_s[:, g, :], s_s[:, g, :], mx_s[:, 5, g:g + 1], None, ALU.mult)
                by(ins, SMP_DVE_P)
                dve.wait_ge(smp_pe, 6)
                nc.vector.tensor_copy(pcT[:, :, :], TB[0][:, 0:2 * P].rearrange("p (g q) -> p g q", g=NKV))
                by(nc.vector.tensor_copy(pnT[:, :, :], TB[1][0:NS, 0:2 * P].rearrange("p (g q) -> p g q", g=NKV)),
                   SMP_DVE_PT)
                dve.wait_ge(smp_dve, SMP_DVE_PT)
                nc.vector.tensor_copy(outc[:, :, 0:(DT - 1) * DB], xs_b[:, :, D3 + DB:D3 + NS])
                nc.vector.tensor_copy(outc[:, :, DT * DB:DT * DB + CONV_W - 1], x_prev[:, :, :])
                by(nc.vector.tensor_copy(outc[:, :, SCOLS - 1], h_prev[:, :]), SMP_DVE_XC)
                dve.wait_ge(smp_pe, 7)
                for g in range(NKV):
                    for j in range(JT):
                        src = (V, TB[0])[g][0:HEAD, 0:P].rearrange("p (b j t) -> p j t b", b=DB, j=JT)[:, j]
                        lo = j % 2 * HEAD
                        head = g * JT + j
                        dst = mixs[lo:lo + HEAD, head // 2, :].rearrange("p (t b) -> p t b", t=DT)
                        ins = nc.vector.tensor_copy(dst, src)
                link(ins)
                dve.wait_ge(smp_act, 2)
                t, i_, q_, gth = l_s[0], l_s[1], l_s[2], l_s[4]
                link(TS(l_s[3][:, :, :], t[:, :, :], -1.0, 1.0, ALU.mult, ALU.add))
                STT(out=i_[:, :, :], in0=i_[:, :, :], scalar=1.0, in1=xc_s[:, :, :], op0=ALU.add, op1=ALU.mult)
                link(nc.vector.reciprocal(l_s[3][:, :, :], l_s[3][:, :, :]))
                link(TT(q_[:, :, :], q_[:, :, :], l_s[3][:, :, :], ALU.mult))
                link(STT(out=t[:, :, :], in0=t[:, :, :], scalar=1.0, in1=l_s[3][:, :, :], op0=ALU.add, op1=ALU.mult))
                link(TT(i_[:, :, :], i_[:, :, :], q_[:, :, :], ALU.mult))
                hs = l_s[5]
                for k in range(DT):
                    prev = hs0[:, :, :] if k == 0 else hs[:, :, (k - 1) * DB:k * DB]
                    cur = slice(k * DB, (k + 1) * DB)
                    link(TT(hs[:, :, cur], t[:, :, cur], prev, ALU.mult))
                    link(TT(hs[:, :, cur], hs[:, :, cur], i_[:, :, cur], ALU.add))
                by(nc.vector.tensor_copy(outc[:, :, (DT - 1) * DB:DT * DB], hs[:, :, NS - DB:NS]), SMP_DVE_OUTC)
                link(STT(out=gth[:, :, :], in0=gth[:, :, :], scalar=1.0, in1=ys_b[:, :, :], op0=ALU.add, op1=ALU.mult))
                by(STT(out=mixs[:, KT - LC:KT, :], in0=gth[:, :, :], scalar=0.5, in1=hs[:, :, :],
                       op0=ALU.mult, op1=ALU.mult), SMP_DVE_MIXF)
                dve.wait_ge(smp_act, 3)
                by(TT(x_lo[:, :, T:W], mixs[:, :, :], x_hi[:, :, T:W], ALU.subtract), SMP_DVE_MIX)
                dve.wait_ge(smp_pe, 9)
                by(nc.vector.tensor_copy(outr[:, :], TB[1][0:SCOLS, :]), SMP_DVE_OUT)

            def back(b, last):
                w = W if last else T
                nch = len(chunks(last))
                add_squares(b, last, 1)
                norm(b, last, 1, x_hi, x_lo, VG2)
                f0 = 0
                for ci, nf in enumerate(FCH):
                    if last and ci == 0:
                        dve.wait_ge(smp_out, 16 * (2 + 2 + 2 * DT + CONV_W - 1 + 3))
                    for f, (ug, uu) in enumerate(U_IN[ci]):
                        n = f0 + f
                        gate_tanh.wait(dve, b, n + 1)
                        turn(b, last, ug, lambda src, c0, c1: STT(
                            out=gt[:, n % 2, c0:c1], in0=th[:, n % 2, c0:c1], scalar=1.0, in1=src,
                            op0=ALU.add, op1=ALU.mult))
                        _, k = freed(ug, nch - 1, last)
                        dve_freed.wait(dve, b, k)
                        for c, (c0, c1) in enumerate(chunks(last)):
                            done(dve, b, uu, c, last)
                            dve_freed.by(STT(out=a32[:, n % 2, c0:c1], in0=gt[:, n % 2, c0:c1], scalar=0.5,
                                             in1=G[job(uu, c, last) % 3][:, 0:c1 - c0], op0=ALU.mult, op1=ALU.mult))
                        _, k = freed(uu, nch - 1, last)
                        dve_freed.wait(dve, b, k)
                        act_f.by(nc.vector.tensor_copy(set_t[0:1, 0, 0:1], set_t[0:1, 5, 0:1]))
                        split(b, uu + RING, last)
                        act_hi.wait(dve, b, n + 1)
                        act_ready.by(TT(a_lo[:, f, 0:w], a32[:, n % 2, 0:w], a_hi[:, f, 0:w], ALU.subtract))
                    for m, u in enumerate(U_OUT[ci]):
                        turn(b, last, u, lambda src, c0, c1: TT(hT[:, m, c0:c1], src, hT[:, m, c0:c1], ALU.add))
                    f0 += nf
                add_squares(b, last, 2)
                std_ready.wait(dve, b, 3)
                if last:
                    nc.vector.reciprocal(rstd_t[0:NS, QB:QB + 1], std_t[0:NS, QB:QB + 1])
                link(nc.vector.reciprocal(rstd_t[:, 0:QB], std_t[:, 0:QB]))
                for m in range(QB):
                    yT_done.wait(dve, b, m + 1)
                    y_out[m % 2].wait(dve, b, m // 2)
                    o = (S, TB)[m % 2]
                    for h in range(2):
                        ins = STT(out=y_tok[:, m % 2, h * 512:(h + 1) * 512], in0=o[h][:, :],
                                  scalar=rstd_t[:, m:m + 1], in1=gfin[:, h * 512:(h + 1) * 512],
                                  op0=ALU.mult, op1=ALU.mult)
                    y_ready.by(ins)
                if last:
                    dve.wait_ge(smp_pe, 10)
                    y_out[0].wait(dve, b, 2)
                    for h in range(2):
                        ins = STT(out=y_tok[0:NS, 0, h * 512:(h + 1) * 512], in0=S[h][0:NS, :],
                                  scalar=rstd_t[0:NS, QB:QB + 1], in1=gfin[0:NS, h * 512:(h + 1) * 512],
                                  op0=ALU.mult, op1=ALU.mult)
                    ins.then_inc(smp_dve, 1)

            for u in range(RING):
                split(0, u)
            dve.sem_clear(dve_chain)
            chain.n = 0
            with dve.Fori(0, NB - 1) as b:
                front(b, False)
                back(b, False)
                dve.sem_clear(dve_chain)
                chain.n = 0
            front(NB - 1, True)
            back(NB - 1, True)


(SMP_DVE_Z, SMP_DVE_Q, SMP_DVE_S, SMP_DVE_GI, SMP_DVE_P, SMP_DVE_PT, SMP_DVE_XC, SMP_DVE_OUTC, SMP_DVE_MIXF,
 SMP_DVE_MIX, SMP_DVE_OUT, SMP_DVE_Y) = range(1, 13)


def kernel(x_prompt, x_sample, cache_k, cache_v, state_conv, state_h, g_mix, w_in, b_in, attn_sinks, conv_w,
           conv_b, w_a, b_a, w_i, b_i, lam, w_out, b_out, g_ffn, w_ffn_in, w_ffn_out, g_final):
    import numpy as np
    import concourse.bacc as bacc
    from concourse.bass_utils import run_bass_kernel_spmd

    f = np.float32
    A = {k: np.asarray(v) for k, v in dict(
        x_prompt=x_prompt, x_sample=x_sample, cache_k=cache_k, cache_v=cache_v, state_conv=state_conv,
        state_h=state_h, w_a=w_a, w_i=w_i).items()}
    DM = A["x_prompt"].shape[2]
    SEQ = A["x_prompt"].shape[1]
    DB, DT = A["x_sample"].shape[:2]
    KT = DM // P
    wi, wo = np.asarray(w_in)[0], np.asarray(w_out)[0]
    fi, fo = np.asarray(w_ffn_in)[0], np.asarray(w_ffn_out)[0]
    FF = fo.shape[0]
    NF = FF // P
    sinks = np.asarray(attn_sinks)[0]
    NH = sinks.shape[0]
    JT = NH // 2
    QE = NH * HEAD
    KE, VE = QE + 2 * HEAD, QE + 4 * HEAD
    LRU = A["state_h"].shape[2]
    LC = LRU // P
    cols = [np.arange(QE, KE), np.arange(KE, VE)]
    for j in range(JT):
        cols.append(np.concatenate([np.arange(j * HEAD, (j + 1) * HEAD),
                                    np.arange((j + JT) * HEAD, (j + JT + 1) * HEAD)]))
    for c in range(LC):
        cols.append(VE + c * P + np.arange(P))
        cols.append(VE + LRU + c * P + np.arange(P))
    packed = []

    def pack(w):
        k = w.shape[0] // P
        u = np.zeros((P, KT * P), f)
        u[:, 0:k * P] = w.reshape(k, P, P).transpose(1, 0, 2).reshape(P, k * P)
        packed.append(u)

    for c in cols:
        pack(wi[:, c])
    for m in range(KT):
        pack(wo[:, m * P:(m + 1) * P])
    n = -(-NF // KT)
    at = 0
    for i in range(n):
        nf = NF // n + (i < NF % n)
        for t in range(at, at + nf):
            pack(fi[:, t * P:(t + 1) * P])
            pack(fi[:, FF + t * P:FF + (t + 1) * P])
        for m in range(KT):
            pack(fo[at * P:(at + nf) * P, m * P:(m + 1) * P])
        at += nf
    A["units"] = np.stack(packed)

    def tiles(a):
        a = np.asarray(a)
        return a.reshape(-1, P).T

    half = np.arange(P) // HEAD
    qs = np.stack([2.0 ** (j + JT * half + 1) / 8 for j in range(JT)], 1).astype(f)
    bi = np.asarray(b_in)[0]
    A["vecs"] = np.ascontiguousarray(np.concatenate(
        [np.stack([bi[c] for c in cols], 1), tiles(g_mix), tiles(b_out), tiles(g_ffn), tiles(conv_w),
         tiles(conv_b), tiles(b_a), tiles(b_i), tiles(lam), qs], 1))
    A["sinks_p"] = np.ascontiguousarray(np.broadcast_to(sinks, (P, NH)))
    jr = np.arange(P) // DT % JT
    tr = np.arange(P) % DT
    br = np.arange(P) // (DT * JT)
    A["sinks_s"] = np.ascontiguousarray(np.stack([sinks[jr], sinks[JT + jr]], 1))
    A["g_fin"] = np.ascontiguousarray(np.broadcast_to(np.asarray(g_final), (P, DM)))
    A["ident_in"] = np.eye(P, dtype=f)
    FAR = -1e30 * 2.0 ** NH
    i, j = np.arange(P)[:, None], np.arange(2 * P)[None]
    d = P + i - j
    A["dist_in"] = np.stack([np.where((d >= 0) & (d < P), -d, FAR),
                             np.where((d >= 0) & (d < P) & (j >= P), -d, FAR)]).astype(f)
    dc = P + tr[:, None] - np.arange(P)[None]
    tn, bn = np.arange(DB * DT)[None] // DB, np.arange(DB * DT)[None] % DB
    dn = tr[:, None] - tn
    A["dist_s_in"] = np.concatenate([np.where((dc >= 0) & (dc < P), -dc, FAR),
                                     np.where((dn >= 0) & (bn == br[:, None]), -dn, FAR)], 1).astype(f)
    A["per_row"] = np.stack([2.0 ** -(jr + 1.0), 2.0 ** -(JT + jr + 1.0), 0 * jr, 0 * jr], 1).astype(f)

    outs = [("y_p", (1, SEQ, DM)), ("y_s", (DB, DT, DM)), ("nk_p", (1, 1, WINDOW, 2, HEAD)),
            ("nv_p", (1, 1, WINDOW, 2, HEAD)), ("nc_p", (1, 1, CONV_W - 1, LRU)), ("nh_p", (1, 1, LRU)),
            ("nk_s", (1, DB, WINDOW, 2, HEAD)), ("nv_s", (1, DB, WINDOW, 2, HEAD)),
            ("nc_s", (1, DB, CONV_W - 1, LRU)), ("nh_s", (1, DB, LRU))]
    nc = bacc.Bacc("TRN2", target_bir_lowering=False, num_devices=1)
    order = ["x_prompt", "x_sample", "cache_k", "cache_v", "state_conv", "state_h", "units", "vecs", "w_a", "w_i",
             "sinks_p", "sinks_s", "g_fin", "ident_in", "dist_in", "dist_s_in", "per_row"]
    arrays, args = {}, []
    for name in order:
        a = np.ascontiguousarray(A[name])
        arrays[f"in_{name}"] = a
        args.append(nc.dram_tensor(f"in_{name}", a.shape, mybir.dt.from_np(a.dtype), kind="ExternalInput").ap())
    for name, shape in outs:
        args.append(nc.dram_tensor(f"out_{name}", shape, F32, kind="ExternalOutput").ap())
    hymba_layer(nc, *args, FF)
    r = run_bass_kernel_spmd(nc, [arrays], core_ids=[0])
    return tuple(r.results[0][f"out_{name}"] for name, _ in outs)
```

```python
import concourse.bass as bass
from concourse import mybir
from contextlib import ExitStack

F32 = mybir.dt.float32
F32R = mybir.dt.float32r
ALU = mybir.AluOpType
ACT = mybir.ActivationFunctionType

P = 128
WINDOW = 128
HEAD = 64
EPS = 1e-6
GELU_K = 0.7978845608028654
GELU_C = 0.044715
CONV_W = 4
RING = 3
RAW = 2


def branch_order(n):
    order = [("x", 0)]
    for c in range(1, n):
        order += [("x", c), ("y", c - 1)]
    return order + [("y", n - 1)]


class Signal:

    def __init__(self, sem, per_block, step=1, primed=True):
        self.sem, self.per, self.step, self.primed = sem, per_block, step, primed

    def prime(self, eng):
        eng.sem_inc(self.sem, self.per * self.step)

    def wait(self, eng, b, k):
        eng.wait_ge(self.sem, (b * self.per + (self.per if self.primed else 0) + k) * self.step)

    def by(self, ins):
        ins.then_inc(self.sem, self.step)


class Chain:

    def __init__(self, eng, sem):
        self.eng, self.sem, self.n = eng, sem, 0

    def link(self, ins):
        ins.then_inc(self.sem, 1)
        self.n += 1
        self.eng.wait_ge(self.sem, self.n)

    def restart(self):
        if self.n:
            self.eng.sem_clear(self.sem)
            self.n = 0


def hymba_layer(nc, x_p, x_s, cache_k, cache_v, conv_in, h_in, units, vecs, w_a, w_i, sinks_p, sinks_s,
                g_fin, ident_in, dist_in, dist_s_in, per_row,
                y_p, y_s, nk_p, nv_p, nc_p, nh_p, nk_s, nv_s, nc_s, nh_s, d_ff):
    SEQ, DM = x_p.shape[1], x_p.shape[2]
    DB, DT = x_s.shape[0], x_s.shape[1]
    NS = DB * DT
    T = 512
    NB = SEQ // T
    W = T + NS
    QB = T // WINDOW
    KT = DM // P
    NKV = 2
    LC = conv_in.shape[3] // P
    NH = sinks_p.shape[1]
    JT = NH // NKV
    NF = d_ff // P
    FCH = []
    n = -(-NF // KT)
    for i in range(n):
        FCH.append(NF // n + (i < NF % n))

    U_K, U_V = 0, 1
    U_Q = [2 + j for j in range(JT)]
    UH = 2 + JT
    ORDER = branch_order(LC)
    U_X = [UH + ORDER.index(("x", c)) for c in range(LC)]
    U_Y = [UH + ORDER.index(("y", c)) for c in range(LC)]
    U_O = [UH + 2 * LC + m for m in range(KT)]
    U_IN, U_OUT, at = [], [], UH + 2 * LC + KT
    for nf in FCH:
        U_IN.append([(at + 2 * f, at + 2 * f + 1) for f in range(nf)])
        U_OUT.append([at + 2 * nf + m for m in range(KT)])
        at += 2 * nf + KT
    NU = at
    assert NU % RING == 0 and NU % RAW == 0 and UH % 3 == 0, (NU, NF, FCH)
    kt_of = [KT] * NU
    for nf, outs in zip(FCH, U_OUT):
        for u in outs:
            kt_of[u] = nf

    def chunks(wide):
        return [(0, W // 2), (W // 2, W)] if wide else [(0, T)]

    def job(u, c, wide):
        base = 0 if u < UH else UH
        return 2 * (u - base) + c if wide else u

    ctx = ExitStack()
    with ctx:
        ctx.enter_context(nc.allow_non_contiguous_dma("small state vectors"))

        top = [-(-nc.sbuf_base // 64) * 64]

        def place(name, shape, dt=F32, at=None):
            size = 4
            for s in shape[1:]:
                size *= s
            size = -(-size // 64) * 64
            where = top[0] if at is None else at[0]
            t = nc.alloc_sbuf_tensor_at(name, list(shape), dt, offset=where)
            if at is None:
                top[0] += size
            else:
                at[0] += size
            return t

        w_raw = place("w_raw", [P, RAW, KT * P])
        w_hi = place("w_hi", [P, RING, KT * P], F32R)
        w_lo = place("w_lo", [P, RING, KT * P], F32R)
        xT = place("xT", [P, KT, W])
        h_at = [top[0]]
        hT = place("hT", [P, KT, W])
        h_end = top[0]
        a_hi = place("a_hi", [P, KT, W], F32R)
        a_lo = place("a_lo", [P, KT, W], F32R)
        x_at = [top[0]]
        x_hi = place("x_hi", [P, KT, W], F32R)
        x_lo = place("x_lo", [P, KT, W], F32R)
        qT = place("qT", [P, JT, W])
        kT = place("kT", [P, WINDOW + W])
        vT_s = place("vT_s", [P, NS])
        v_tok = place("v_tok", [P, 1 + QB, P])
        ident = place("ident", [P, P])
        ones = place("ones", [P, P])
        dist = place("dist", [P, 2 * WINDOW])
        dist_b = place("dist_b", [P, 2 * WINDOW])
        sinks = place("sinks", [P, NH])
        gates_w = place("gates_w", [P, 2, LC, P])
        gfin = place("gfin", [P, DM])
        vec = place("vec", [P, vecs.shape[1]])
        rows = place("rows", [P, 4])
        sink_s = place("sink_s", [P, NKV])
        lru_c = place("lru_c", [P, 4, LC])
        set_t = place("set_t", [P, 6, LC])
        qb_t = place("qb_t", [P, JT])
        eps_t = place("eps_t", [P, 1])
        x_prev = place("x_prev", [P, LC, CONV_W - 1])
        h_prev = place("h_prev", [P, LC])
        a_tok = place("a_tok", [P, NH * HEAD], at=[top[0]])
        ssum = place("ssum", [P, W])
        rinv = place("rinv", [P, W])
        mx = place("mx", [P, 2, NH // 2])
        nm = place("nm", [P, 2, NH // 2])
        sd = place("sd", [P, 2, NH // 2])
        rs = place("rs", [P, 2, NH // 2])
        es = place("es", [P, 2, NH // 2])
        rec = place("rec", [P, 2, NH])
        std_t = place("std_t", [P, QB + 1])
        rstd_t = place("rstd_t", [P, QB + 1])
        xs_b = place("xs_b", [P, LC, (CONV_W - 1) * DB + NS])
        ys_b = place("ys_b", [P, LC, NS])
        HH = NH // 2

        r = top[0]
        x_tok = place("x_tok", [P, QB, DM])
        a2 = [r]
        s_p = place("s_p", [P, 2, HH, 2 * WINDOW], at=a2)
        pT = place("pT", [P, 2, HH * 2, P], at=a2)
        top[0] = max(top[0], a2[0])
        r = top[0]
        xb = place("xb", [P, 2, CONV_W - 1 + W])
        vT = place("vT", [P, W], at=[top[0]])
        yb = place("yb", [P, 2, W])
        xc = place("xc", [P, 2, T])
        a3 = [r]
        th = place("th", [P, W], at=a3)
        gt = place("gt", [P, W], at=a3)
        a32 = place("a32", [P, 2, W], at=a3)
        sq = place("sq", [P, 2, W], at=a3)
        top[0] = max(top[0], a3[0])
        r = top[0]
        gl = place("gl", [P, 2, T])
        ra = place("ra", [P, T])
        ii = place("ii", [P, T])
        qq = place("qq", [P, T])
        om = place("om", [P, T])
        a2 = [r]
        y_tok = place("y_tok", [P, 2, DM], at=a2)
        ssum_y = place("ssum_y", [P, W], at=a2)
        top[0] = max(top[0], a2[0])
        xs_tok = place("xs_tok", [NS, DM], at=[r])
        a4 = [r]
        SCOLS = (DT - 1) * DB + DB + CONV_W - 1 + 1
        outr = place("outr", [SCOLS, LC * P], at=a4)
        k_out = place("k_out", [P, P], at=a4)
        ks_out = place("ks_out", [NS, P], at=a4)
        vs_tok = place("vs_tok", [NS, P], at=a4)
        assert top[0] <= nc.sbuf_usable_end, top[0]

        SC = WINDOW + NS
        kc_tok = place("kc_tok", [P, DB, P], at=h_at)
        vc_tok = place("vc_tok", [P, DB, P], at=h_at)
        dist_s = place("dist_s", [P, SC], at=h_at)
        st_s = place("st_s", [(CONV_W - 1) * DB + DB, LC * P], at=h_at)
        kc_T = place("kc_T", [P, DB, P], at=h_at)
        s_s = place("s_s", [P, NKV, SC], at=h_at)
        assert h_at[0] <= h_end
        q_d = place("q_d", [P, DB, P], at=x_at)
        mx_s = place("mx_s", [P, 6, NKV], at=x_at)
        pcT = place("pcT", [P, NKV, P], at=x_at)
        pnT = place("pnT", [NS, NKV, P], at=x_at)
        q_r = place("q_r", [P, P], at=x_at)
        mixs = place("mixs", [P, KT, NS], at=x_at)
        xc_s = place("xc_s", [P, LC, NS], at=x_at)
        hs0 = place("hs0", [P, LC, DB], at=x_at)
        l_s = [place(f"l_s{i}", [P, LC, NS], at=x_at) for i in range(6)]
        outc = place("outc", [P, LC, SCOLS], at=x_at)

        bank = [ctx.enter_context(nc.psum_tensor(f"bank{i}", [P, 512], F32)) for i in range(8)]
        G = bank[0:3]
        S = bank[3:5]
        TB = bank[5:7]
        V = bank[7]

        def sem(name):
            return ctx.enter_context(nc.semaphore(name))

        raw_in = [Signal(sem(f"raw_in{i}"), NU // RAW, 16) for i in range(RAW)]
        w_hi_ready = Signal(sem("w_hi_ready"), NU)
        w_ready = Signal(sem("w_ready"), NU)
        gemm_done = Signal(sem("gemm_done"), NU)
        gemm_half = sem("gemm_half")
        freed = Signal(sem("freed"), NU)
        freed_half = sem("freed_half")
        z_ready = Signal(sem("z_ready"), UH + LC)
        x_in = Signal(sem("x_in"), QB, 16, primed=False)
        xT_done = Signal(sem("xT_done"), KT)
        sqx_ready = Signal(sem("sqx_ready"), KT)
        sqx_added = Signal(sem("sqx_added"), KT)
        xhi_ready = Signal(sem("xhi_ready"), KT)
        xlo_ready = Signal(sem("xlo_ready"), KT)
        sqh_ready = Signal(sem("sqh_ready"), KT)
        sqh_added = Signal(sem("sqh_added"), KT)
        hhi_ready = Signal(sem("hhi_ready"), KT)
        hlo_ready = Signal(sem("hlo_ready"), KT)
        sqy_ready = Signal(sem("sqy_ready"), KT)
        sqy_added = Signal(sem("sqy_added"), KT)
        statx_done = Signal(sem("statx_done"), 1)
        stath_done = Signal(sem("stath_done"), 1)
        staty_done = Signal(sem("staty_done"), 1)
        stdx_ready = Signal(sem("stdx_ready"), 1)
        stdh_ready = Signal(sem("stdh_ready"), 1)
        stdy_ready = Signal(sem("stdy_ready"), 1)
        vT_done = Signal(sem("vT_done"), 1)
        v_ready = Signal(sem("v_ready"), 1)
        NUN = 2 * QB
        sc_done = Signal(sem("sc_done"), NUN)
        sc_read = Signal(sem("sc_read"), NUN)
        p_ready = Signal(sem("p_ready"), NUN)
        pT_done = Signal(sem("pT_done"), NUN)
        pTa_ready = Signal(sem("pTa_ready"), NUN)
        pTb_ready = Signal(sem("pTb_ready"), NUN)
        av_done = Signal(sem("av_done"), NUN)
        atok_ready = Signal(sem("atok_ready"), QB)
        attnT_done = Signal(sem("attnT_done"), QB)
        amix_hi = Signal(sem("amix_hi"), QB)
        amix_ready = Signal(sem("amix_ready"), QB)
        xc_ready = Signal(sem("xc_ready"), LC)
        gates_done = Signal(sem("gates_done"), LC)
        gates_read = Signal(sem("gates_read"), LC)
        gelu_sq = Signal(sem("gelu_sq"), LC)
        gelu_in = Signal(sem("gelu_in"), LC)
        gelu_th = Signal(sem("gelu_th"), LC)
        lru_exp = Signal(sem("lru_exp"), LC)
        lru_m = Signal(sem("lru_m"), LC)
        lru_sqrt = Signal(sem("lru_sqrt"), LC)
        lmix_f = Signal(sem("lmix_f"), LC)
        lmix_hi = Signal(sem("lmix_hi"), LC)
        lmix_ready = Signal(sem("lmix_ready"), LC)
        gate_tanh = Signal(sem("gate_tanh"), NF)
        act_f = Signal(sem("act_f"), NF)
        act_hi = Signal(sem("act_hi"), NF)
        act_ready = Signal(sem("act_ready"), NF)
        yT_done = Signal(sem("yT_done"), QB)
        y_ready = Signal(sem("y_ready"), QB)
        y_out = [Signal(sem(f"y_out{i}"), QB // 2, 16) for i in range(2)]
        const_in = sem("const_in")
        zeroed = sem("zeroed")
        setup_act = sem("setup_act")
        setup_done = sem("setup_done")
        xs_in = sem("xs_in")
        smp_in = sem("smp_in")
        smp_out = sem("smp_out")
        smp_pe = sem("smp_pe")
        smp_act = sem("smp_act")
        smp_dve = sem("smp_dve")
        dve_chain = sem("dve_chain")
        act_chain = sem("act_chain")

        VB = 0
        VG1 = VB + UH + 2 * LC
        VBO = VG1 + KT
        VG2 = VBO + KT
        VCW = VG2 + KT
        VCB = VCW + CONV_W * LC
        VBA = VCB + LC
        VBI = VBA + LC
        VLAM = VBI + LC
        VQS = VLAM + LC

        def v(i):
            return vec[:, i:i + 1]

        N_CONST = 12

        def done(eng, b, u, c, wide):
            if wide and u >= 0 and c == 0:
                eng.wait_ge(gemm_half, u + 1)
            else:
                gemm_done.wait(eng, b, u + 1)

        def unit_done(eng, b, u):
            gemm_done.wait(eng, b, u + 1)

        block = ctx.enter_context(nc.Block())

        @block.sync
        def _(sp):
            for s in raw_in:
                s.prime(sp)

            def load_unit(b, u):
                w_ready.wait(sp, b, u - RAW + 1)
                n = kt_of[u % NU] * P
                raw_in[u % RAW].by(sp.dma_start(w_raw[:, u % RAW, 0:n], units[u % NU, :, 0:n]))

            w_ready.wait(sp, 0, 0)
            for u in range(RAW):
                load_unit(0, u)
            with sp.Fori(0, NB - 1) as b:
                for u in range(RAW, NU + RAW):
                    load_unit(b, u)
            for u in range(RAW, NU):
                load_unit(NB - 1, u)

        @block.gpsimd
        def _(pool):
            nc.gpsimd.memset(gates_w[:, :, :, :], 0.0).then_inc(zeroed, 1)
            nc.gpsimd.memset(kT[:, :], 0.0).then_inc(zeroed, 1)
            nc.gpsimd.memset(v_tok[:, :, :], 0.0).then_inc(zeroed, 1)
            nc.gpsimd.memset(x_prev[:, :, :], 0.0).then_inc(zeroed, 1)
            nc.gpsimd.memset(h_prev[:, :], 0.0).then_inc(zeroed, 1)
            nc.gpsimd.memset(ones[:, :], 1.0).then_inc(zeroed, 1)
            nc.gpsimd.memset(eps_t[:, :], EPS).then_inc(zeroed, 1)

            def load_x(b):
                for m in range(QB):
                    x_in.by(pool.dma_start(x_tok[:, m, :], x_p[0, bass.ds(b * T + m * P, P), :]))

            load_x(0)
            for t in range(DT):
                pool.dma_start(xs_tok[t * DB:(t + 1) * DB, :], x_s[:, t, :]).then_inc(xs_in, 16)
            for dst, src in ((ident[:, :], ident_in), (vec[:, :], vecs), (dist[:, :], dist_in[0]),
                             (dist_b[:, :], dist_in[1]), (sinks[:, :], sinks_p), (gfin[:, :], g_fin),
                             (rows[:, :], per_row), (sink_s[:, :], sinks_s)):
                pool.dma_start(dst, src).then_inc(const_in, 16)
            pool.wait_ge(zeroed, 1)
            for n, w in enumerate((w_a, w_i)):
                for half in range(2):
                    lo = half * HEAD
                    pool.dma_start(gates_w[lo:lo + HEAD, n, :, lo:lo + HEAD],
                                   w[0, half::2].rearrange("n d e -> d n e")).then_inc(const_in, 16)

            with pool.Fori(0, NB - 1) as b:
                amix_ready.wait(pool, b, QB)
                xT_done.wait(pool, b, KT)
                load_x(b + 1)
            b = NB - 1
            yT_done.wait(pool, b, 0)
            for dst, src in ((kc_tok[:, :, :], cache_k[0].rearrange("b s g d -> s b (g d)")),
                             (vc_tok[:, :, :], cache_v[0].rearrange("b s g d -> s b (g d)")),
                             (dist_s[:, :], dist_s_in)):
                pool.dma_start(dst, src).then_inc(smp_in, 16)
            for t in range(CONV_W - 1):
                pool.dma_start(st_s[t * DB:(t + 1) * DB, :], conv_in[0, :, t, :]).then_inc(smp_in, 16)
            pool.dma_start(st_s[(CONV_W - 1) * DB:CONV_W * DB, :], h_in[0]).then_inc(smp_in, 16)
            for o, c in ((nk_s, cache_k), (nv_s, cache_v)):
                pool.dma_start(o[0, :, 0:WINDOW - DT].rearrange("b s g d -> b (s g d)"),
                               c[0, :, DT:WINDOW].rearrange("b s g d -> b (s g d)")).then_inc(smp_out, 16)
            n_out = 2
            pool.wait_ge(smp_dve, SMP_DVE_OUT)
            pool.dma_start(nv_p[0, 0].rearrange("s g d -> s (g d)"), v_tok[:, QB, :]).then_inc(smp_out, 16)
            pool.dma_start(nk_p[0, 0].rearrange("s g d -> s (g d)"), k_out[:, :]).then_inc(smp_out, 16)
            n_out += 2
            for t in range(DT):
                r0 = t * DB
                pool.dma_start(nk_s[0, :, WINDOW - DT + t].rearrange("b g d -> b (g d)"),
                               ks_out[r0:r0 + DB, :]).then_inc(smp_out, 16)
                pool.dma_start(nv_s[0, :, WINDOW - DT + t].rearrange("b g d -> b (g d)"),
                               vs_tok[r0:r0 + DB, :]).then_inc(smp_out, 16)
                n_out += 2
            r0 = 0
            for t in range(CONV_W - 1):
                pool.dma_start(nc_s[0, :, t], outr[r0:r0 + DB, :]).then_inc(smp_out, 16)
                r0 += DB
            pool.dma_start(nh_s[0], outr[r0:r0 + DB, :]).then_inc(smp_out, 16)
            r0 += DB
            pool.dma_start(nc_p[0, 0], outr[r0:r0 + CONV_W - 1, :]).then_inc(smp_out, 16)
            r0 += CONV_W - 1
            pool.dma_start(nh_p[0], outr[r0:r0 + 1, :]).then_inc(smp_out, 16)
            n_out += CONV_W - 1 + 3
            pool.wait_ge(smp_dve, SMP_DVE_Y)
            for t in range(DT):
                pool.dma_start(y_s[:, t, :], y_tok[t * DB:(t + 1) * DB, 0, :]).then_inc(smp_out, 16)
            n_out += DT
            pool.wait_ge(smp_out, 16 * n_out)
            for o in y_out:
                o.wait(pool, b, QB // 2)

        @block.tensor
        def _(pe):
            for s in (gemm_done, xT_done, statx_done, stath_done, staty_done, vT_done, sc_done, pT_done, av_done, attnT_done,
                      gates_done, yT_done):
                s.prime(pe)
            pe.wait_ge(const_in, 16 * N_CONST)
            pe.wait_ge(zeroed, 7)
            smp = [0]

            def smp_by(ins):
                smp[0] += 1
                ins.then_inc(smp_pe, 1)

            def gemm(b, wide, u, hi, lo, tile_ready=None, kts=None):
                whole = list(range(kt_of[u]))
                kts = kts or whole
                first = kts[0] == (KT - LC if kts != whole else 0)
                final = kts[-1] == kt_of[u] - 1
                w_ready.wait(pe, b, u + 1)
                base = 0 if u < UH else UH
                for c, (c0, c1) in enumerate(chunks(wide)):
                    j = job(u, c, wide)
                    if not first:
                        pass
                    elif not wide:
                        freed.wait(pe, b, u - 2)
                    elif j < 3:
                        freed.wait(pe, b, base + j - 2)
                    elif j % 2:
                        pe.wait_ge(freed_half, base + (j - 3) // 2 + 1)
                    else:
                        freed.wait(pe, b, base + (j - 3) // 2 + 1)
                    out = G[j % 3][:, 0:c1 - c0]
                    for kt in kts:
                        if tile_ready and c == 0:
                            tile_ready(kt)
                        h = w_hi[:, u % RING, kt * P:(kt + 1) * P]
                        l = w_lo[:, u % RING, kt * P:(kt + 1) * P]
                        nc.tensor.matmul(out, h, hi[:, kt, c0:c1], start=(first and kt == kts[0]), stop=False)
                        nc.tensor.matmul(out, h, lo[:, kt, c0:c1], start=False, stop=False)
                        mm = nc.tensor.matmul(out, l, hi[:, kt, c0:c1], start=False, stop=(kt == kt_of[u] - 1))
                    if wide and c == 0 and final:
                        mm.then_inc(gemm_half, 1)
                if final:
                    gemm_done.by(mm)

            def feature_sums(wide):
                for c, (c0, c1) in enumerate(chunks(wide)):
                    mm = nc.tensor.matmul((V, TB[0])[c][:, 0:c1 - c0], ones[:, :], ssum[:, c0:c1],
                                          start=True, stop=True)
                return mm

            xbank = [S[0], S[1], TB[0], TB[1]]

            def x_T(n, kt):
                if kt == 0:
                    x_in.wait(pe, n, QB)
                if kt >= 4:
                    xhi_ready.wait(pe, n, kt - 3)
                for m in range(QB):
                    mm = nc.tensor.transpose(xbank[kt % 4][:, m * P:(m + 1) * P],
                                             x_tok[:, m, kt * P:(kt + 1) * P], ident[:, :])
                xT_done.by(mm)

            def values_T(n):
                z_ready.wait(pe, n, U_V + 1)
                for m in range(QB):
                    mm = nc.tensor.transpose(TB[0][:, m * P:(m + 1) * P], vT[:, m * P:(m + 1) * P], ident[:, :])
                vT_done.by(mm)

            def y_stat(b, wide):
                sqy_added.wait(pe, b, KT)
                for m in range(QB):
                    mm = nc.tensor.matmul(V[:, m:m + 1], ssum_y[:, m * P:(m + 1) * P], ones[:, 0:1],
                                          start=True, stop=True)
                if wide:
                    mm = nc.tensor.matmul(V[0:NS, QB:QB + 1], ssum_y[:, T:W], ones[:, 0:1], start=True, stop=True)
                staty_done.by(mm)

            def y_T(b, m):
                if m >= 2:
                    y_ready.wait(pe, b, m - 1)
                o = (S, TB)[m % 2]
                for kt in range(KT):
                    mm = nc.tensor.transpose(o[kt // 4][:, kt % 4 * P:(kt % 4 + 1) * P],
                                             hT[:, kt, m * P:(m + 1) * P], ident[:, :])
                yT_done.by(mm)

            def head(n, wide, b=None):
                gemm(n, wide, U_K, x_hi, x_lo, lambda kt: xlo_ready.wait(pe, n, kt + 1))
                sqx_added.wait(pe, n, KT)
                statx_done.by(feature_sums(wide))
                gemm(n, wide, U_V, x_hi, x_lo)
                if b is not None:
                    stdx_ready.wait(pe, n, 1)
                    y_stat(b, False)
                gemm(n, wide, U_Q[0], x_hi, x_lo)
                if b is not None:
                    y_T(b, 0)
                gemm(n, wide, U_Q[1], x_hi, x_lo)
                stdx_ready.wait(pe, n, 1)
                values_T(n)
                gemm(n, wide, U_Q[2], x_hi, x_lo)
                if b is not None:
                    v_ready.wait(pe, n, 1)
                    y_T(b, 1)
                    y_T(b, 2)
                gemm(n, wide, U_Q[3], x_hi, x_lo)
                if b is not None:
                    y_T(b, 3)

            def mixers(b, last):
                def scores(s):
                    qb, jp = s // 2, s % 2
                    if s == 0:
                        z_ready.wait(pe, b, UH)
                        y_ready.wait(pe, b, 0)
                    elif s % 2 == 0:
                        gates_read.wait(pe, b, s // 2)
                    else:
                        sc_read.wait(pe, b, s)
                    for g in range(NKV):
                        r = slice(g * HEAD, (g + 1) * HEAD)
                        for jj in range(2):
                            mm = nc.tensor.matmul(S[g][:, jj * 256:(jj + 1) * 256],
                                                  qT[r, 2 * jp + jj, qb * P:(qb + 1) * P],
                                                  kT[r, qb * P:qb * P + 2 * WINDOW], start=True, stop=True)
                    sc_done.by(mm)

                def probs_T(s):
                    p_ready.wait(pe, b, s + 1)
                    if s == 0:
                        v_ready.wait(pe, b, 1)
                    else:
                        pTa_ready.wait(pe, b, s)
                        pTb_ready.wait(pe, b, s)
                    for n in range(2 * HH):
                        mm = nc.tensor.transpose(TB[n // 4][:, n % 4 * P:(n % 4 + 1) * P],
                                                 s_p[:, s % 2, n // 2, n % 2 * P:(n % 2 + 1) * P], ident[:, :])
                    pT_done.by(mm)

                def attend(s):
                    qb, jp = s // 2, s % 2
                    pTa_ready.wait(pe, b, s + 1)
                    pTb_ready.wait(pe, b, s + 1)
                    if jp == 0 and qb > 0:
                        amix_ready.wait(pe, b, qb)
                    for hh in range(HH):
                        g, jj = hh // 2, hh % 2
                        head = g * JT + 2 * jp + jj
                        for half in range(2):
                            mm = nc.tensor.matmul(V[:, head * HEAD:(head + 1) * HEAD],
                                                  pT[:, s % 2, 2 * hh + half, :],
                                                  v_tok[:, qb + half, g * HEAD:(g + 1) * HEAD],
                                                  start=(half == 0), stop=(half == 1))
                    av_done.by(mm)

                def attn_T(qb):
                    atok_ready.wait(pe, b, qb + 1)
                    for c in range(4):
                        mm = nc.tensor.transpose(V[:, c * P:(c + 1) * P], a_tok[:, c * P:(c + 1) * P], ident[:, :])
                    attnT_done.by(mm)

                def gates(c):
                    xc_ready.wait(pe, b, c + 1)
                    sc_read.wait(pe, b, 2 * c + 2)
                    for n in range(2):
                        mm = nc.tensor.matmul(S[n][:, :], gates_w[:, n, c, :], xc[:, c % 2, :],
                                              start=True, stop=True)
                    gates_done.by(mm)

                for s in range(NUN):
                    if s >= 1:
                        probs_T(s - 1)
                    if s >= 2:
                        attend(s - 2)
                    scores(s)
                    gemm(b, last, UH + s, x_hi, x_lo)
                    if s % 2 == 1:
                        gates(s // 2)
                    if s >= 3 and s % 2 == 1:
                        attn_T((s - 3) // 2)

                def mix_ready(kt):
                    if kt >= KT - LC:
                        lmix_ready.wait(pe, b, kt - (KT - LC) + 1)
                    else:
                        amix_ready.wait(pe, b, QB)

                def part(m, kts):
                    gemm(b, last, U_O[m], a_hi, a_lo, mix_ready, kts)

                early = list(range(KT - LC, KT - 1))
                probs_T(NUN - 1)
                attend(NUN - 2)
                if last:
                    attend(NUN - 1)
                    attn_T(QB - 1)
                    sample_pe(b)
                    pe.wait_ge(smp_dve, SMP_DVE_MIX)
                    gemm(b, last, U_O[0], a_hi, a_lo, mix_ready, None)
                    rest = 1
                else:
                    part(0, early)
                    attend(NUN - 1)
                    part(1, early)
                    attn_T(QB - 1)
                    part(2, early)
                    for m in range(3):
                        part(m, list(range(KT - LC)))
                    for m in range(3):
                        part(m, [KT - 1])
                    rest = 3
                for u in U_O[rest:]:
                    gemm(b, last, u, a_hi, a_lo)

            def sample_pe(b):
                pe.wait_ge(smp_in, 16 * 7)
                gates_read.wait(pe, b, LC)
                R = CONV_W * DB
                for c in range(LC):
                    mm = nc.tensor.transpose(S[0][:, c * R:(c + 1) * R], st_s[:, c * P:(c + 1) * P], ident[0:R, 0:R])
                smp_by(mm)
                pTa_ready.wait(pe, b, NUN)
                pTb_ready.wait(pe, b, NUN)
                for bb in range(DB):
                    mm = nc.tensor.transpose(TB[bb // 4][:, bb % 4 * P:(bb % 4 + 1) * P], kc_tok[:, bb, :], ident[:, :])
                smp_by(mm)
                amix_ready.wait(pe, b, QB)
                nc.tensor.transpose(V[0:NS, 0:P], vT_s[:, :], ident[:, :])
                nc.tensor.transpose(V[0:NS, P:2 * P], kT[:, WINDOW + T:WINDOW + W], ident[:, :])
                smp_by(nc.tensor.transpose(V[:, 2 * P:3 * P], kT[:, T:T + WINDOW], ident[:, :]))
                pe.wait_ge(smp_dve, SMP_DVE_Q)
                for g in range(NKV):
                    r = slice(g * HEAD, (g + 1) * HEAD)
                    for bb in range(DB):
                        nc.tensor.matmul(S[g][:, 0:WINDOW], q_d[r, bb, :], kc_T[r, bb, :],
                                         start=(bb == 0), stop=(bb == DB - 1))
                    mm = nc.tensor.matmul(S[g][:, WINDOW:SC], q_r[r, :], kT[r, WINDOW + T:WINDOW + W],
                                          start=False, stop=True, skip_group_check=True)
                smp_by(mm)
                pe.wait_ge(smp_dve, SMP_DVE_P)
                for g in range(NKV):
                    nc.tensor.transpose(TB[0][:, g * P:(g + 1) * P], s_s[:, g, 0:WINDOW], ident[:, :])
                    mm = nc.tensor.transpose(TB[1][0:NS, g * P:(g + 1) * P], s_s[:, g, WINDOW:SC], ident[:, :])
                smp_by(mm)
                pe.wait_ge(smp_dve, SMP_DVE_PT)
                for g in range(NKV):
                    d = slice(g * HEAD, (g + 1) * HEAD)
                    o = (V, TB[0])[g]
                    for bb in range(DB):
                        rr = slice(bb * DT * JT, (bb + 1) * DT * JT)
                        nc.tensor.matmul(o[0:HEAD, rr], vc_tok[:, bb, d], pcT[:, g, rr],
                                         start=(bb == 0), stop=(bb == DB - 1), skip_group_check=True)
                    mm = nc.tensor.matmul(o[0:HEAD, 0:P], vs_tok[:, d], pnT[:, g, :], start=False, stop=True,
                                          skip_group_check=True)
                smp_by(mm)
                pe.wait_ge(smp_dve, SMP_DVE_XC)
                for n in range(2):
                    for c in range(LC):
                        mm = nc.tensor.matmul(S[n][:, c * NS:(c + 1) * NS], gates_w[:, n, c, :], xc_s[:, c, :],
                                              start=True, stop=True)
                smp_by(mm)
                pe.wait_ge(smp_dve, SMP_DVE_OUTC)
                for c in range(LC):
                    mm = nc.tensor.transpose(TB[1][0:SCOLS, c * P:(c + 1) * P], outc[:, c, :], ident[:, :])
                smp_by(mm)

            def ffn(b, last):
                f0 = 0
                for ci, nf in enumerate(FCH):
                    for f, (ug, uu) in enumerate(U_IN[ci]):
                        first = ci == 0 and f == 0
                        gemm(b, last, ug, x_hi, x_lo,
                             (lambda kt: hlo_ready.wait(pe, b, kt + 1)) if first else None)
                        if first:
                            sqh_added.wait(pe, b, KT)
                            amix_ready.wait(pe, b, QB)
                            if last:
                                pe.wait_ge(smp_dve, SMP_DVE_OUT)
                            stath_done.by(feature_sums(last))
                        gemm(b, last, uu, x_hi, x_lo)
                    for m, u in enumerate(U_OUT[ci]):
                        gemm(b, last, u, a_hi, a_lo,
                             (lambda kt, f0=f0: act_ready.wait(pe, b, f0 + kt + 1)) if m == 0 else None)
                        if ci == len(FCH) - 1 and not last:
                            x_T(b + 1, m)
                    f0 += nf

            pe.wait_ge(xs_in, 16 * DT)
            for kt in range(KT):
                mm = nc.tensor.transpose(V[:, kt * NS:(kt + 1) * NS], xs_tok[:, kt * P:(kt + 1) * P],
                                         ident[0:NS, 0:NS])
            smp_by(mm)
            for kt in range(KT):
                x_T(0, kt)
            head(0, True)
            freed.wait(pe, 0, UH)
            with pe.Fori(0, NB - 1) as b:
                mixers(b, False)
                ffn(b, False)
                head(b + 1, False, b)
            mixers(NB - 1, True)
            ffn(NB - 1, True)
            y_stat(NB - 1, True)
            for m in range(QB):
                y_T(NB - 1, m)
            y_ready.wait(pe, NB - 1, 3)
            for kt in range(KT):
                mm = nc.tensor.transpose(S[kt // 4][0:NS, kt % 4 * P:(kt % 4 + 1) * P], hT[:, kt, T:W], ident[:, :])
            smp_by(mm)

        @block.scalar
        def _(act):
            for s in (w_hi_ready, z_ready, sqx_ready, sqh_ready, sqy_ready, xhi_ready, hhi_ready, stdx_ready,
                      stdh_ready, stdy_ready, p_ready, pTa_ready, amix_hi,
                      gates_read, lru_exp, gelu_sq, gelu_th, lru_sqrt, lmix_hi, gate_tanh, act_hi, *y_out):
                s.prime(act)
            chain = Chain(act, act_chain)
            smp = [0]

            def smp_by(ins):
                smp[0] += 1
                ins.then_inc(smp_act, 1)

            A = nc.scalar.activation
            act.wait_ge(const_in, 16 * N_CONST)
            act.wait_ge(zeroed, 7)
            act.wait_ge(setup_done, 1)
            A(set_t[:, 1, :], set_t[:, 0, :], ACT.Exp, scale=-1.0).then_inc(setup_act, 1)
            act.wait_ge(setup_done, 2)

            def split(b, u, end=False):
                if end and u >= NU:
                    return
                raw_in[u % RAW].wait(act, b, u // RAW + 1)
                unit_done(act, b, u - RING)
                n = kt_of[u % NU] * P
                w_hi_ready.by(A(w_hi[:, u % RING, 0:n], w_raw[:, u % RAW, 0:n], ACT.Copy))

            def rms(wide, ready):
                for c, (c0, c1) in enumerate(chunks(wide)):
                    ins = A(rinv[:, c0:c1], (V, TB[0])[c][:, 0:c1 - c0], ACT.Sqrt, bias=eps_t[:, 0:1], scale=1.0 / DM)
                ready.by(ins)

            xbank = [S[0], S[1], TB[0], TB[1]]

            def x_tile(n, wide, kt):
                w = W if wide else T
                xT_done.wait(act, n, kt + 1)
                chain.link(A(xT[:, kt, 0:T], xbank[kt % 4][:, :], ACT.Copy))
                sqx_added.wait(act, n, kt)
                sqx_ready.by(A(sq[:, 1, 0:w], xT[:, kt, 0:w], ACT.Square))
                xhi_ready.by(A(x_hi[:, kt, 0:w], xT[:, kt, 0:w], ACT.Copy, scale=v(VG1 + kt)))

            def h_tile(b, wide, m):
                w = W if wide else T
                freed.wait(act, b, U_O[m] + 1)
                sqh_added.wait(act, b, m)
                sqh_ready.by(A(sq[:, 0, 0:w], hT[:, m, 0:w], ACT.Square))
                hhi_ready.by(A(x_hi[:, m, 0:w], hT[:, m, 0:w], ACT.Copy, scale=v(VG2 + m)))

            def y_tile(b, wide, m):
                w = W if wide else T
                freed.wait(act, b, U_OUT[-1][m] + 1)
                sqy_added.wait(act, b, m)
                sqy_ready.by(A(sq[:, 0, 0:w], hT[:, m, 0:w], ACT.Square))

            def y_rms(b, wide):
                staty_done.wait(act, b, 1)
                if wide:
                    A(std_t[0:NS, QB:QB + 1], V[0:NS, QB:QB + 1], ACT.Sqrt, bias=eps_t[0:NS, 0:1], scale=1.0 / DM)
                stdy_ready.by(A(std_t[:, 0:QB], V[:, 0:QB], ACT.Sqrt, bias=eps_t[:, 0:1], scale=1.0 / DM))

            def y_store(b, m):
                y_ready.wait(act, b, m + 1)
                y_out[m % 2].by(act.dma_start(y_p[0, bass.ds(b * T + m * P, P), :], y_tok[:, m % 2, :]))

            def head(n, wide, b=None):
                w = W if wide else T
                split(n, U_K + RING)
                statx_done.wait(act, n, 1)
                rms(wide, stdx_ready)
                freed.wait(act, n, U_K + 1)
                kn = kT[:, WINDOW:WINDOW + w]
                z_ready.by(A(kn, kn, ACT.Identity, bias=v(VB + U_K)))
                split(n, U_V + RING)
                freed.wait(act, n, U_V + 1)
                if wide:
                    A(vT_s[:, :], vT[:, T:W], ACT.Identity, bias=v(VB + U_V))
                z_ready.by(A(vT[:, 0:T], vT[:, 0:T], ACT.Identity, bias=v(VB + U_V)))
                if b is not None:
                    y_rms(b, False)
                for j, u in enumerate(U_Q):
                    split(n, u + RING)
                    freed.wait(act, n, u + 1)
                    z_ready.by(A(qT[:, j, 0:w], qT[:, j, 0:w], ACT.Identity, bias=qb_t[:, j:j + 1],
                                 scale=v(VQS + j)))
                    if b is not None and j == 0:
                        y_store(b, 0)
                    if b is not None and j == 2:
                        y_store(b, 1)
                        y_store(b, 2)
                if b is not None:
                    y_store(b, 3)

            def mixers(b, last):
                for o in y_out:
                    o.wait(act, b, 0)

                def exps(s):
                    sc_read.wait(act, b, s + 1)
                    for hh in range(HH):
                        A(s_p[:, s % 2, hh, :], s_p[:, s % 2, hh, :], ACT.Exp, bias=nm[:, s % 2, hh:hh + 1],
                          accum_out=rs[:, s % 2, hh:hh + 1])
                    p_ready.by(A(es[:, s % 2, :], sd[:, s % 2, :], ACT.Exp))

                def probs_T(s):
                    pT_done.wait(act, b, s + 1)
                    av_done.wait(act, b, s - 1)
                    pTa_ready.by(A(pT[:, s % 2, 0:4, :], TB[0][:, :].rearrange("p (n q) -> p n q", n=4), ACT.Copy))

                def lru_1(c):
                    gates_done.wait(act, b, c + 1)
                    lmix_f.wait(act, b, c)
                    chain.link(A(ra[:, :], S[0][:, :], ACT.Tanh, bias=lru_c[:, 0, c:c + 1], scale=0.5))
                    gates_read.by(A(ii[:, :], S[1][:, :], ACT.Tanh, bias=lru_c[:, 1, c:c + 1], scale=0.5))
                    chain.link(A(qq[:, :], ra[:, :], ACT.Tanh, bias=lru_c[:, 3, c:c + 1], scale=lru_c[:, 3, c:c + 1]))
                    chain.link(A(ra[:, :], ra[:, :], ACT.Exp, bias=lru_c[:, 2, c:c + 1], scale=lru_c[:, 2, c:c + 1]))
                    lru_exp.by(A(om[:, :], ra[:, :], ACT.Square))

                def lru_root(c):
                    lru_m.wait(act, b, c + 1)
                    lru_sqrt.by(A(qq[:, :], qq[:, :], ACT.Sqrt, scale=0.25))

                def gelu_tanh(c):
                    gelu_in.wait(act, b, c + 1)
                    gelu_th.by(A(gl[:, c % 2, :], gl[:, c % 2, :], ACT.Tanh))

                def lru_hi(c):
                    lmix_f.wait(act, b, c + 1)
                    lmix_hi.by(A(a_hi[:, KT - LC + c, 0:T], gl[:, c % 2, :], ACT.Copy, scale=0.5))

                def attn_hi(qb):
                    attnT_done.wait(act, b, qb + 1)
                    amix_hi.by(A(a_hi[:, 0:4, qb * P:(qb + 1) * P],
                                 V[:, :].rearrange("p (c q) -> p c q", c=4), ACT.Copy))

                for s in range(NUN):
                    if s >= 1:
                        probs_T(s - 1)
                    exps(s)
                    if s >= 2 and s % 2 == 0:
                        lru_root((s - 2) // 2)
                    kind, c = ORDER[s]
                    u = UH + s
                    freed.wait(act, b, u + 1)
                    if kind == "x":
                        xi = xb[:, c % 2, CONV_W - 1:CONV_W - 1 + (W if last else T)]
                        z_ready.by(A(xi, xi, ACT.Identity, bias=v(VB + u)))
                    else:
                        lmix_ready.wait(act, b, c - 1)
                        gelu_sq.by(A(gl[:, c % 2, :], yb[:, c % 2, 0:T], ACT.Square, bias=v(VB + u)))
                        if c < LC - 1:
                            gelu_tanh(c)
                    if s >= 3 and s % 2 == 1:
                        attn_hi((s - 3) // 2)
                    if s % 2 == 1:
                        lru_1(s // 2)
                    split(b, u + RING)
                    if s >= 3 and s % 2 == 1:
                        lru_hi((s - 3) // 2)
                probs_T(NUN - 1)
                lru_root(LC - 1)
                gelu_tanh(LC - 1)
                attn_hi(QB - 1)
                lru_hi(LC - 1)
                if last:
                    sample_act(b)
                for m, u in enumerate(U_O):
                    split(b, u + RING)
                    h_tile(b, last, m)

            def sample_act(b):
                act.wait_ge(smp_dve, SMP_DVE_S)
                for g in range(NKV):
                    A(s_s[:, g, :], s_s[:, g, :], ACT.Exp, bias=mx_s[:, 1, g:g + 1], accum_out=mx_s[:, 2, g:g + 1])
                smp_by(A(mx_s[:, 3, :], mx_s[:, 4, :], ACT.Exp))
                act.wait_ge(smp_pe, 8)
                for n in range(2):
                    for c in range(LC):
                        ins = A(l_s[n][:, c, :], S[n][:, c * NS:(c + 1) * NS], ACT.Tanh,
                                bias=lru_c[:, n, c:c + 1], scale=0.5)
                chain.link(ins)
                for c in range(LC):
                    A(l_s[3][:, c, :], l_s[0][:, c, :], ACT.Exp, bias=lru_c[:, 2, c:c + 1], scale=lru_c[:, 2, c:c + 1])
                    A(l_s[2][:, c, :], l_s[0][:, c, :], ACT.Tanh, bias=lru_c[:, 3, c:c + 1],
                      scale=lru_c[:, 3, c:c + 1])
                act.wait_ge(smp_dve, SMP_DVE_GI)
                smp_by(A(l_s[4][:, :, :], l_s[4][:, :, :], ACT.Tanh))
                act.wait_ge(smp_dve, SMP_DVE_M)
                smp_by(A(l_s[2][:, :, :], l_s[2][:, :, :], ACT.Sqrt, scale=0.25))
                act.wait_ge(smp_dve, SMP_DVE_MIXF)
                smp_by(A(a_hi[:, :, T:W], mixs[:, :, :], ACT.Copy))

            def ffn(b, last):
                w = W if last else T
                f0 = 0
                for ci, nf in enumerate(FCH):
                    for f, (ug, uu) in enumerate(U_IN[ci]):
                        n = f0 + f
                        split(b, ug + RING)
                        if n == 0:
                            stath_done.wait(act, b, 1)
                            rms(last, stdh_ready)
                        freed.wait(act, b, ug + 1)
                        gate_tanh.by(A(th[:, 0:w], gt[:, 0:w], ACT.Tanh, scale=0.5))
                        split(b, uu + RING, last)
                        act_f.wait(act, b, n + 1)
                        act_hi.by(A(a_hi[:, f, 0:w], a32[:, n % 2, 0:w], ACT.Copy))
                    for m, u in enumerate(U_OUT[ci]):
                        split(b, u + RING, last)
                        if ci == len(FCH) - 1:
                            if not last:
                                x_tile(b + 1, False, m)
                            y_tile(b, last, m)
                    f0 += nf

            for u in range(RING):
                split(0, u)
            act.wait_ge(smp_pe, 1)
            chain.link(A(xT[:, :, T:W], V[:, 0:KT * NS].rearrange("p (k n) -> p k n", k=KT), ACT.Copy))
            for kt in range(KT):
                x_tile(0, True, kt)
            head(0, True)
            chain.restart()
            with act.Fori(0, NB - 1) as b:
                mixers(b, False)
                ffn(b, False)
                head(b + 1, False, b)
                chain.restart()
            b = NB - 1
            mixers(b, True)
            ffn(b, True)
            y_rms(b, True)
            for m in range(QB):
                y_store(b, m)

        @block.vector
        def _(dve):
            for s in (w_ready, freed, sqx_added, sqh_added, sqy_added, xlo_ready, hlo_ready, v_ready, sc_read, pTb_ready,
                      atok_ready, amix_ready, xc_ready, lru_m, gelu_in, lmix_f, lmix_ready, act_f, act_ready,
                      y_ready):
                s.prime(dve)
            chain = Chain(dve, dve_chain)
            link = chain.link
            TT = nc.vector.tensor_tensor
            TS = nc.vector.tensor_scalar
            STT = nc.vector.scalar_tensor_tensor
            dve.wait_ge(const_in, 16 * N_CONST)
            dve.wait_ge(zeroed, 7)

            lam = vec[:, VLAM:VLAM + LC]
            link(TS(set_t[:, 5, :], lam, -1.0, None, ALU.mult))
            TT(set_t[:, 0, :], set_t[:, 5, :], lam, ALU.max).then_inc(setup_done, 1)
            dve.wait_ge(setup_act, 1)
            e = set_t[:, 1, :]
            link(TS(set_t[:, 2, :], e, 2.0, None, ALU.add))
            link(nc.vector.reciprocal(set_t[:, 2, :], set_t[:, 2, :]))
            link(TT(set_t[:, 2, :], set_t[:, 2, :], e, ALU.mult))
            link(TT(set_t[:, 3, :], set_t[:, 2, :], set_t[:, 2, :], ALU.mult))
            link(TS(set_t[:, 4, :], set_t[:, 3, :], 1.0 / 19, None, ALU.mult))
            for k in (17, 15, 13, 11, 9, 7, 5, 3):
                link(STT(out=set_t[:, 4, :], in0=set_t[:, 4, :], scalar=1.0 / k, in1=set_t[:, 3, :],
                         op0=ALU.add, op1=ALU.mult))
            link(STT(out=set_t[:, 4, :], in0=set_t[:, 4, :], scalar=1.0, in1=set_t[:, 2, :],
                     op0=ALU.add, op1=ALU.mult))
            link(TS(set_t[:, 4, :], set_t[:, 4, :], 8.0, None, ALU.mult))
            link(TS(set_t[:, 5, :], set_t[:, 5, :], 0.0, 4.0, ALU.max, ALU.mult))
            link(TT(lru_c[:, 3, :], set_t[:, 4, :], set_t[:, 5, :], ALU.add))
            TS(lru_c[:, 2, :], lru_c[:, 3, :], -1.0, None, ALU.mult)
            TT(qb_t[:, :], vec[:, VB + U_Q[0]:VB + UH], vec[:, VQS:VQS + JT], ALU.mult)
            TS(lru_c[:, 0, :], vec[:, VBA:VBA + LC], 0.5, None, ALU.mult)
            TS(lru_c[:, 1, :], vec[:, VBI:VBI + LC], 0.5, None, ALU.mult).then_inc(setup_done, 1)

            def split(b, u, end=False):
                if end and u >= NU:
                    return
                w_hi_ready.wait(dve, b, u + 1)
                n = kt_of[u % NU] * P
                w_ready.by(TT(w_lo[:, u % RING, 0:n], w_raw[:, u % RAW, 0:n], w_hi[:, u % RING, 0:n], ALU.subtract))

            def evacuate(b, wide, u, op):
                for c, (c0, c1) in enumerate(chunks(wide)):
                    done(dve, b, u, c, wide)
                    ins = op(G[job(u, c, wide) % 3][:, 0:c1 - c0], c0, c1)
                    if c < len(chunks(wide)) - 1:
                        ins.then_inc(freed_half, 1)
                freed.by(ins)

            def scaled(dst):
                return lambda src, c0, c1: TT(dst(c0, c1), src, rinv[:, c0:c1], ALU.mult)

            def add_square(b, wide, kt, total, src, ready, added):
                w = W if wide else T
                ready.wait(dve, b, kt + 1)
                if kt == 0:
                    ins = nc.vector.tensor_copy(total[:, 0:w], src[:, 0:w])
                else:
                    added.wait(dve, b, kt)
                    ins = TT(total[:, 0:w], total[:, 0:w], src[:, 0:w], ALU.add)
                added.by(ins)

            def x_tile(n, wide, kt):
                w = W if wide else T
                add_square(n, wide, kt, ssum, sq[:, 1], sqx_ready, sqx_added)
                xhi_ready.wait(dve, n, kt + 1)
                xlo_ready.by(STT(out=x_lo[:, kt, 0:w], in0=xT[:, kt, 0:w], scalar=v(VG1 + kt),
                                 in1=x_hi[:, kt, 0:w], op0=ALU.mult, op1=ALU.subtract))

            def h_tile(b, wide, m):
                w = W if wide else T
                add_square(b, wide, m, ssum, sq[:, 0], sqh_ready, sqh_added)
                hhi_ready.wait(dve, b, m + 1)
                hlo_ready.by(STT(out=x_lo[:, m, 0:w], in0=hT[:, m, 0:w], scalar=v(VG2 + m),
                                 in1=x_hi[:, m, 0:w], op0=ALU.mult, op1=ALU.subtract))

            def y_tile(b, wide, m):
                add_square(b, wide, m, ssum_y, sq[:, 0], sqy_ready, sqy_added)

            def invert(b, wide, ready):
                w = W if wide else T
                ready.wait(dve, b, 1)
                link(nc.vector.reciprocal(rinv[:, 0:w], rinv[:, 0:w]))

            def y_scale(b, m):
                yT_done.wait(dve, b, m + 1)
                y_out[m % 2].wait(dve, b, m // 2)
                o = (S, TB)[m % 2]
                for h in range(2):
                    ins = STT(out=y_tok[:, m % 2, h * 512:(h + 1) * 512], in0=o[h][:, :],
                              scalar=rstd_t[:, m:m + 1], in1=gfin[:, h * 512:(h + 1) * 512],
                              op0=ALU.mult, op1=ALU.mult)
                y_ready.by(ins)

            def y_rstd(b, wide):
                stdy_ready.wait(dve, b, 1)
                if wide:
                    nc.vector.reciprocal(rstd_t[0:NS, QB:QB + 1], std_t[0:NS, QB:QB + 1])
                link(nc.vector.reciprocal(rstd_t[:, 0:QB], std_t[:, 0:QB]))

            def head(n, wide, b=None):
                link(nc.vector.tensor_copy(kT[:, 0:WINDOW], kT[:, T:T + WINDOW]))
                link(nc.vector.tensor_copy(v_tok[:, 0, :], v_tok[:, QB, :]))
                split(n, U_K + RING)
                invert(n, wide, stdx_ready)
                evacuate(n, wide, U_K, scaled(lambda c0, c1: kT[:, WINDOW + c0:WINDOW + c1]))
                evacuate(n, wide, U_V, scaled(lambda c0, c1: vT[:, c0:c1]))
                split(n, U_V + RING)
                if b is not None:
                    y_rstd(b, False)
                for j, u in enumerate(U_Q):
                    evacuate(n, wide, u, scaled(lambda c0, c1: qT[:, j, c0:c1]))
                    split(n, u + RING)
                    if b is not None and j == 0:
                        y_scale(b, 0)
                    if b is not None and j == 2:
                        y_scale(b, 1)
                        y_scale(b, 2)
                    if j == 1:
                        vT_done.wait(dve, n, 1)
                        v_ready.by(nc.vector.tensor_copy(v_tok[:, 1:1 + QB, :],
                                                         TB[0][:, :].rearrange("p (m q) -> p m q", m=QB)))
                if b is not None:
                    y_scale(b, 3)

            def mixers(b, last):
                def softmax_1(s):
                    qb, jp = s // 2, s % 2
                    sc_done.wait(dve, b, s + 1)
                    pT_done.wait(dve, b, s - 1)
                    link(nc.vector.memset(mx[:, s % 2, :], 0.0))
                    for hh in range(HH):
                        g, jj = hh // 2, hh % 2
                        head = g * JT + 2 * jp + jj
                        d = dist_b if qb == 0 else dist
                        ins = nc.vector.tensor_tensor_reduce(
                            s_p[:, s % 2, hh, :], S[g][:, jj * 256:(jj + 1) * 256], d[:, :], 2.0 ** -(head + 1),
                            sinks[:, head:head + 1], ALU.add, ALU.max, mx[:, s % 2, hh:hh + 1])
                    link(ins)
                    link(TS(nm[:, s % 2, :], mx[:, s % 2, :], -1.0, None, ALU.mult))
                    sk = sinks[:, :].rearrange("p (g j) -> p g j", g=NKV)[:, :, 2 * jp:2 * jp + 2]
                    sc_read.by(TT(sd[:, s % 2, :].rearrange("p (g j) -> p g j", g=NKV), sk,
                                  nm[:, s % 2, :].rearrange("p (g j) -> p g j", g=NKV), ALU.add))

                def softmax_2(s):
                    qb, jp = s // 2, s % 2
                    p_ready.wait(dve, b, s + 1)
                    link(TT(es[:, s % 2, :], es[:, s % 2, :], rs[:, s % 2, :], ALU.add))
                    ro = rec[:, qb % 2, :].rearrange("p (g j) -> p g j", g=NKV)[:, :, 2 * jp:2 * jp + 2]
                    link(nc.vector.reciprocal(ro, es[:, s % 2, :].rearrange("p (g j) -> p g j", g=NKV)))

                def probs_T(s):
                    pT_done.wait(dve, b, s + 1)
                    av_done.wait(dve, b, s - 1)
                    pTb_ready.by(nc.vector.tensor_copy(pT[:, s % 2, 4:8, :],
                                                       TB[1][:, :].rearrange("p (n q) -> p n q", n=4)))

                def attn_out(qb):
                    av_done.wait(dve, b, 2 * qb + 2)
                    attnT_done.wait(dve, b, qb)
                    bc = rec[:, qb % 2, :].rearrange("p (h o) -> p h o", o=1).to_broadcast([P, NH, HEAD])
                    atok_ready.by(TT(a_tok[:, :].rearrange("p (h d) -> p h d", h=NH),
                                     V[:, :].rearrange("p (h d) -> p h d", h=NH), bc, ALU.mult))

                def conv(c):
                    z_ready.wait(dve, b, UH + c + 1)
                    xi = xb[:, c % 2, :]
                    link(nc.vector.tensor_copy(xi[:, 0:CONV_W - 1], x_prev[:, c, :]))
                    nc.vector.tensor_copy(x_prev[:, c, :], xi[:, T:T + CONV_W - 1])
                    o = xc[:, c % 2, :]
                    lmix_f.wait(dve, b, c - 1)
                    link(TS(o, xi[:, 0:T], v(VCW + c), v(VCB + c), ALU.mult, ALU.add))
                    for k in range(1, CONV_W):
                        ins = STT(out=o, in0=xi[:, k:k + T], scalar=v(VCW + k * LC + c), in1=o,
                                  op0=ALU.mult, op1=ALU.add)
                        if k < CONV_W - 1:
                            link(ins)
                    if last:
                        link(ins)
                        ins = nc.vector.tensor_copy(xs_b[:, c, (CONV_W - 1) * DB:], xi[:, CONV_W - 1 + T:])
                    xc_ready.by(ins)

                def gelu_arg(c):
                    gelu_sq.wait(dve, b, c + 1)
                    g = gl[:, c % 2, :]
                    if last:
                        TS(ys_b[:, c, :], yb[:, c % 2, T:W], v(VB + U_Y[c]), None, ALU.add)
                    link(TS(g, g, GELU_K * GELU_C, GELU_K, ALU.mult, ALU.add))
                    gelu_in.by(STT(out=g, in0=yb[:, c % 2, 0:T], scalar=v(VB + U_Y[c]), in1=g,
                                   op0=ALU.add, op1=ALU.mult))

                def lru_square(c):
                    lru_exp.wait(dve, b, c + 1)
                    STT(out=ii[:, :], in0=ii[:, :], scalar=1.0, in1=xc[:, c % 2, :], op0=ALU.add, op1=ALU.mult)
                    lru_m.by(STT(out=qq[:, :], in0=om[:, :], scalar=1.0, in1=qq[:, :], op0=ALU.add, op1=ALU.mult))

                def lru_scan(c):
                    lru_sqrt.wait(dve, b, c + 1)
                    link(TT(ii[:, :], ii[:, :], qq[:, :], ALU.mult))
                    link(nc.vector.tensor_tensor_scan(om[:, :], ra[:, :], ii[:, :], h_prev[:, c:c + 1],
                                                      ALU.mult, ALU.add))
                    link(nc.vector.tensor_copy(h_prev[:, c:c + 1], om[:, T - 1:T]))

                def lru_mix(c):
                    g = gl[:, c % 2, :]
                    gelu_th.wait(dve, b, c + 1)
                    link(STT(out=g, in0=g, scalar=1.0, in1=om[:, :], op0=ALU.add, op1=ALU.mult))
                    lmix_f.by(STT(out=g, in0=yb[:, c % 2, 0:T], scalar=v(VB + U_Y[c]), in1=g,
                                  op0=ALU.add, op1=ALU.mult))

                def lru_lo(c):
                    lmix_hi.wait(dve, b, c + 1)
                    lmix_ready.by(STT(out=a_lo[:, KT - LC + c, 0:T], in0=gl[:, c % 2, :], scalar=0.5,
                                      in1=a_hi[:, KT - LC + c, 0:T], op0=ALU.mult, op1=ALU.subtract))

                def attn_lo(qb):
                    amix_hi.wait(dve, b, qb + 1)
                    amix_ready.by(TT(a_lo[:, 0:4, qb * P:(qb + 1) * P],
                                     V[:, :].rearrange("p (c q) -> p c q", c=4),
                                     a_hi[:, 0:4, qb * P:(qb + 1) * P], ALU.subtract))

                for s in range(NUN):
                    if s >= 1:
                        probs_T(s - 1)
                    softmax_1(s)
                    if s >= 2 and s % 2 == 0:
                        lru_square((s - 2) // 2)
                    if s >= 4 and s % 2 == 0:
                        lru_lo((s - 4) // 2)
                    if s >= 1:
                        softmax_2(s - 1)
                    if s >= 3 and s % 2 == 1:
                        attn_out((s - 3) // 2)
                    if s >= 1:
                        split(b, UH + s - 1 + RING)
                    if s >= 3 and s % 2 == 1:
                        lru_mix((s - 3) // 2)
                    kind, c = ORDER[s]
                    if kind == "x":
                        evacuate(b, last, UH + s, scaled(
                            lambda c0, c1: xb[:, c % 2, CONV_W - 1 + c0:CONV_W - 1 + c1]))
                    else:
                        evacuate(b, last, UH + s, scaled(lambda c0, c1: yb[:, c % 2, c0:c1]))
                    if s >= 3 and s % 2 == 1:
                        attn_lo((s - 3) // 2)
                    if kind == "x":
                        conv(c)
                    if s >= 2 and s % 2 == 0:
                        lru_scan((s - 2) // 2)
                    if kind == "y":
                        gelu_arg(c)
                lru_lo(LC - 2)
                probs_T(NUN - 1)
                lru_square(LC - 1)
                softmax_2(NUN - 1)
                attn_out(QB - 1)
                split(b, UH + NUN - 1 + RING)
                lru_scan(LC - 1)
                attn_lo(QB - 1)
                lru_mix(LC - 1)
                lru_lo(LC - 1)
                if last:
                    sample_dve(b)
                else:
                    link(nc.vector.tensor_copy(dist_b[:, :], dist[:, :]))
                for m, u in enumerate(U_O):
                    evacuate(b, last, u, lambda src, c0, c1: STT(
                        out=hT[:, m, c0:c1], in0=src, scalar=v(VBO + m), in1=xT[:, m, c0:c1],
                        op0=ALU.add, op1=ALU.add))
                    split(b, u + RING)
                    h_tile(b, last, m)

            def sample_dve(b):
                n = [0]

                def by(ins, want=None):
                    n[0] += 1
                    ins.then_inc(smp_dve, 1)
                    dve.wait_ge(smp_dve, n[0])
                    assert want is None or want == n[0], (want, n[0])

                D3 = (CONV_W - 1) * DB
                by(nc.vector.memset(q_d[:, :, :], 0.0))
                R = DT * JT
                for bb in range(DB):
                    src = qT[:, :, T + bb:W:DB]
                    nc.vector.tensor_copy(q_d[:, bb, bb * R:(bb + 1) * R].rearrange("p (j t) -> p j t", j=JT), src)
                    ins = nc.vector.tensor_copy(q_r[:, bb * R:(bb + 1) * R].rearrange("p (j t) -> p j t", j=JT), src)
                link(ins)
                dve.wait_ge(smp_pe, 2)
                sv = S[0][:, 0:LC * CONV_W * DB].rearrange("p (c r) -> p c r", c=LC)
                nc.vector.tensor_copy(xs_b[:, :, 0:D3], sv[:, :, 0:D3])
                link(nc.vector.tensor_copy(hs0[:, :, :], sv[:, :, D3:D3 + DB]))
                dve.wait_ge(smp_pe, 3)
                nc.vector.tensor_copy(kc_T[:, 0:4, :], TB[0][:, :].rearrange("p (n q) -> p n q", n=4))
                by(nc.vector.tensor_copy(kc_T[:, 4:8, :], TB[1][:, :].rearrange("p (n q) -> p n q", n=4)), SMP_DVE_Q)
                dve.wait_ge(smp_pe, 4)
                nc.vector.tensor_copy(vs_tok[:, :], V[0:NS, 0:P])
                nc.vector.tensor_copy(ks_out[:, :], V[0:NS, P:2 * P])
                link(nc.vector.tensor_copy(k_out[:, :], V[:, 2 * P:3 * P]))
                for c in range(LC):
                    ins = TS(xc_s[:, c, :], xs_b[:, c, 0:NS], v(VCW + c), v(VCB + c), ALU.mult, ALU.add)
                link(ins)
                for k in range(1, CONV_W):
                    for c in range(LC):
                        ins = STT(out=xc_s[:, c, :], in0=xs_b[:, c, k * DB:k * DB + NS], scalar=v(VCW + k * LC + c),
                                  in1=xc_s[:, c, :], op0=ALU.mult, op1=ALU.add)
                    link(ins)
                dve.wait_ge(smp_pe, 5)
                dve.wait_ge(smp_in, 16 * 7)
                for g in range(NKV):
                    ins = nc.vector.tensor_tensor_reduce(s_s[:, g, :], S[g][:, 0:SC], dist_s[:, :], rows[:, g:g + 1],
                                                         sink_s[:, g:g + 1], ALU.add, ALU.max, mx_s[:, 0, g:g + 1])
                link(ins)
                link(TS(mx_s[:, 1, :], mx_s[:, 0, :], -1.0, None, ALU.mult))
                by(TT(mx_s[:, 4, :], sink_s[:, :], mx_s[:, 1, :], ALU.add), SMP_DVE_S)
                link(TT(l_s[4][:, :, :], ys_b[:, :, :], ys_b[:, :, :], ALU.mult))
                link(TS(l_s[4][:, :, :], l_s[4][:, :, :], GELU_K * GELU_C, GELU_K, ALU.mult, ALU.add))
                by(TT(l_s[4][:, :, :], l_s[4][:, :, :], ys_b[:, :, :], ALU.mult), SMP_DVE_GI)
                dve.wait_ge(smp_act, 1)
                link(TT(mx_s[:, 3, :], mx_s[:, 3, :], mx_s[:, 2, :], ALU.add))
                link(nc.vector.reciprocal(mx_s[:, 5, :], mx_s[:, 3, :]))
                for g in range(NKV):
                    ins = TS(s_s[:, g, :], s_s[:, g, :], mx_s[:, 5, g:g + 1], None, ALU.mult)
                by(ins, SMP_DVE_P)
                dve.wait_ge(smp_pe, 6)
                nc.vector.tensor_copy(pcT[:, :, :], TB[0][:, 0:2 * P].rearrange("p (g q) -> p g q", g=NKV))
                by(nc.vector.tensor_copy(pnT[:, :, :], TB[1][0:NS, 0:2 * P].rearrange("p (g q) -> p g q", g=NKV)),
                   SMP_DVE_PT)
                dve.wait_ge(smp_dve, SMP_DVE_PT)
                nc.vector.tensor_copy(outc[:, :, 0:(DT - 1) * DB], xs_b[:, :, D3 + DB:D3 + NS])
                nc.vector.tensor_copy(outc[:, :, DT * DB:DT * DB + CONV_W - 1], x_prev[:, :, :])
                by(nc.vector.tensor_copy(outc[:, :, SCOLS - 1], h_prev[:, :]), SMP_DVE_XC)
                dve.wait_ge(smp_pe, 7)
                for g in range(NKV):
                    for j in range(JT):
                        src = (V, TB[0])[g][0:HEAD, 0:P].rearrange("p (b j t) -> p j t b", b=DB, j=JT)[:, j]
                        lo = j % 2 * HEAD
                        head = g * JT + j
                        dst = mixs[lo:lo + HEAD, head // 2, :].rearrange("p (t b) -> p t b", t=DT)
                        ins = nc.vector.tensor_copy(dst, src)
                link(ins)
                dve.wait_ge(smp_act, 2)
                t, i_, q_, gth = l_s[3], l_s[1], l_s[2], l_s[4]
                link(TT(l_s[0][:, :, :], t[:, :, :], t[:, :, :], ALU.mult))
                STT(out=i_[:, :, :], in0=i_[:, :, :], scalar=1.0, in1=xc_s[:, :, :], op0=ALU.add, op1=ALU.mult)
                by(STT(out=q_[:, :, :], in0=l_s[0][:, :, :], scalar=1.0, in1=q_[:, :, :], op0=ALU.add, op1=ALU.mult),
                   SMP_DVE_M)
                dve.wait_ge(smp_act, 3)
                link(TT(i_[:, :, :], i_[:, :, :], q_[:, :, :], ALU.mult))
                hs = l_s[5]
                for k in range(DT):
                    prev = hs0[:, :, :] if k == 0 else hs[:, :, (k - 1) * DB:k * DB]
                    cur = slice(k * DB, (k + 1) * DB)
                    link(TT(hs[:, :, cur], t[:, :, cur], prev, ALU.mult))
                    link(TT(hs[:, :, cur], hs[:, :, cur], i_[:, :, cur], ALU.add))
                by(nc.vector.tensor_copy(outc[:, :, (DT - 1) * DB:DT * DB], hs[:, :, NS - DB:NS]), SMP_DVE_OUTC)
                link(STT(out=gth[:, :, :], in0=gth[:, :, :], scalar=1.0, in1=ys_b[:, :, :], op0=ALU.add, op1=ALU.mult))
                by(STT(out=mixs[:, KT - LC:KT, :], in0=gth[:, :, :], scalar=0.5, in1=hs[:, :, :],
                       op0=ALU.mult, op1=ALU.mult), SMP_DVE_MIXF)
                dve.wait_ge(smp_act, 4)
                by(TT(a_lo[:, :, T:W], mixs[:, :, :], a_hi[:, :, T:W], ALU.subtract), SMP_DVE_MIX)
                dve.wait_ge(smp_pe, 9)
                by(nc.vector.tensor_copy(outr[:, :], TB[1][0:SCOLS, :]), SMP_DVE_OUT)

            def ffn(b, last):
                w = W if last else T
                f0 = 0
                for ci, nf in enumerate(FCH):
                    for f, (ug, uu) in enumerate(U_IN[ci]):
                        n = f0 + f
                        if n == 0:
                            split(b, ug + RING)
                            invert(b, last, stdh_ready)
                        evacuate(b, last, ug, scaled(lambda c0, c1: gt[:, c0:c1]))
                        if n > 0:
                            split(b, ug + RING)
                        gate_tanh.wait(dve, b, n + 1)
                        link(STT(out=gt[:, 0:w], in0=th[:, 0:w], scalar=1.0, in1=gt[:, 0:w],
                                 op0=ALU.add, op1=ALU.mult))
                        evacuate(b, last, uu, scaled(lambda c0, c1: a32[:, n % 2, c0:c1]))
                        freed.wait(dve, b, uu + 1)
                        act_f.by(STT(out=a32[:, n % 2, 0:w], in0=gt[:, 0:w], scalar=0.5, in1=a32[:, n % 2, 0:w],
                                     op0=ALU.mult, op1=ALU.mult))
                        split(b, uu + RING, last)
                        act_hi.wait(dve, b, n + 1)
                        act_ready.by(TT(a_lo[:, f, 0:w], a32[:, n % 2, 0:w], a_hi[:, f, 0:w], ALU.subtract))
                    for m, u in enumerate(U_OUT[ci]):
                        evacuate(b, last, u, lambda src, c0, c1: TT(hT[:, m, c0:c1], src, hT[:, m, c0:c1], ALU.add))
                        split(b, u + RING, last)
                        if ci == len(FCH) - 1:
                            if not last:
                                x_tile(b + 1, False, m)
                            y_tile(b, last, m)
                    f0 += nf

            for u in range(RING):
                split(0, u)
            for kt in range(KT):
                x_tile(0, True, kt)
            head(0, True)
            chain.restart()
            with dve.Fori(0, NB - 1) as b:
                mixers(b, False)
                ffn(b, False)
                head(b + 1, False, b)
                chain.restart()
            b = NB - 1
            mixers(b, True)
            ffn(b, True)
            y_rstd(b, True)
            dve.wait_ge(smp_out, 16 * (2 + 2 + 2 * DT + CONV_W - 1 + 3))
            for m in range(QB):
                y_scale(b, m)
            dve.wait_ge(smp_pe, 10)
            y_out[0].wait(dve, b, 2)
            for h in range(2):
                ins = STT(out=y_tok[0:NS, 0, h * 512:(h + 1) * 512], in0=S[h][0:NS, :],
                          scalar=rstd_t[0:NS, QB:QB + 1], in1=gfin[0:NS, h * 512:(h + 1) * 512],
                          op0=ALU.mult, op1=ALU.mult)
            ins.then_inc(smp_dve, 1)


(SMP_DVE_Z, SMP_DVE_Q, SMP_DVE_S, SMP_DVE_GI, SMP_DVE_P, SMP_DVE_PT, SMP_DVE_XC, SMP_DVE_M, SMP_DVE_OUTC,
 SMP_DVE_MIXF, SMP_DVE_MIX, SMP_DVE_OUT, SMP_DVE_Y) = range(1, 14)


def kernel(x_prompt, x_sample, cache_k, cache_v, state_conv, state_h, g_mix, w_in, b_in, attn_sinks, conv_w,
           conv_b, w_a, b_a, w_i, b_i, lam, w_out, b_out, g_ffn, w_ffn_in, w_ffn_out, g_final):
    import numpy as np
    import concourse.bacc as bacc
    from concourse.bass_utils import run_bass_kernel_spmd

    f = np.float32
    A = {k: np.asarray(v) for k, v in dict(
        x_prompt=x_prompt, x_sample=x_sample, cache_k=cache_k, cache_v=cache_v, state_conv=state_conv,
        state_h=state_h, w_a=w_a, w_i=w_i).items()}
    DM = A["x_prompt"].shape[2]
    SEQ = A["x_prompt"].shape[1]
    DB, DT = A["x_sample"].shape[:2]
    KT = DM // P
    wi, wo = np.asarray(w_in)[0], np.asarray(w_out)[0]
    fi, fo = np.asarray(w_ffn_in)[0], np.asarray(w_ffn_out)[0]
    FF = fo.shape[0]
    NF = FF // P
    sinks = np.asarray(attn_sinks)[0]
    NH = sinks.shape[0]
    JT = NH // 2
    QE = NH * HEAD
    KE, VE = QE + 2 * HEAD, QE + 4 * HEAD
    LRU = A["state_h"].shape[2]
    LC = LRU // P
    cols = [np.arange(QE, KE), np.arange(KE, VE)]
    for j in range(JT):
        cols.append(np.concatenate([np.arange(j * HEAD, (j + 1) * HEAD),
                                    np.arange((j + JT) * HEAD, (j + JT + 1) * HEAD)]))
    for kind, c in branch_order(LC):
        cols.append(VE + (LRU if kind == "y" else 0) + c * P + np.arange(P))
    packed = []

    def pack(w):
        k = w.shape[0] // P
        u = np.zeros((P, KT * P), f)
        u[:, 0:k * P] = w.reshape(k, P, P).transpose(1, 0, 2).reshape(P, k * P)
        packed.append(u)

    for c in cols:
        pack(wi[:, c])
    for m in range(KT):
        pack(wo[:, m * P:(m + 1) * P])
    n = -(-NF // KT)
    at = 0
    for i in range(n):
        nf = NF // n + (i < NF % n)
        for t in range(at, at + nf):
            pack(fi[:, t * P:(t + 1) * P])
            pack(fi[:, FF + t * P:FF + (t + 1) * P])
        for m in range(KT):
            pack(fo[at * P:(at + nf) * P, m * P:(m + 1) * P])
        at += nf
    A["units"] = np.stack(packed)

    def tiles(a):
        a = np.asarray(a)
        return a.reshape(-1, P).T

    half = np.arange(P) // HEAD
    qs = np.stack([2.0 ** (j + JT * half + 1) / 8 for j in range(JT)], 1).astype(f)
    bi = np.asarray(b_in)[0]
    A["vecs"] = np.ascontiguousarray(np.concatenate(
        [np.stack([bi[c] for c in cols], 1), tiles(g_mix), tiles(b_out), tiles(g_ffn), tiles(conv_w),
         tiles(conv_b), tiles(b_a), tiles(b_i), tiles(lam), qs], 1))
    A["sinks_p"] = np.ascontiguousarray(np.broadcast_to(sinks, (P, NH)))
    jr = np.arange(P) // DT % JT
    tr = np.arange(P) % DT
    br = np.arange(P) // (DT * JT)
    A["sinks_s"] = np.ascontiguousarray(np.stack([sinks[jr], sinks[JT + jr]], 1))
    A["g_fin"] = np.ascontiguousarray(np.broadcast_to(np.asarray(g_final), (P, DM)))
    A["ident_in"] = np.eye(P, dtype=f)
    FAR = -1e30 * 2.0 ** NH
    i, j = np.arange(P)[:, None], np.arange(2 * P)[None]
    d = P + i - j
    A["dist_in"] = np.stack([np.where((d >= 0) & (d < P), -d, FAR),
                             np.where((d >= 0) & (d < P) & (j >= P), -d, FAR)]).astype(f)
    dc = P + tr[:, None] - np.arange(P)[None]
    tn, bn = np.arange(DB * DT)[None] // DB, np.arange(DB * DT)[None] % DB
    dn = tr[:, None] - tn
    A["dist_s_in"] = np.concatenate([np.where((dc >= 0) & (dc < P), -dc, FAR),
                                     np.where((dn >= 0) & (bn == br[:, None]), -dn, FAR)], 1).astype(f)
    A["per_row"] = np.stack([2.0 ** -(jr + 1.0), 2.0 ** -(JT + jr + 1.0), 0 * jr, 0 * jr], 1).astype(f)

    outs = [("y_p", (1, SEQ, DM)), ("y_s", (DB, DT, DM)), ("nk_p", (1, 1, WINDOW, 2, HEAD)),
            ("nv_p", (1, 1, WINDOW, 2, HEAD)), ("nc_p", (1, 1, CONV_W - 1, LRU)), ("nh_p", (1, 1, LRU)),
            ("nk_s", (1, DB, WINDOW, 2, HEAD)), ("nv_s", (1, DB, WINDOW, 2, HEAD)),
            ("nc_s", (1, DB, CONV_W - 1, LRU)), ("nh_s", (1, DB, LRU))]
    nc = bacc.Bacc("TRN2", target_bir_lowering=False, num_devices=1)
    order = ["x_prompt", "x_sample", "cache_k", "cache_v", "state_conv", "state_h", "units", "vecs", "w_a", "w_i",
             "sinks_p", "sinks_s", "g_fin", "ident_in", "dist_in", "dist_s_in", "per_row"]
    arrays, args = {}, []
    for name in order:
        a = np.ascontiguousarray(A[name])
        arrays[f"in_{name}"] = a
        args.append(nc.dram_tensor(f"in_{name}", a.shape, mybir.dt.from_np(a.dtype), kind="ExternalInput").ap())
    for name, shape in outs:
        args.append(nc.dram_tensor(f"out_{name}", shape, F32, kind="ExternalOutput").ap())
    hymba_layer(nc, *args, FF)
    r = run_bass_kernel_spmd(nc, [arrays], core_ids=[0])
    return tuple(r.results[0][f"out_{name}"] for name, _ in outs)
```

```python
import concourse.bass as bass
from concourse import mybir
from contextlib import ExitStack

F32 = mybir.dt.float32
F32R = mybir.dt.float32r
ALU = mybir.AluOpType
ACT = mybir.ActivationFunctionType

P = 128
WINDOW = 128
HEAD = 64
EPS = 1e-6
GELU_K = 0.7978845608028654
GELU_C = 0.044715
CONV_W = 4
RING = 3
RAW = 2


def branch_order(n):
    order = [("x", 0)]
    for c in range(1, n):
        order += [("x", c), ("y", c - 1)]
    return order + [("y", n - 1)]


class Signal:

    def __init__(self, sem, per_block, step=1, primed=True):
        self.sem, self.per, self.step, self.primed = sem, per_block, step, primed

    def prime(self, eng):
        eng.sem_inc(self.sem, self.per * self.step)

    def wait(self, eng, b, k):
        eng.wait_ge(self.sem, (b * self.per + (self.per if self.primed else 0) + k) * self.step)

    def by(self, ins):
        ins.then_inc(self.sem, self.step)


class Chain:

    def __init__(self, eng, sem):
        self.eng, self.sem, self.n = eng, sem, 0

    def link(self, ins):
        ins.then_inc(self.sem, 1)
        self.n += 1
        self.eng.wait_ge(self.sem, self.n)

    def restart(self):
        if self.n:
            self.eng.sem_clear(self.sem)
            self.n = 0


def hymba_layer(nc, x_p, x_s, cache_k, cache_v, conv_in, h_in, units, vecs, w_a, w_i, sinks_p, sinks_s,
                g_fin, ident_in, dist_in, dist_s_in, per_row,
                y_p, y_s, nk_p, nv_p, nc_p, nh_p, nk_s, nv_s, nc_s, nh_s, d_ff):
    SEQ, DM = x_p.shape[1], x_p.shape[2]
    DB, DT = x_s.shape[0], x_s.shape[1]
    NS = DB * DT
    T = 512
    NB = SEQ // T
    W = T + NS
    QB = T // WINDOW
    KT = DM // P
    NKV = 2
    LC = conv_in.shape[3] // P
    NH = sinks_p.shape[1]
    JT = NH // NKV
    NF = d_ff // P
    FCH = []
    n = -(-NF // KT)
    for i in range(n):
        FCH.append(NF // n + (i < NF % n))

    U_K, U_V = 0, 1
    U_Q = [2 + j for j in range(JT)]
    UH = 2 + JT
    ORDER = branch_order(LC)
    U_X = [UH + ORDER.index(("x", c)) for c in range(LC)]
    U_Y = [UH + ORDER.index(("y", c)) for c in range(LC)]
    U_O = [UH + 2 * LC + m for m in range(KT)]
    U_IN, U_OUT, at = [], [], UH + 2 * LC + KT
    for nf in FCH:
        U_IN.append([(at + 2 * f, at + 2 * f + 1) for f in range(nf)])
        U_OUT.append([at + 2 * nf + m for m in range(KT)])
        at += 2 * nf + KT
    NU = at
    assert NU % RING == 0 and NU % RAW == 0 and UH % 3 == 0, (NU, NF, FCH)
    kt_of = [KT] * NU
    for nf, outs in zip(FCH, U_OUT):
        for u in outs:
            kt_of[u] = nf

    def chunks(wide):
        return [(0, W // 2), (W // 2, W)] if wide else [(0, T)]

    def job(u, c, wide):
        base = 0 if u < UH else UH
        return 2 * (u - base) + c if wide else u

    ctx = ExitStack()
    with ctx:
        ctx.enter_context(nc.allow_non_contiguous_dma("small state vectors"))

        top = [-(-nc.sbuf_base // 64) * 64]

        def place(name, shape, dt=F32, at=None):
            size = 4
            for s in shape[1:]:
                size *= s
            size = -(-size // 64) * 64
            where = top[0] if at is None else at[0]
            t = nc.alloc_sbuf_tensor_at(name, list(shape), dt, offset=where)
            if at is None:
                top[0] += size
            else:
                at[0] += size
            return t

        w_raw = place("w_raw", [P, RAW, KT * P])
        w_hi = place("w_hi", [P, RING, KT * P], F32R)
        w_lo = place("w_lo", [P, RING, KT * P], F32R)
        xT = place("xT", [P, KT, W])
        h_at = [top[0]]
        hT = place("hT", [P, KT, W])
        h_end = top[0]
        a_hi = place("a_hi", [P, KT, W], F32R)
        a_lo = place("a_lo", [P, KT, W], F32R)
        x_at = [top[0]]
        x_hi = place("x_hi", [P, KT, W], F32R)
        x_lo = place("x_lo", [P, KT, W], F32R)
        qT = place("qT", [P, JT, W])
        kT = place("kT", [P, WINDOW + W])
        vT_s = place("vT_s", [P, NS])
        v_tok = place("v_tok", [P, 1 + QB, P])
        ident = place("ident", [P, P])
        ones = place("ones", [P, P])
        dist = place("dist", [P, 2 * WINDOW])
        dist_b = place("dist_b", [P, 2 * WINDOW])
        sinks = place("sinks", [P, NH])
        gates_w = place("gates_w", [P, 2, LC, P])
        gfin = place("gfin", [P, DM])
        vec = place("vec", [P, vecs.shape[1]])
        rows = place("rows", [P, 4])
        sink_s = place("sink_s", [P, NKV])
        lru_c = place("lru_c", [P, 4, LC])
        set_t = place("set_t", [P, 6, LC])
        qb_t = place("qb_t", [P, JT])
        eps_t = place("eps_t", [P, 1])
        x_prev = place("x_prev", [P, LC, CONV_W - 1])
        h_prev = place("h_prev", [P, LC])
        a_tok = place("a_tok", [P, NH * HEAD], at=[top[0]])
        ssum = place("ssum", [P, W])
        rinv = place("rinv", [P, W])
        mx = place("mx", [P, 2, NH // 2])
        nm = place("nm", [P, 2, NH // 2])
        sd = place("sd", [P, 2, NH // 2])
        rs = place("rs", [P, 2, NH // 2])
        es = place("es", [P, 2, NH // 2])
        rec = place("rec", [P, 2, NH])
        std_t = place("std_t", [P, QB + 1])
        rstd_t = place("rstd_t", [P, QB + 1])
        xs_b = place("xs_b", [P, LC, (CONV_W - 1) * DB + NS])
        ys_b = place("ys_b", [P, LC, NS])
        HH = NH // 2

        r = top[0]
        x_tok = place("x_tok", [P, QB, DM])
        a2 = [r]
        s_p = place("s_p", [P, 2, HH, 2 * WINDOW], at=a2)
        pT = place("pT", [P, 2, HH * 2, P], at=a2)
        top[0] = max(top[0], a2[0])
        r = top[0]
        xb = place("xb", [P, 2, CONV_W - 1 + W])
        vT = place("vT", [P, W], at=[top[0]])
        yb = place("yb", [P, 2, W])
        xc = place("xc", [P, 2, T])
        a3 = [r]
        th = place("th", [P, W], at=a3)
        gt = place("gt", [P, W], at=a3)
        a32 = place("a32", [P, 2, W], at=a3)
        sq = place("sq", [P, 2, W], at=a3)
        top[0] = max(top[0], a3[0])
        r = top[0]
        gl = place("gl", [P, 2, T])
        ra = place("ra", [P, T])
        ii = place("ii", [P, T])
        qq = place("qq", [P, T])
        om = place("om", [P, T])
        a2 = [r]
        y_tok = place("y_tok", [P, 2, DM], at=a2)
        ssum_y = place("ssum_y", [P, W], at=a2)
        top[0] = max(top[0], a2[0])
        xs_tok = place("xs_tok", [NS, DM], at=[r])
        SCOLS = (DT - 1) * DB + DB + CONV_W - 1 + 1
        outr = place("outr", [SCOLS, LC * P], at=[r])
        assert top[0] <= nc.sbuf_usable_end, top[0]

        SC = WINDOW + NS
        c_at = [h_at[0]]
        kc_tok = place("kc_tok", [P, DB, P], at=h_at)
        v_at = [h_at[0]]
        vc_tok = place("vc_tok", [P, DB, P], at=h_at)
        s_at = [h_at[0]]
        st_s = place("st_s", [(CONV_W - 1) * DB + DB, LC * P], at=h_at)
        k_at = [h_at[0]]
        kc_T = place("kc_T", [P, DB, P], at=h_at)
        dist_s = place("dist_s", [P, SC], at=h_at)
        s_s = place("s_s", [P, NKV, SC], at=h_at)
        q_r = place("q_r", [P, P], at=h_at)
        xc_s = place("xc_s", [P, LC, NS], at=h_at)
        hs0 = place("hs0", [P, LC, DB], at=h_at)
        assert h_at[0] <= h_end
        q_d = place("q_d", [P, DB, P], at=c_at)
        vs_tok = place("vs_tok", [NS, P], at=s_at)
        ks_out = place("ks_out", [NS, P], at=s_at)
        k_out = place("k_out", [P, P], at=s_at)
        mx_s = place("mx_s", [P, 6, NKV], at=s_at)
        pcT = place("pcT", [P, NKV, P], at=k_at)
        pnT = place("pnT", [NS, NKV, P], at=k_at)
        mixs = place("mixs", [P, KT, NS], at=k_at)
        l_s = [place(f"l_s{i}", [P, LC, NS], at=v_at) for i in range(6)]
        outc = place("outc", [P, LC, SCOLS], at=v_at)

        bank = [ctx.enter_context(nc.psum_tensor(f"bank{i}", [P, 512], F32)) for i in range(8)]
        G = bank[0:3]
        S = bank[3:5]
        TB = bank[5:7]
        V = bank[7]

        def sem(name):
            return ctx.enter_context(nc.semaphore(name))

        raw_in = [Signal(sem(f"raw_in{i}"), NU // RAW, 16) for i in range(RAW)]
        w_hi_ready = Signal(sem("w_hi_ready"), NU)
        w_ready = Signal(sem("w_ready"), NU)
        gemm_done = Signal(sem("gemm_done"), NU)
        gemm_half = sem("gemm_half")
        freed = Signal(sem("freed"), NU)
        freed_half = sem("freed_half")
        z_ready = Signal(sem("z_ready"), UH + LC)
        x_in = Signal(sem("x_in"), QB, 16, primed=False)
        xT_done = Signal(sem("xT_done"), KT)
        sqx_ready = Signal(sem("sqx_ready"), KT)
        sqx_added = Signal(sem("sqx_added"), KT)
        xhi_ready = Signal(sem("xhi_ready"), KT)
        xlo_ready = Signal(sem("xlo_ready"), KT)
        sqh_ready = Signal(sem("sqh_ready"), KT)
        sqh_added = Signal(sem("sqh_added"), KT)
        hhi_ready = Signal(sem("hhi_ready"), KT)
        hlo_ready = Signal(sem("hlo_ready"), KT)
        sqy_ready = Signal(sem("sqy_ready"), KT)
        sqy_added = Signal(sem("sqy_added"), KT)
        statx_done = Signal(sem("statx_done"), 1)
        stath_done = Signal(sem("stath_done"), 1)
        staty_done = Signal(sem("staty_done"), 1)
        stdx_ready = Signal(sem("stdx_ready"), 1)
        stdh_ready = Signal(sem("stdh_ready"), 1)
        stdy_ready = Signal(sem("stdy_ready"), 1)
        vT_done = Signal(sem("vT_done"), 1)
        v_ready = Signal(sem("v_ready"), 1)
        NUN = 2 * QB
        sc_done = Signal(sem("sc_done"), NUN)
        sc_read = Signal(sem("sc_read"), NUN)
        p_ready = Signal(sem("p_ready"), NUN)
        pT_done = Signal(sem("pT_done"), NUN)
        pTa_ready = Signal(sem("pTa_ready"), NUN)
        pTb_ready = Signal(sem("pTb_ready"), NUN)
        av_done = Signal(sem("av_done"), NUN)
        atok_ready = Signal(sem("atok_ready"), QB)
        attnT_done = Signal(sem("attnT_done"), QB)
        attn_moved = Signal(sem("attn_moved"), QB)
        amix_hi = Signal(sem("amix_hi"), QB)
        amix_ready = Signal(sem("amix_ready"), QB)
        xc_ready = Signal(sem("xc_ready"), LC)
        gates_done = Signal(sem("gates_done"), LC)
        gates_read = Signal(sem("gates_read"), LC)
        gelu_sq = Signal(sem("gelu_sq"), LC)
        gelu_in = Signal(sem("gelu_in"), LC)
        gelu_th = Signal(sem("gelu_th"), LC)
        lru_exp = Signal(sem("lru_exp"), LC)
        lru_m = Signal(sem("lru_m"), LC)
        lru_sqrt = Signal(sem("lru_sqrt"), LC)
        lmix_f = Signal(sem("lmix_f"), LC)
        lmix_hi = Signal(sem("lmix_hi"), LC)
        lmix_ready = Signal(sem("lmix_ready"), LC)
        gate_tanh = Signal(sem("gate_tanh"), NF)
        act_f = Signal(sem("act_f"), NF)
        act_hi = Signal(sem("act_hi"), NF)
        act_ready = Signal(sem("act_ready"), NF)
        yT_done = Signal(sem("yT_done"), QB)
        y_ready = Signal(sem("y_ready"), QB)
        y_out = [Signal(sem(f"y_out{i}"), QB // 2, 16) for i in range(2)]
        first_in = sem("first_in")
        const_in = sem("const_in")
        zeroed = sem("zeroed")
        setup_act = sem("setup_act")
        setup_done = sem("setup_done")
        xs_in = sem("xs_in")
        smp_in = sem("smp_in")
        cache_out = sem("cache_out")
        kv_out = sem("kv_out")
        state_out = sem("state_out")
        ys_out = sem("ys_out")
        smp_pe = sem("smp_pe")
        smp_act = sem("smp_act")
        smp_dve = sem("smp_dve")
        dve_chain = sem("dve_chain")
        act_chain = sem("act_chain")

        VB = 0
        VG1 = VB + UH + 2 * LC
        VBO = VG1 + KT
        VG2 = VBO + KT
        VCW = VG2 + KT
        VCB = VCW + CONV_W * LC
        VBA = VCB + LC
        VBI = VBA + LC
        VLAM = VBI + LC
        VQS = VLAM + LC

        def v(i):
            return vec[:, i:i + 1]

        N_FIRST = 2
        N_CONST = 10
        N_KV_OUT = 2 + 2 * DT
        N_STATE_OUT = CONV_W - 1 + 3

        def done(eng, b, u, c, wide):
            if wide and u >= 0 and c == 0:
                eng.wait_ge(gemm_half, u + 1)
            else:
                gemm_done.wait(eng, b, u + 1)

        def unit_done(eng, b, u):
            gemm_done.wait(eng, b, u + 1)

        block = ctx.enter_context(nc.Block())

        @block.sync
        def _(sp):
            for s in raw_in:
                s.prime(sp)

            def load_unit(b, u):
                w_ready.wait(sp, b, u - RAW + 1)
                n = kt_of[u % NU] * P
                raw_in[u % RAW].by(sp.dma_start(w_raw[:, u % RAW, 0:n], units[u % NU, :, 0:n]))

            w_ready.wait(sp, 0, 0)
            for u in range(RAW):
                load_unit(0, u)
            with sp.Fori(0, NB - 1) as b:
                for u in range(RAW, NU + RAW):
                    load_unit(b, u)
            for u in range(RAW, NU):
                load_unit(NB - 1, u)

        @block.gpsimd
        def _(pool):
            def load_x(b):
                for m in range(QB):
                    x_in.by(pool.dma_start(x_tok[:, m, :], x_p[0, bass.ds(b * T + m * P, P), :]))

            load_x(0)
            nc.gpsimd.memset(gates_w[:, :, :, :], 0.0).then_inc(zeroed, 1)
            nc.gpsimd.memset(ones[:, :], 1.0).then_inc(zeroed, 1)
            nc.gpsimd.memset(eps_t[:, :], EPS).then_inc(zeroed, 1)
            nc.gpsimd.memset(kT[:, :], 0.0).then_inc(zeroed, 1)
            nc.gpsimd.memset(v_tok[:, :, :], 0.0).then_inc(zeroed, 1)
            nc.gpsimd.memset(x_prev[:, :, :], 0.0).then_inc(zeroed, 1)
            nc.gpsimd.memset(h_prev[:, :], 0.0).then_inc(zeroed, 1)
            for dst, src in ((dist[:, :], dist_in[0]), (dist_b[:, :], dist_in[1]), (sinks[:, :], sinks_p),
                             (gfin[:, :], g_fin), (rows[:, :], per_row), (sink_s[:, :], sinks_s)):
                pool.dma_start(dst, src).then_inc(const_in, 16)
            pool.wait_ge(zeroed, 1)
            for n, w in enumerate((w_a, w_i)):
                for half in range(2):
                    lo = half * HEAD
                    pool.dma_start(gates_w[lo:lo + HEAD, n, :, lo:lo + HEAD],
                                   w[0, half::2].rearrange("n d e -> d n e")).then_inc(const_in, 16)

            for o, c in ((nk_s, cache_k), (nv_s, cache_v)):
                pool.dma_start(o[0, :, 0:WINDOW - DT].rearrange("b s g d -> b (s g d)"),
                               c[0, :, DT:WINDOW].rearrange("b s g d -> b (s g d)")).then_inc(cache_out, 16)

            with pool.Fori(0, NB - 1) as b:
                amix_ready.wait(pool, b, QB)
                xT_done.wait(pool, b, KT)
                load_x(b + 1)
            b = NB - 1
            yT_done.wait(pool, b, 0)
            for dst, src in ((kc_tok[:, :, :], cache_k[0].rearrange("b s g d -> s b (g d)")),
                             (vc_tok[:, :, :], cache_v[0].rearrange("b s g d -> s b (g d)")),
                             (dist_s[:, :], dist_s_in)):
                pool.dma_start(dst, src).then_inc(smp_in, 16)
            for t in range(CONV_W - 1):
                pool.dma_start(st_s[t * DB:(t + 1) * DB, :], conv_in[0, :, t, :]).then_inc(smp_in, 16)
            pool.dma_start(st_s[(CONV_W - 1) * DB:CONV_W * DB, :], h_in[0]).then_inc(smp_in, 16)
            pool.wait_ge(smp_dve, SMP_DVE_L)
            pool.dma_start(nv_p[0, 0].rearrange("s g d -> s (g d)"), v_tok[:, QB, :]).then_inc(kv_out, 16)
            pool.dma_start(nk_p[0, 0].rearrange("s g d -> s (g d)"), k_out[:, :]).then_inc(kv_out, 16)
            for t in range(DT):
                r0 = t * DB
                pool.dma_start(nk_s[0, :, WINDOW - DT + t].rearrange("b g d -> b (g d)"),
                               ks_out[r0:r0 + DB, :]).then_inc(kv_out, 16)
                pool.dma_start(nv_s[0, :, WINDOW - DT + t].rearrange("b g d -> b (g d)"),
                               vs_tok[r0:r0 + DB, :]).then_inc(kv_out, 16)
            pool.wait_ge(smp_dve, SMP_DVE_OUT)
            r0 = 0
            for t in range(CONV_W - 1):
                pool.dma_start(nc_s[0, :, t], outr[r0:r0 + DB, :]).then_inc(state_out, 16)
                r0 += DB
            pool.dma_start(nh_s[0], outr[r0:r0 + DB, :]).then_inc(state_out, 16)
            r0 += DB
            pool.dma_start(nc_p[0, 0], outr[r0:r0 + CONV_W - 1, :]).then_inc(state_out, 16)
            r0 += CONV_W - 1
            pool.dma_start(nh_p[0], outr[r0:r0 + 1, :]).then_inc(state_out, 16)
            pool.wait_ge(smp_dve, SMP_DVE_Y)
            for t in range(DT):
                pool.dma_start(y_s[:, t, :], y_tok[t * DB:(t + 1) * DB, 0, :]).then_inc(ys_out, 16)
            for done_, n in ((cache_out, 2), (kv_out, N_KV_OUT), (state_out, N_STATE_OUT), (ys_out, DT)):
                pool.wait_ge(done_, 16 * n)
            for o in y_out:
                o.wait(pool, b, QB // 2)

        @block.tensor
        def _(pe):
            for s in (gemm_done, xT_done, statx_done, stath_done, staty_done, vT_done, sc_done, pT_done,
                      av_done, attnT_done,
                      gates_done, yT_done):
                s.prime(pe)
            smp = [0]

            def smp_by(ins):
                smp[0] += 1
                ins.then_inc(smp_pe, 1)

            def gemm(b, wide, u, hi, lo, tile_ready=None, kts=None, only=None):
                whole = list(range(kt_of[u]))
                kts = kts or whole
                first = kts[0] == (KT - LC if kts != whole else 0)
                final = kts[-1] == kt_of[u] - 1
                w_ready.wait(pe, b, u + 1)
                base = 0 if u < UH else UH
                for c, (c0, c1) in enumerate(chunks(wide)):
                    if only is not None and c != only:
                        continue
                    j = job(u, c, wide)
                    if not first:
                        pass
                    elif not wide:
                        freed.wait(pe, b, u - 2)
                    elif j < 3:
                        freed.wait(pe, b, base + j - 2)
                    elif j % 2:
                        pe.wait_ge(freed_half, base + (j - 3) // 2 + 1)
                    else:
                        freed.wait(pe, b, base + (j - 3) // 2 + 1)
                    out = G[j % 3][:, 0:c1 - c0]
                    for kt in kts:
                        if tile_ready and (c == 0 or only == c):
                            tile_ready(kt)
                        h = w_hi[:, u % RING, kt * P:(kt + 1) * P]
                        l = w_lo[:, u % RING, kt * P:(kt + 1) * P]
                        nc.tensor.matmul(out, h, hi[:, kt, c0:c1], start=(first and kt == kts[0]), stop=False)
                        nc.tensor.matmul(out, h, lo[:, kt, c0:c1], start=False, stop=False)
                        mm = nc.tensor.matmul(out, l, hi[:, kt, c0:c1], start=False, stop=(kt == kt_of[u] - 1))
                    if wide and c == 0 and final:
                        mm.then_inc(gemm_half, 1)
                if final and only in (None, len(chunks(wide)) - 1):
                    gemm_done.by(mm)

            def feature_sums(wide):
                for c, (c0, c1) in enumerate(chunks(wide)):
                    mm = nc.tensor.matmul((V, TB[0])[c][:, 0:c1 - c0], ones[:, :], ssum[:, c0:c1],
                                          start=True, stop=True)
                return mm

            xbank = [S[0], S[1], TB[0], TB[1]]

            def x_T(n, kt):
                if kt == 0:
                    x_in.wait(pe, n, QB)
                if kt >= 4:
                    xhi_ready.wait(pe, n, kt - 3)
                for m in range(QB):
                    mm = nc.tensor.transpose(xbank[kt % 4][:, m * P:(m + 1) * P],
                                             x_tok[:, m, kt * P:(kt + 1) * P], ident[:, :])
                xT_done.by(mm)

            def values_T(n):
                z_ready.wait(pe, n, U_V + 1)
                for m in range(QB):
                    mm = nc.tensor.transpose(TB[0][:, m * P:(m + 1) * P], vT[:, m * P:(m + 1) * P], ident[:, :])
                vT_done.by(mm)

            def y_stat(b, wide):
                sqy_added.wait(pe, b, KT)
                for m in range(QB):
                    mm = nc.tensor.matmul(V[:, m:m + 1], ssum_y[:, m * P:(m + 1) * P], ones[:, 0:1],
                                          start=True, stop=True)
                if wide:
                    mm = nc.tensor.matmul(V[0:NS, QB:QB + 1], ssum_y[:, T:W], ones[:, 0:1], start=True, stop=True)
                staty_done.by(mm)

            def y_T(b, m):
                if m >= 2:
                    y_ready.wait(pe, b, m - 1)
                o = (S, TB)[m % 2]
                for kt in range(KT):
                    mm = nc.tensor.transpose(o[kt // 4][:, kt % 4 * P:(kt % 4 + 1) * P],
                                             hT[:, kt, m * P:(m + 1) * P], ident[:, :])
                yT_done.by(mm)

            def head(n, wide, b=None):
                ready = lambda kt: xlo_ready.wait(pe, n, kt + 1)
                gemm(n, wide, U_K, x_hi, x_lo, ready, None, 0)
                sqx_added.wait(pe, n, KT)
                statx_done.by(feature_sums(wide))
                if wide:
                    gemm(n, wide, U_K, x_hi, x_lo, None, None, 1)
                gemm(n, wide, U_V, x_hi, x_lo)
                if b is not None:
                    stdx_ready.wait(pe, n, 1)
                    y_stat(b, False)
                for j, u in enumerate(U_Q):
                    if b is not None:
                        y_T(b, j)
                    gemm(n, wide, u, x_hi, x_lo)
                stdx_ready.wait(pe, n, 1)
                if b is not None:
                    y_ready.wait(pe, b, QB)
                values_T(n)

            def mixers(b, last):
                def scores(s):
                    qb, jp = s // 2, s % 2
                    if s == 0:
                        z_ready.wait(pe, b, UH)
                        y_ready.wait(pe, b, 0)
                    elif s % 2 == 0:
                        gates_read.wait(pe, b, s // 2)
                    else:
                        sc_read.wait(pe, b, s)
                    if last and s == 5:
                        pe.wait_ge(smp_dve, SMP_DVE_S)
                    if last and s == 7:
                        pe.wait_ge(smp_act, 2)
                    for g in range(NKV):
                        r = slice(g * HEAD, (g + 1) * HEAD)
                        for jj in range(2):
                            mm = nc.tensor.matmul(S[g][:, jj * 256:(jj + 1) * 256],
                                                  qT[r, 2 * jp + jj, qb * P:(qb + 1) * P],
                                                  kT[r, qb * P:qb * P + 2 * WINDOW], start=True, stop=True)
                    sc_done.by(mm)

                def probs_T(s):
                    p_ready.wait(pe, b, s + 1)
                    if s == 0:
                        v_ready.wait(pe, b, 1)
                    else:
                        pTa_ready.wait(pe, b, s)
                        pTb_ready.wait(pe, b, s)
                    if last and s in (1, 5, 6):
                        pe.wait_ge(smp_dve, {1: SMP_DVE_L, 5: SMP_DVE_PT, 6: SMP_DVE_AT}[s])
                    for n in range(2 * HH):
                        mm = nc.tensor.transpose(TB[n // 4][:, n % 4 * P:(n % 4 + 1) * P],
                                                 s_p[:, s % 2, n // 2, n % 2 * P:(n % 2 + 1) * P], ident[:, :])
                    pT_done.by(mm)

                def attend(s):
                    qb, jp = s // 2, s % 2
                    pTa_ready.wait(pe, b, s + 1)
                    pTb_ready.wait(pe, b, s + 1)
                    if last and s == 0:
                        pe.wait_ge(smp_dve, SMP_DVE_L)
                    if jp == 0 and qb > 0:
                        attn_moved.wait(pe, b, qb)
                    for hh in range(HH):
                        g, jj = hh // 2, hh % 2
                        head = g * JT + 2 * jp + jj
                        for half in range(2):
                            mm = nc.tensor.matmul(V[:, head * HEAD:(head + 1) * HEAD],
                                                  pT[:, s % 2, 2 * hh + half, :],
                                                  v_tok[:, qb + half, g * HEAD:(g + 1) * HEAD],
                                                  start=(half == 0), stop=(half == 1))
                    av_done.by(mm)

                def attn_T(qb):
                    atok_ready.wait(pe, b, qb + 1)
                    for c in range(4):
                        mm = nc.tensor.transpose(V[:, c * P:(c + 1) * P], a_tok[:, c * P:(c + 1) * P], ident[:, :])
                    attnT_done.by(mm)

                def gates(c):
                    xc_ready.wait(pe, b, c + 1)
                    sc_read.wait(pe, b, 2 * c + 2)
                    for n in range(2):
                        mm = nc.tensor.matmul(S[n][:, :], gates_w[:, n, c, :], xc[:, c % 2, :],
                                              start=True, stop=True)
                    gates_done.by(mm)

                for s in range(NUN):
                    if s >= 1:
                        probs_T(s - 1)
                    if s >= 2:
                        attend(s - 2)
                    scores(s)
                    gemm(b, last, UH + s, x_hi, x_lo)
                    if last:
                        for step in sample_at.get(s, ()):
                            step(b, s)
                    if s % 2 == 1:
                        gates(s // 2)
                    if s >= 3 and s % 2 == 1:
                        attn_T((s - 3) // 2)

                def mix_ready(kt):
                    if kt >= KT - LC:
                        lmix_ready.wait(pe, b, kt - (KT - LC) + 1)
                    else:
                        amix_ready.wait(pe, b, QB)

                def part(m, kts, c=0):
                    gemm(b, last, U_O[m], a_hi, a_lo, mix_ready, kts, c)

                early, late, end_ = list(range(KT - LC, KT - 2)), [KT - 2] + list(range(KT - LC)), [KT - 1]
                probs_T(NUN - 1)
                attend(NUN - 2)
                part(0, early)
                attend(NUN - 1)
                part(1, early)
                attn_T(QB - 1)
                ahead = 2 if last else 3
                for m in range(2, ahead):
                    part(m, early)
                part(0, late)
                part(1, late)
                part(0, end_)
                for m in range(2, ahead):
                    part(m, late)
                for m in range(1, ahead):
                    part(m, end_)
                if last:
                    pe.wait_ge(smp_dve, SMP_DVE_OUTC)
                    for c in range(LC):
                        mm = nc.tensor.transpose(TB[1][0:SCOLS, c * P:(c + 1) * P], outc[:, c, :], ident[:, :])
                    smp_by(mm)
                    pe.wait_ge(smp_dve, SMP_DVE_MIX)
                    for m in range(ahead):
                        part(m, None, 1)
                rest = ahead
                for u in U_O[rest:]:
                    gemm(b, last, u, a_hi, a_lo)


            def sample_load(b, s):
                pe.wait_ge(smp_in, 16 * 7)
                pTa_ready.wait(pe, b, s)
                pTb_ready.wait(pe, b, s)
                for bb in range(DB):
                    nc.tensor.transpose(TB[bb // 4][:, bb % 4 * P:(bb % 4 + 1) * P], kc_tok[:, bb, :], ident[:, :])
                nc.tensor.transpose(V[0:NS, 0:P], vT_s[:, :], ident[:, :])
                nc.tensor.transpose(V[0:NS, P:2 * P], kT[:, WINDOW + T:WINDOW + W], ident[:, :])
                nc.tensor.transpose(V[:, 2 * P:3 * P], kT[:, T:T + WINDOW], ident[:, :])
                R = CONV_W * DB
                for c in range(LC):
                    mm = nc.tensor.transpose(V[:, 3 * P + c * R:3 * P + (c + 1) * R], st_s[:, c * P:(c + 1) * P],
                                             ident[0:R, 0:R])
                smp_by(mm)

            def sample_scores(b, s):
                pe.wait_ge(smp_dve, SMP_DVE_Q)
                sc_read.wait(pe, b, s + 1)
                for g in range(NKV):
                    r = slice(g * HEAD, (g + 1) * HEAD)
                    for bb in range(DB):
                        nc.tensor.matmul(S[g][:, 0:WINDOW], q_d[r, bb, :], kc_T[r, bb, :],
                                         start=(bb == 0), stop=(bb == DB - 1))
                    mm = nc.tensor.matmul(S[g][:, WINDOW:SC], q_r[r, :], kT[r, WINDOW + T:WINDOW + W],
                                          start=False, stop=True, skip_group_check=True)
                smp_by(mm)

            def sample_probs(b, s):
                pe.wait_ge(smp_dve, SMP_DVE_P)
                pTa_ready.wait(pe, b, s)
                pTb_ready.wait(pe, b, s)
                for g in range(NKV):
                    nc.tensor.transpose(TB[0][:, g * P:(g + 1) * P], s_s[:, g, 0:WINDOW], ident[:, :])
                    mm = nc.tensor.transpose(TB[1][0:NS, g * P:(g + 1) * P], s_s[:, g, WINDOW:SC], ident[:, :])
                smp_by(mm)

            def sample_attend(b, s):
                pe.wait_ge(smp_dve, SMP_DVE_PT)
                pTa_ready.wait(pe, b, s)
                pTb_ready.wait(pe, b, s)
                for g in range(NKV):
                    d = slice(g * HEAD, (g + 1) * HEAD)
                    for bb in range(DB):
                        rr = slice(bb * DT * JT, (bb + 1) * DT * JT)
                        nc.tensor.matmul(TB[g][0:HEAD, rr], vc_tok[:, bb, d], pcT[:, g, rr],
                                         start=(bb == 0), stop=(bb == DB - 1), skip_group_check=True)
                    mm = nc.tensor.matmul(TB[g][0:HEAD, 0:P], vs_tok[:, d], pnT[:, g, :], start=False, stop=True,
                                          skip_group_check=True)
                smp_by(mm)

            def sample_gates(b, s):
                pe.wait_ge(smp_dve, SMP_DVE_XC)
                sc_read.wait(pe, b, s + 1)
                for n in range(2):
                    for c in range(LC):
                        mm = nc.tensor.matmul(S[n][:, c * NS:(c + 1) * NS], gates_w[:, n, c, :], xc_s[:, c, :],
                                              start=True, stop=True)
                smp_by(mm)

            sample_at = {1: (sample_load,), 4: (sample_scores,), 5: (sample_probs,), 6: (sample_attend, sample_gates)}

            def ffn(b, last):
                f0 = 0
                for ci, nf in enumerate(FCH):
                    for f, (ug, uu) in enumerate(U_IN[ci]):
                        first = ci == 0 and f == 0
                        gemm(b, last, ug, x_hi, x_lo,
                             (lambda kt: hlo_ready.wait(pe, b, kt + 1)) if first else None, None,
                             0 if first else None)
                        if first:
                            sqh_added.wait(pe, b, KT)
                            amix_ready.wait(pe, b, QB)
                            if last:
                                pe.wait_ge(smp_dve, SMP_DVE_OUT)
                            stath_done.by(feature_sums(last))
                            if last:
                                gemm(b, last, ug, x_hi, x_lo, None, None, 1)
                        gemm(b, last, uu, x_hi, x_lo)
                    for m, u in enumerate(U_OUT[ci]):
                        gemm(b, last, u, a_hi, a_lo,
                             (lambda kt, f0=f0: act_ready.wait(pe, b, f0 + kt + 1)) if m == 0 else None)
                        if ci == len(FCH) - 1 and not last:
                            x_T(b + 1, m)
                    f0 += nf

            pe.wait_ge(first_in, 16 * N_FIRST)
            pe.wait_ge(xs_in, 16 * DT)
            for kt in range(KT):
                mm = nc.tensor.transpose(V[:, kt * NS:(kt + 1) * NS], xs_tok[:, kt * P:(kt + 1) * P],
                                         ident[0:NS, 0:NS])
            smp_by(mm)
            for kt in range(KT):
                x_T(0, kt)
            pe.wait_ge(zeroed, 7)
            head(0, True)
            pe.wait_ge(const_in, 16 * N_CONST)
            freed.wait(pe, 0, UH)
            with pe.Fori(0, NB - 1) as b:
                mixers(b, False)
                ffn(b, False)
                head(b + 1, False, b)
            mixers(NB - 1, True)
            ffn(NB - 1, True)
            freed.wait(pe, NB - 1, NU)
            y_T(NB - 1, 0)
            y_T(NB - 1, 1)
            y_stat(NB - 1, True)
            y_T(NB - 1, 2)
            y_T(NB - 1, 3)
            y_ready.wait(pe, NB - 1, 3)
            for kt in range(KT):
                mm = nc.tensor.transpose(S[kt // 4][0:NS, kt % 4 * P:(kt % 4 + 1) * P], hT[:, kt, T:W], ident[:, :])
            smp_by(mm)

        @block.scalar
        def _(act):
            for s in (w_hi_ready, z_ready, sqx_ready, sqh_ready, sqy_ready, xhi_ready, hhi_ready, stdx_ready,
                      stdh_ready, stdy_ready, p_ready, pTa_ready, attn_moved, amix_hi,
                      gates_read, lru_exp, gelu_sq, gelu_th, lru_sqrt, lmix_hi, gate_tanh, act_hi, *y_out):
                s.prime(act)
            chain = Chain(act, act_chain)
            smp = [0]

            def smp_by(ins):
                smp[0] += 1
                ins.then_inc(smp_act, 1)

            A = nc.scalar.activation
            for dst, src in ((ident[:, :], ident_in), (vec[:, :], vecs)):
                act.dma_start(dst, src).then_inc(first_in, 16)
            for t in range(DT):
                act.dma_start(xs_tok[t * DB:(t + 1) * DB, :], x_s[:, t, :]).then_inc(xs_in, 16)
            def split(b, u, end=False):
                if end and u >= NU:
                    return
                raw_in[u % RAW].wait(act, b, u // RAW + 1)
                unit_done(act, b, u - RING)
                n = kt_of[u % NU] * P
                w_hi_ready.by(A(w_hi[:, u % RING, 0:n], w_raw[:, u % RAW, 0:n], ACT.Copy))

            def rms(wide, ready):
                for c, (c0, c1) in enumerate(chunks(wide)):
                    ins = A(rinv[:, c0:c1], (V, TB[0])[c][:, 0:c1 - c0], ACT.Sqrt, bias=eps_t[:, 0:1], scale=1.0 / DM)
                ready.by(ins)

            xbank = [S[0], S[1], TB[0], TB[1]]

            def x_tile(n, wide, kt):
                w = W if wide else T
                xT_done.wait(act, n, kt + 1)
                chain.link(A(xT[:, kt, 0:T], xbank[kt % 4][:, :], ACT.Copy))
                sqx_added.wait(act, n, kt)
                sqx_ready.by(A(sq[:, 1, 0:w], xT[:, kt, 0:w], ACT.Square))
                xhi_ready.by(A(x_hi[:, kt, 0:w], xT[:, kt, 0:w], ACT.Copy, scale=v(VG1 + kt)))

            def h_tile(b, wide, m):
                w = W if wide else T
                freed.wait(act, b, U_O[m] + 1)
                sqh_added.wait(act, b, m)
                sqh_ready.by(A(sq[:, 0, 0:w], hT[:, m, 0:w], ACT.Square))
                hhi_ready.by(A(x_hi[:, m, 0:w], hT[:, m, 0:w], ACT.Copy, scale=v(VG2 + m)))

            def y_tile(b, wide, m):
                w = W if wide else T
                freed.wait(act, b, U_OUT[-1][m] + 1)
                sqy_added.wait(act, b, m)
                sqy_ready.by(A(sq[:, 0, 0:w], hT[:, m, 0:w], ACT.Square))

            def y_rms(b, wide):
                staty_done.wait(act, b, 1)
                if wide:
                    A(std_t[0:NS, QB:QB + 1], V[0:NS, QB:QB + 1], ACT.Sqrt, bias=eps_t[0:NS, 0:1], scale=1.0 / DM)
                stdy_ready.by(A(std_t[:, 0:QB], V[:, 0:QB], ACT.Sqrt, bias=eps_t[:, 0:1], scale=1.0 / DM))

            def y_store(b, m):
                y_ready.wait(act, b, m + 1)
                y_out[m % 2].by(act.dma_start(y_p[0, bass.ds(b * T + m * P, P), :], y_tok[:, m % 2, :]))

            def head(n, wide, b=None):
                w = W if wide else T
                if not wide:
                    split(n, U_K + RING)
                statx_done.wait(act, n, 1)
                rms(wide, stdx_ready)
                if wide:
                    split(n, U_K + RING)
                freed.wait(act, n, U_K + 1)
                kn = kT[:, WINDOW:WINDOW + w]
                z_ready.by(A(kn, kn, ACT.Identity, bias=v(VB + U_K)))
                split(n, U_V + RING)
                freed.wait(act, n, U_V + 1)
                if wide:
                    A(vT_s[:, :], vT[:, T:W], ACT.Identity, bias=v(VB + U_V))
                z_ready.by(A(vT[:, 0:T], vT[:, 0:T], ACT.Identity, bias=v(VB + U_V)))
                if b is not None:
                    y_rms(b, False)
                for j, u in enumerate(U_Q):
                    split(n, u + RING)
                    freed.wait(act, n, u + 1)
                    z_ready.by(A(qT[:, j, 0:w], qT[:, j, 0:w], ACT.Identity, bias=qb_t[:, j:j + 1],
                                 scale=v(VQS + j)))
                    if b is not None:
                        y_store(b, j)

            def mixers(b, last):
                for o in y_out:
                    o.wait(act, b, 0)

                def exps(s):
                    sc_read.wait(act, b, s + 1)
                    for hh in range(HH):
                        A(s_p[:, s % 2, hh, :], s_p[:, s % 2, hh, :], ACT.Exp, bias=nm[:, s % 2, hh:hh + 1],
                          accum_out=rs[:, s % 2, hh:hh + 1])
                    p_ready.by(A(es[:, s % 2, :], sd[:, s % 2, :], ACT.Exp))

                def probs_T(s):
                    pT_done.wait(act, b, s + 1)
                    av_done.wait(act, b, s - 1)
                    pTa_ready.by(A(pT[:, s % 2, 0:4, :], TB[0][:, :].rearrange("p (n q) -> p n q", n=4), ACT.Copy))

                def lru_gates(c):
                    gates_done.wait(act, b, c + 1)
                    lmix_f.wait(act, b, c)
                    chain.link(A(ra[:, :], S[0][:, :], ACT.Tanh, bias=lru_c[:, 0, c:c + 1], scale=0.5))
                    gates_read.by(A(ii[:, :], S[1][:, :], ACT.Tanh, bias=lru_c[:, 1, c:c + 1], scale=0.5))

                def lru_decay(c):
                    chain.link(A(qq[:, :], ra[:, :], ACT.Tanh, bias=lru_c[:, 3, c:c + 1], scale=lru_c[:, 3, c:c + 1]))
                    chain.link(A(ra[:, :], ra[:, :], ACT.Exp, bias=lru_c[:, 2, c:c + 1], scale=lru_c[:, 2, c:c + 1]))
                    lru_exp.by(A(om[:, :], ra[:, :], ACT.Square))

                def lru_root(c):
                    lru_m.wait(act, b, c + 1)
                    lru_sqrt.by(A(qq[:, :], qq[:, :], ACT.Sqrt, scale=0.25))

                def gelu_tanh(c):
                    gelu_in.wait(act, b, c + 1)
                    gelu_th.by(A(gl[:, c % 2, :], gl[:, c % 2, :], ACT.Tanh))

                def lru_hi(c):
                    lmix_f.wait(act, b, c + 1)
                    lmix_hi.by(A(a_hi[:, KT - LC + c, 0:T], gl[:, c % 2, :], ACT.Copy, scale=0.5))

                def attn_hi(qb):
                    attnT_done.wait(act, b, qb + 1)
                    attn_moved.by(A(a_tok[:, :], V[:, :], ACT.Copy))
                    attn_moved.wait(act, b, qb + 1)
                    amix_hi.by(A(a_hi[:, 0:4, qb * P:(qb + 1) * P],
                                 a_tok[:, :].rearrange("p (c q) -> p c q", c=4), ACT.Copy))

                for s in range(NUN):
                    if s >= 1:
                        probs_T(s - 1)
                    exps(s)
                    if s >= 2 and s % 2 == 0:
                        lru_root((s - 2) // 2)
                    kind, c = ORDER[s]
                    u = UH + s
                    freed.wait(act, b, u + 1)
                    if kind == "x":
                        xi = xb[:, c % 2, CONV_W - 1:CONV_W - 1 + (W if last else T)]
                        z_ready.by(A(xi, xi, ACT.Identity, bias=v(VB + u)))
                    else:
                        lmix_ready.wait(act, b, c - 1)
                        gelu_sq.by(A(gl[:, c % 2, :], yb[:, c % 2, 0:T], ACT.Square, bias=v(VB + u)))
                        if c < LC - 1:
                            gelu_tanh(c)
                    if s >= 3 and s % 2 == 1:
                        attn_hi((s - 3) // 2)
                    if s % 2 == 1:
                        lru_gates(s // 2)
                    if s == NUN - 1:
                        break
                    if s % 2 == 1:
                        lru_decay(s // 2)
                    split(b, u + RING)
                    if s >= 3 and s % 2 == 1:
                        lru_hi((s - 3) // 2)
                    if last and s == 4:
                        sample_exps()
                    if last and s == 6:
                        sample_gates()
                        sample_decay()
                probs_T(NUN - 1)
                split(b, U_O[0] - 1 + RING)
                lru_hi(LC - 2)
                lru_decay(LC - 1)
                gelu_tanh(LC - 1)
                attn_hi(QB - 1)
                if last:
                    act.wait_ge(smp_dve, SMP_DVE_GI)
                    chain.link(A(l_s[4][:, :, :], l_s[4][:, :, :], ACT.Tanh))
                lru_root(LC - 1)
                if last:
                    act.wait_ge(smp_dve, SMP_DVE_M)
                    smp_by(A(l_s[2][:, :, :], l_s[2][:, :, :], ACT.Sqrt, scale=0.25))
                lru_hi(LC - 1)
                if last:
                    sample_mix()
                for m, u in enumerate(U_O):
                    split(b, u + RING)
                    h_tile(b, last, m)

            def sample_exps():
                act.wait_ge(smp_dve, SMP_DVE_S)
                for g in range(NKV):
                    A(s_s[:, g, :], s_s[:, g, :], ACT.Exp, bias=mx_s[:, 1, g:g + 1], accum_out=mx_s[:, 2, g:g + 1])
                smp_by(A(mx_s[:, 3, :], mx_s[:, 4, :], ACT.Exp))

            def sample_gates():
                act.wait_ge(smp_pe, 6)
                for n in range(2):
                    for c in range(LC):
                        ins = A(l_s[n][:, c, :], S[n][:, c * NS:(c + 1) * NS], ACT.Tanh,
                                bias=lru_c[:, n, c:c + 1], scale=0.5)
                smp_by(ins)

            def sample_decay():
                act.wait_ge(smp_act, 2)
                for c in range(LC):
                    A(l_s[3][:, c, :], l_s[0][:, c, :], ACT.Exp, bias=lru_c[:, 2, c:c + 1], scale=lru_c[:, 2, c:c + 1])
                    ins = A(l_s[2][:, c, :], l_s[0][:, c, :], ACT.Tanh, bias=lru_c[:, 3, c:c + 1],
                            scale=lru_c[:, 3, c:c + 1])
                smp_by(ins)

            def sample_mix():
                act.wait_ge(smp_dve, SMP_DVE_MIXF)
                smp_by(A(a_hi[:, :, T:W], mixs[:, :, :], ACT.Copy))

            def ffn(b, last):
                w = W if last else T
                f0 = 0
                for ci, nf in enumerate(FCH):
                    for f, (ug, uu) in enumerate(U_IN[ci]):
                        n = f0 + f
                        if n == 0 and last:
                            stath_done.wait(act, b, 1)
                            rms(last, stdh_ready)
                        split(b, ug + RING)
                        if n == 0 and not last:
                            stath_done.wait(act, b, 1)
                            rms(last, stdh_ready)
                        freed.wait(act, b, ug + 1)
                        gate_tanh.by(A(th[:, 0:w], gt[:, 0:w], ACT.Tanh, scale=0.5))
                        split(b, uu + RING, last)
                        act_f.wait(act, b, n + 1)
                        act_hi.by(A(a_hi[:, f, 0:w], a32[:, n % 2, 0:w], ACT.Copy))
                    for m, u in enumerate(U_OUT[ci]):
                        split(b, u + RING, last)
                        if ci == len(FCH) - 1:
                            if not last:
                                x_tile(b + 1, False, m)
                            y_tile(b, last, m)
                    f0 += nf

            split(0, 0)
            act.wait_ge(smp_pe, 1)
            act.wait_ge(first_in, 16 * N_FIRST)
            chain.link(A(xT[:, :, T:W], V[:, 0:KT * NS].rearrange("p (k n) -> p k n", k=KT), ACT.Copy))
            for kt in range(KT):
                x_tile(0, True, kt)
            for u in range(1, RING):
                split(0, u)
            act.wait_ge(zeroed, 7)
            act.wait_ge(setup_done, 1)
            head(0, True)
            act.wait_ge(setup_done, 2)
            A(set_t[:, 1, :], set_t[:, 0, :], ACT.Exp, scale=-1.0).then_inc(setup_act, 1)
            act.wait_ge(setup_done, 3)
            chain.restart()
            with act.Fori(0, NB - 1) as b:
                mixers(b, False)
                ffn(b, False)
                head(b + 1, False, b)
                chain.restart()
            b = NB - 1
            mixers(b, True)
            ffn(b, True)
            y_rms(b, True)
            for m in range(QB):
                y_store(b, m)

        @block.vector
        def _(dve):
            for s in (w_ready, freed, sqx_added, sqh_added, sqy_added, xlo_ready, hlo_ready, v_ready,
                      sc_read, pTb_ready,
                      atok_ready, amix_ready, xc_ready, lru_m, gelu_in, lmix_f, lmix_ready, act_f, act_ready,
                      y_ready):
                s.prime(dve)
            chain = Chain(dve, dve_chain)
            link = chain.link
            TT = nc.vector.tensor_tensor
            TS = nc.vector.tensor_scalar
            STT = nc.vector.scalar_tensor_tensor
            def split(b, u, end=False):
                if end and u >= NU:
                    return
                w_hi_ready.wait(dve, b, u + 1)
                n = kt_of[u % NU] * P
                w_ready.by(TT(w_lo[:, u % RING, 0:n], w_raw[:, u % RAW, 0:n], w_hi[:, u % RING, 0:n], ALU.subtract))

            def evacuate(b, wide, u, op):
                for c, (c0, c1) in enumerate(chunks(wide)):
                    done(dve, b, u, c, wide)
                    ins = op(G[job(u, c, wide) % 3][:, 0:c1 - c0], c0, c1)
                    if c < len(chunks(wide)) - 1:
                        ins.then_inc(freed_half, 1)
                freed.by(ins)

            def scaled(dst):
                return lambda src, c0, c1: TT(dst(c0, c1), src, rinv[:, c0:c1], ALU.mult)

            def add_square(b, wide, kt, total, src, ready, added):
                w = W if wide else T
                ready.wait(dve, b, kt + 1)
                if kt == 0:
                    ins = nc.vector.tensor_copy(total[:, 0:w], src[:, 0:w])
                else:
                    added.wait(dve, b, kt)
                    ins = TT(total[:, 0:w], total[:, 0:w], src[:, 0:w], ALU.add)
                added.by(ins)

            def x_tile(n, wide, kt):
                w = W if wide else T
                add_square(n, wide, kt, ssum, sq[:, 1], sqx_ready, sqx_added)
                xhi_ready.wait(dve, n, kt + 1)
                xlo_ready.by(STT(out=x_lo[:, kt, 0:w], in0=xT[:, kt, 0:w], scalar=v(VG1 + kt),
                                 in1=x_hi[:, kt, 0:w], op0=ALU.mult, op1=ALU.subtract))

            def h_tile(b, wide, m):
                w = W if wide else T
                add_square(b, wide, m, ssum, sq[:, 0], sqh_ready, sqh_added)
                hhi_ready.wait(dve, b, m + 1)
                hlo_ready.by(STT(out=x_lo[:, m, 0:w], in0=hT[:, m, 0:w], scalar=v(VG2 + m),
                                 in1=x_hi[:, m, 0:w], op0=ALU.mult, op1=ALU.subtract))

            def y_tile(b, wide, m):
                add_square(b, wide, m, ssum_y, sq[:, 0], sqy_ready, sqy_added)

            def invert(b, wide, ready):
                w = W if wide else T
                ready.wait(dve, b, 1)
                link(nc.vector.reciprocal(rinv[:, 0:w], rinv[:, 0:w]))

            def y_scale(b, m):
                yT_done.wait(dve, b, m + 1)
                y_out[m % 2].wait(dve, b, m // 2)
                o = (S, TB)[m % 2]
                for h in range(2):
                    ins = STT(out=y_tok[:, m % 2, h * 512:(h + 1) * 512], in0=o[h][:, :],
                              scalar=rstd_t[:, m:m + 1], in1=gfin[:, h * 512:(h + 1) * 512],
                              op0=ALU.mult, op1=ALU.mult)
                y_ready.by(ins)

            def y_rstd(b, wide):
                stdy_ready.wait(dve, b, 1)
                if wide:
                    nc.vector.reciprocal(rstd_t[0:NS, QB:QB + 1], std_t[0:NS, QB:QB + 1])
                link(nc.vector.reciprocal(rstd_t[:, 0:QB], std_t[:, 0:QB]))

            def head(n, wide, b=None):
                link(nc.vector.tensor_copy(kT[:, 0:WINDOW], kT[:, T:T + WINDOW]))
                link(nc.vector.tensor_copy(v_tok[:, 0, :], v_tok[:, QB, :]))
                if not wide:
                    split(n, U_K + RING)
                invert(n, wide, stdx_ready)
                evacuate(n, wide, U_K, scaled(lambda c0, c1: kT[:, WINDOW + c0:WINDOW + c1]))
                if wide:
                    split(n, U_K + RING)
                evacuate(n, wide, U_V, scaled(lambda c0, c1: vT[:, c0:c1]))
                split(n, U_V + RING)
                if b is not None:
                    y_rstd(b, False)
                for j, u in enumerate(U_Q):
                    if b is not None:
                        y_scale(b, j)
                    evacuate(n, wide, u, scaled(lambda c0, c1: qT[:, j, c0:c1]))
                    split(n, u + RING)
                vT_done.wait(dve, n, 1)
                v_ready.by(nc.vector.tensor_copy(v_tok[:, 1:1 + QB, :],
                                                 TB[0][:, :].rearrange("p (m q) -> p m q", m=QB)))

            def mixers(b, last):
                def softmax_1(s):
                    qb, jp = s // 2, s % 2
                    sc_done.wait(dve, b, s + 1)
                    pT_done.wait(dve, b, s - 1)
                    link(nc.vector.memset(mx[:, s % 2, :], 0.0))
                    for hh in range(HH):
                        g, jj = hh // 2, hh % 2
                        head = g * JT + 2 * jp + jj
                        d = dist_b if qb == 0 else dist
                        ins = nc.vector.tensor_tensor_reduce(
                            s_p[:, s % 2, hh, :], S[g][:, jj * 256:(jj + 1) * 256], d[:, :], 2.0 ** -(head + 1),
                            sinks[:, head:head + 1], ALU.add, ALU.max, mx[:, s % 2, hh:hh + 1])
                    link(ins)
                    link(TS(nm[:, s % 2, :], mx[:, s % 2, :], -1.0, None, ALU.mult))
                    sk = sinks[:, :].rearrange("p (g j) -> p g j", g=NKV)[:, :, 2 * jp:2 * jp + 2]
                    sc_read.by(TT(sd[:, s % 2, :].rearrange("p (g j) -> p g j", g=NKV), sk,
                                  nm[:, s % 2, :].rearrange("p (g j) -> p g j", g=NKV), ALU.add))

                def softmax_2(s):
                    qb, jp = s // 2, s % 2
                    p_ready.wait(dve, b, s + 1)
                    link(TT(es[:, s % 2, :], es[:, s % 2, :], rs[:, s % 2, :], ALU.add))
                    ro = rec[:, qb % 2, :].rearrange("p (g j) -> p g j", g=NKV)[:, :, 2 * jp:2 * jp + 2]
                    link(nc.vector.reciprocal(ro, es[:, s % 2, :].rearrange("p (g j) -> p g j", g=NKV)))

                def probs_T(s):
                    pT_done.wait(dve, b, s + 1)
                    av_done.wait(dve, b, s - 1)
                    pTb_ready.by(nc.vector.tensor_copy(pT[:, s % 2, 4:8, :],
                                                       TB[1][:, :].rearrange("p (n q) -> p n q", n=4)))

                def attn_out(qb):
                    av_done.wait(dve, b, 2 * qb + 2)
                    amix_ready.wait(dve, b, qb)
                    bc = rec[:, qb % 2, :].rearrange("p (h o) -> p h o", o=1).to_broadcast([P, NH, HEAD])
                    atok_ready.by(TT(a_tok[:, :].rearrange("p (h d) -> p h d", h=NH),
                                     V[:, :].rearrange("p (h d) -> p h d", h=NH), bc, ALU.mult))

                def conv(c):
                    z_ready.wait(dve, b, UH + c + 1)
                    xi = xb[:, c % 2, :]
                    link(nc.vector.tensor_copy(xi[:, 0:CONV_W - 1], x_prev[:, c, :]))
                    nc.vector.tensor_copy(x_prev[:, c, :], xi[:, T:T + CONV_W - 1])
                    o = xc[:, c % 2, :]
                    lmix_f.wait(dve, b, c - 1)
                    link(TS(o, xi[:, 0:T], v(VCW + c), v(VCB + c), ALU.mult, ALU.add))
                    for k in range(1, CONV_W):
                        ins = STT(out=o, in0=xi[:, k:k + T], scalar=v(VCW + k * LC + c), in1=o,
                                  op0=ALU.mult, op1=ALU.add)
                        if k < CONV_W - 1:
                            link(ins)
                    if last:
                        link(ins)
                        ins = nc.vector.tensor_copy(xs_b[:, c, (CONV_W - 1) * DB:], xi[:, CONV_W - 1 + T:])
                    xc_ready.by(ins)

                def gelu_arg(c):
                    gelu_sq.wait(dve, b, c + 1)
                    g = gl[:, c % 2, :]
                    if last:
                        TS(ys_b[:, c, :], yb[:, c % 2, T:W], v(VB + U_Y[c]), None, ALU.add)
                    link(TS(g, g, GELU_K * GELU_C, GELU_K, ALU.mult, ALU.add))
                    gelu_in.by(STT(out=g, in0=yb[:, c % 2, 0:T], scalar=v(VB + U_Y[c]), in1=g,
                                   op0=ALU.add, op1=ALU.mult))

                def lru_square(c):
                    lru_exp.wait(dve, b, c + 1)
                    STT(out=ii[:, :], in0=ii[:, :], scalar=1.0, in1=xc[:, c % 2, :], op0=ALU.add, op1=ALU.mult)
                    lru_m.by(STT(out=qq[:, :], in0=om[:, :], scalar=1.0, in1=qq[:, :], op0=ALU.add, op1=ALU.mult))

                def lru_scan(c):
                    lru_sqrt.wait(dve, b, c + 1)
                    link(TT(ii[:, :], ii[:, :], qq[:, :], ALU.mult))
                    link(nc.vector.tensor_tensor_scan(om[:, :], ra[:, :], ii[:, :], h_prev[:, c:c + 1],
                                                      ALU.mult, ALU.add))
                    link(nc.vector.tensor_copy(h_prev[:, c:c + 1], om[:, T - 1:T]))

                def lru_mix(c):
                    g = gl[:, c % 2, :]
                    gelu_th.wait(dve, b, c + 1)
                    link(STT(out=g, in0=g, scalar=1.0, in1=om[:, :], op0=ALU.add, op1=ALU.mult))
                    lmix_f.by(STT(out=g, in0=yb[:, c % 2, 0:T], scalar=v(VB + U_Y[c]), in1=g,
                                  op0=ALU.add, op1=ALU.mult))

                def lru_lo(c):
                    lmix_hi.wait(dve, b, c + 1)
                    lmix_ready.by(STT(out=a_lo[:, KT - LC + c, 0:T], in0=gl[:, c % 2, :], scalar=0.5,
                                      in1=a_hi[:, KT - LC + c, 0:T], op0=ALU.mult, op1=ALU.subtract))

                def attn_lo(qb):
                    amix_hi.wait(dve, b, qb + 1)
                    amix_ready.by(TT(a_lo[:, 0:4, qb * P:(qb + 1) * P],
                                     a_tok[:, :].rearrange("p (c q) -> p c q", c=4),
                                     a_hi[:, 0:4, qb * P:(qb + 1) * P], ALU.subtract))

                for s in range(NUN):
                    if s >= 1:
                        probs_T(s - 1)
                    softmax_1(s)
                    if s >= 2 and s % 2 == 0:
                        lru_square((s - 2) // 2)
                    if s >= 4 and s % 2 == 0:
                        lru_lo((s - 4) // 2)
                    if s >= 1:
                        softmax_2(s - 1)
                    if last and s == 5:
                        sample_norm()
                    if last and s == 6:
                        sample_conv()
                    if last and s == 7:
                        sample_square()
                    if s >= 3 and s % 2 == 1:
                        attn_out((s - 3) // 2)
                    if s >= 1:
                        split(b, UH + s - 1 + RING)
                    if s >= 3 and s % 2 == 1:
                        lru_mix((s - 3) // 2)
                    kind, c = ORDER[s]
                    if kind == "x":
                        evacuate(b, last, UH + s, scaled(
                            lambda c0, c1: xb[:, c % 2, CONV_W - 1 + c0:CONV_W - 1 + c1]))
                    else:
                        evacuate(b, last, UH + s, scaled(lambda c0, c1: yb[:, c % 2, c0:c1]))
                    if last and s in sample_at:
                        sample_at[s]()
                    if s >= 3 and s % 2 == 1:
                        attn_lo((s - 3) // 2)
                    if kind == "x":
                        conv(c)
                    if s == NUN - 1:
                        probs_T(s)
                    if s >= 2 and s % 2 == 0:
                        lru_scan((s - 2) // 2)
                    if kind == "y":
                        gelu_arg(c)
                    if last and s in sample_after:
                        sample_after[s]()
                softmax_2(NUN - 1)
                lru_lo(LC - 2)
                split(b, UH + NUN - 1 + RING)
                attn_out(QB - 1)
                lru_square(LC - 1)
                attn_lo(QB - 1)
                lru_scan(LC - 1)
                lru_mix(LC - 1)
                lru_lo(LC - 1)
                if last:
                    sample_lru()
                else:
                    link(nc.vector.tensor_copy(dist_b[:, :], dist[:, :]))
                for m, u in enumerate(U_O):
                    evacuate(b, last, u, lambda src, c0, c1: STT(
                        out=hT[:, m, c0:c1], in0=src, scalar=v(VBO + m), in1=xT[:, m, c0:c1],
                        op0=ALU.add, op1=ALU.add))
                    split(b, u + RING)
                    h_tile(b, last, m)

            smp = [0]

            def by(ins, want=None):
                smp[0] += 1
                ins.then_inc(smp_dve, 1)
                dve.wait_ge(smp_dve, smp[0])
                assert want is None or want == smp[0], (want, smp[0])

            D3 = (CONV_W - 1) * DB

            def sample_load():
                dve.wait_ge(smp_pe, 2)
                sv = V[:, 3 * P:4 * P].rearrange("p (c r) -> p c r", c=LC)
                nc.vector.tensor_copy(xs_b[:, :, 0:D3], sv[:, :, 0:D3])
                nc.vector.tensor_copy(hs0[:, :, :], sv[:, :, D3:D3 + DB])
                nc.vector.tensor_copy(vs_tok[:, :], V[0:NS, 0:P])
                nc.vector.tensor_copy(ks_out[:, :], V[0:NS, P:2 * P])
                nc.vector.tensor_copy(k_out[:, :], V[:, 2 * P:3 * P])
                nc.vector.tensor_copy(kc_T[:, 0:4, :], TB[0][:, :].rearrange("p (n q) -> p n q", n=4))
                by(nc.vector.tensor_copy(kc_T[:, 4:8, :], TB[1][:, :].rearrange("p (n q) -> p n q", n=4)), SMP_DVE_L)

            def sample_q():
                link(nc.vector.memset(q_d[:, :, :], 0.0))
                R = DT * JT
                for bb in range(DB):
                    src = qT[:, :, T + bb:W:DB]
                    nc.vector.tensor_copy(q_r[:, bb * R:(bb + 1) * R].rearrange("p (j t) -> p j t", j=JT), src)
                    ins = nc.vector.tensor_copy(q_d[:, bb, bb * R:(bb + 1) * R].rearrange("p (j t) -> p j t", j=JT),
                                                src)
                by(ins, SMP_DVE_Q)

            def sample_max():
                dve.wait_ge(smp_pe, 3)
                dve.wait_ge(smp_in, 16 * 7)
                for g in range(NKV):
                    ins = nc.vector.tensor_tensor_reduce(s_s[:, g, :], S[g][:, 0:SC], dist_s[:, :], rows[:, g:g + 1],
                                                         sink_s[:, g:g + 1], ALU.add, ALU.max, mx_s[:, 0, g:g + 1])
                link(ins)
                link(TS(mx_s[:, 1, :], mx_s[:, 0, :], -1.0, None, ALU.mult))
                by(TT(mx_s[:, 4, :], sink_s[:, :], mx_s[:, 1, :], ALU.add), SMP_DVE_S)

            def sample_norm():
                dve.wait_ge(smp_act, 1)
                link(TT(mx_s[:, 3, :], mx_s[:, 3, :], mx_s[:, 2, :], ALU.add))
                link(nc.vector.reciprocal(mx_s[:, 5, :], mx_s[:, 3, :]))
                for g in range(NKV):
                    ins = TS(s_s[:, g, :], s_s[:, g, :], mx_s[:, 5, g:g + 1], None, ALU.mult)
                by(ins, SMP_DVE_P)

            def sample_probs():
                dve.wait_ge(smp_pe, 4)
                nc.vector.tensor_copy(pcT[:, :, :], TB[0][:, 0:2 * P].rearrange("p (g q) -> p g q", g=NKV))
                by(nc.vector.tensor_copy(pnT[:, :, :], TB[1][0:NS, 0:2 * P].rearrange("p (g q) -> p g q", g=NKV)),
                   SMP_DVE_PT)

            def sample_attend():
                dve.wait_ge(smp_pe, 5)
                for g in range(NKV):
                    for j in range(JT):
                        src = TB[g][0:HEAD, 0:P].rearrange("p (b j t) -> p j t b", b=DB, j=JT)[:, j]
                        lo = j % 2 * HEAD
                        head_ = g * JT + j
                        dst = mixs[lo:lo + HEAD, head_ // 2, :].rearrange("p (t b) -> p t b", t=DT)
                        ins = nc.vector.tensor_copy(dst, src)
                by(ins, SMP_DVE_AT)

            def sample_conv():
                xc_ready.wait(dve, NB - 1, LC)
                for c in range(LC):
                    ins = TS(xc_s[:, c, :], xs_b[:, c, 0:NS], v(VCW + c), v(VCB + c), ALU.mult, ALU.add)
                link(ins)
                for k in range(1, CONV_W):
                    for c in range(LC):
                        ins = STT(out=xc_s[:, c, :], in0=xs_b[:, c, k * DB:k * DB + NS], scalar=v(VCW + k * LC + c),
                                  in1=xc_s[:, c, :], op0=ALU.mult, op1=ALU.add)
                    if k < CONV_W - 1:
                        link(ins)
                by(ins, SMP_DVE_XC)

            t_s, i_s, m_s, g_s, h_s = l_s[3], l_s[1], l_s[2], l_s[4], l_s[5]

            def sample_square():
                dve.wait_ge(smp_act, 3)
                link(TT(l_s[0][:, :, :], t_s[:, :, :], t_s[:, :, :], ALU.mult))
                STT(out=i_s[:, :, :], in0=i_s[:, :, :], scalar=1.0, in1=xc_s[:, :, :], op0=ALU.add, op1=ALU.mult)
                by(STT(out=m_s[:, :, :], in0=l_s[0][:, :, :], scalar=1.0, in1=m_s[:, :, :], op0=ALU.add,
                       op1=ALU.mult), SMP_DVE_M)

            def sample_gelu():
                link(TT(g_s[:, :, :], ys_b[:, :, :], ys_b[:, :, :], ALU.mult))
                link(TS(g_s[:, :, :], g_s[:, :, :], GELU_K * GELU_C, GELU_K, ALU.mult, ALU.add))
                by(TT(g_s[:, :, :], g_s[:, :, :], ys_b[:, :, :], ALU.mult), SMP_DVE_GI)

            def sample_lru():
                nc.vector.tensor_copy(outc[:, :, 0:(DT - 1) * DB], xs_b[:, :, D3 + DB:D3 + NS])
                nc.vector.tensor_copy(outc[:, :, DT * DB:DT * DB + CONV_W - 1], x_prev[:, :, :])
                nc.vector.tensor_copy(outc[:, :, SCOLS - 1], h_prev[:, :])
                dve.wait_ge(smp_act, 4)
                link(TT(i_s[:, :, :], i_s[:, :, :], m_s[:, :, :], ALU.mult))
                for k in range(DT):
                    prev = hs0[:, :, :] if k == 0 else h_s[:, :, (k - 1) * DB:k * DB]
                    cur = slice(k * DB, (k + 1) * DB)
                    link(TT(h_s[:, :, cur], t_s[:, :, cur], prev, ALU.mult))
                    link(TT(h_s[:, :, cur], h_s[:, :, cur], i_s[:, :, cur], ALU.add))
                by(nc.vector.tensor_copy(outc[:, :, (DT - 1) * DB:DT * DB], h_s[:, :, NS - DB:NS]), SMP_DVE_OUTC)
                link(STT(out=g_s[:, :, :], in0=g_s[:, :, :], scalar=1.0, in1=ys_b[:, :, :], op0=ALU.add,
                         op1=ALU.mult))
                by(STT(out=mixs[:, KT - LC:KT, :], in0=g_s[:, :, :], scalar=0.5, in1=h_s[:, :, :],
                       op0=ALU.mult, op1=ALU.mult), SMP_DVE_MIXF)
                dve.wait_ge(smp_act, 5)
                by(TT(a_lo[:, :, T:W], mixs[:, :, :], a_hi[:, :, T:W], ALU.subtract), SMP_DVE_MIX)
                dve.wait_ge(smp_pe, 7)
                by(nc.vector.tensor_copy(outr[:, :], TB[1][0:SCOLS, :]), SMP_DVE_OUT)
                dve.wait_ge(kv_out, 16 * N_KV_OUT)

            sample_at = {1: sample_load, 4: sample_max, 5: sample_probs, 6: sample_attend}
            sample_after = {2: sample_q, 7: sample_gelu}

            def ffn(b, last):
                w = W if last else T
                f0 = 0
                for ci, nf in enumerate(FCH):
                    for f, (ug, uu) in enumerate(U_IN[ci]):
                        n = f0 + f
                        early = n == 0 and not last
                        if early:
                            split(b, ug + RING)
                        if n == 0:
                            invert(b, last, stdh_ready)
                        evacuate(b, last, ug, scaled(lambda c0, c1: gt[:, c0:c1]))
                        if not early:
                            split(b, ug + RING)
                        gate_tanh.wait(dve, b, n + 1)
                        link(STT(out=gt[:, 0:w], in0=th[:, 0:w], scalar=1.0, in1=gt[:, 0:w],
                                 op0=ALU.add, op1=ALU.mult))
                        evacuate(b, last, uu, scaled(lambda c0, c1: a32[:, n % 2, c0:c1]))
                        freed.wait(dve, b, uu + 1)
                        act_f.by(STT(out=a32[:, n % 2, 0:w], in0=gt[:, 0:w], scalar=0.5, in1=a32[:, n % 2, 0:w],
                                     op0=ALU.mult, op1=ALU.mult))
                        split(b, uu + RING, last)
                        act_hi.wait(dve, b, n + 1)
                        act_ready.by(TT(a_lo[:, f, 0:w], a32[:, n % 2, 0:w], a_hi[:, f, 0:w], ALU.subtract))
                    for m, u in enumerate(U_OUT[ci]):
                        evacuate(b, last, u, lambda src, c0, c1: TT(hT[:, m, c0:c1], src, hT[:, m, c0:c1], ALU.add))
                        split(b, u + RING, last)
                        if ci == len(FCH) - 1:
                            if not last:
                                x_tile(b + 1, False, m)
                            y_tile(b, last, m)
                    f0 += nf

            split(0, 0)
            dve.wait_ge(first_in, 16 * N_FIRST)
            for kt in range(KT):
                x_tile(0, True, kt)
            for u in range(1, RING):
                split(0, u)

            TT(qb_t[:, :], vec[:, VB + U_Q[0]:VB + UH], vec[:, VQS:VQS + JT], ALU.mult).then_inc(setup_done, 1)
            dve.wait_ge(zeroed, 7)
            head(0, True)

            lam = vec[:, VLAM:VLAM + LC]
            link(TS(set_t[:, 5, :], lam, -1.0, None, ALU.mult))
            TT(set_t[:, 0, :], set_t[:, 5, :], lam, ALU.max).then_inc(setup_done, 1)
            dve.wait_ge(setup_act, 1)
            e = set_t[:, 1, :]
            link(TS(set_t[:, 2, :], e, 2.0, None, ALU.add))
            link(nc.vector.reciprocal(set_t[:, 2, :], set_t[:, 2, :]))
            link(TT(set_t[:, 2, :], set_t[:, 2, :], e, ALU.mult))
            link(TT(set_t[:, 3, :], set_t[:, 2, :], set_t[:, 2, :], ALU.mult))
            link(TS(set_t[:, 4, :], set_t[:, 3, :], 1.0 / 19, None, ALU.mult))
            for k in (17, 15, 13, 11, 9, 7, 5, 3):
                link(STT(out=set_t[:, 4, :], in0=set_t[:, 4, :], scalar=1.0 / k, in1=set_t[:, 3, :],
                         op0=ALU.add, op1=ALU.mult))
            link(STT(out=set_t[:, 4, :], in0=set_t[:, 4, :], scalar=1.0, in1=set_t[:, 2, :],
                     op0=ALU.add, op1=ALU.mult))
            link(TS(set_t[:, 4, :], set_t[:, 4, :], 8.0, None, ALU.mult))
            link(TS(set_t[:, 5, :], set_t[:, 5, :], 0.0, 4.0, ALU.max, ALU.mult))
            link(TT(lru_c[:, 3, :], set_t[:, 4, :], set_t[:, 5, :], ALU.add))
            TS(lru_c[:, 2, :], lru_c[:, 3, :], -1.0, None, ALU.mult)
            TS(lru_c[:, 0, :], vec[:, VBA:VBA + LC], 0.5, None, ALU.mult)
            TS(lru_c[:, 1, :], vec[:, VBI:VBI + LC], 0.5, None, ALU.mult).then_inc(setup_done, 1)

            dve.wait_ge(const_in, 16 * N_CONST)
            chain.restart()
            with dve.Fori(0, NB - 1) as b:
                mixers(b, False)
                ffn(b, False)
                head(b + 1, False, b)
                chain.restart()
            b = NB - 1
            mixers(b, True)
            ffn(b, True)
            y_rstd(b, True)
            dve.wait_ge(state_out, 16 * N_STATE_OUT)
            for m in range(QB):
                y_scale(b, m)
            dve.wait_ge(smp_pe, 8)
            y_out[0].wait(dve, b, 2)
            for h in range(2):
                ins = STT(out=y_tok[0:NS, 0, h * 512:(h + 1) * 512], in0=S[h][0:NS, :],
                          scalar=rstd_t[0:NS, QB:QB + 1], in1=gfin[0:NS, h * 512:(h + 1) * 512],
                          op0=ALU.mult, op1=ALU.mult)
            ins.then_inc(smp_dve, 1)


(SMP_DVE_L, SMP_DVE_Q, SMP_DVE_S, SMP_DVE_P, SMP_DVE_PT, SMP_DVE_XC, SMP_DVE_AT, SMP_DVE_M, SMP_DVE_GI,
 SMP_DVE_OUTC, SMP_DVE_MIXF, SMP_DVE_MIX, SMP_DVE_OUT, SMP_DVE_Y) = range(1, 15)


def kernel(x_prompt, x_sample, cache_k, cache_v, state_conv, state_h, g_mix, w_in, b_in, attn_sinks, conv_w,
           conv_b, w_a, b_a, w_i, b_i, lam, w_out, b_out, g_ffn, w_ffn_in, w_ffn_out, g_final):
    import numpy as np
    import concourse.bacc as bacc
    from concourse.bass_utils import run_bass_kernel_spmd

    f = np.float32
    A = {k: np.asarray(v) for k, v in dict(
        x_prompt=x_prompt, x_sample=x_sample, cache_k=cache_k, cache_v=cache_v, state_conv=state_conv,
        state_h=state_h, w_a=w_a, w_i=w_i).items()}
    DM = A["x_prompt"].shape[2]
    SEQ = A["x_prompt"].shape[1]
    DB, DT = A["x_sample"].shape[:2]
    KT = DM // P
    wi, wo = np.asarray(w_in)[0], np.asarray(w_out)[0]
    fi, fo = np.asarray(w_ffn_in)[0], np.asarray(w_ffn_out)[0]
    FF = fo.shape[0]
    NF = FF // P
    sinks = np.asarray(attn_sinks)[0]
    NH = sinks.shape[0]
    JT = NH // 2
    QE = NH * HEAD
    KE, VE = QE + 2 * HEAD, QE + 4 * HEAD
    LRU = A["state_h"].shape[2]
    LC = LRU // P
    cols = [np.arange(QE, KE), np.arange(KE, VE)]
    for j in range(JT):
        cols.append(np.concatenate([np.arange(j * HEAD, (j + 1) * HEAD),
                                    np.arange((j + JT) * HEAD, (j + JT + 1) * HEAD)]))
    for kind, c in branch_order(LC):
        cols.append(VE + (LRU if kind == "y" else 0) + c * P + np.arange(P))
    packed = []

    def pack(w):
        k = w.shape[0] // P
        u = np.zeros((P, KT * P), f)
        u[:, 0:k * P] = w.reshape(k, P, P).transpose(1, 0, 2).reshape(P, k * P)
        packed.append(u)

    for c in cols:
        pack(wi[:, c])
    for m in range(KT):
        pack(wo[:, m * P:(m + 1) * P])
    n = -(-NF // KT)
    at = 0
    for i in range(n):
        nf = NF // n + (i < NF % n)
        for t in range(at, at + nf):
            pack(fi[:, t * P:(t + 1) * P])
            pack(fi[:, FF + t * P:FF + (t + 1) * P])
        for m in range(KT):
            pack(fo[at * P:(at + nf) * P, m * P:(m + 1) * P])
        at += nf
    A["units"] = np.stack(packed)

    def tiles(a):
        a = np.asarray(a)
        return a.reshape(-1, P).T

    half = np.arange(P) // HEAD
    qs = np.stack([2.0 ** (j + JT * half + 1) / 8 for j in range(JT)], 1).astype(f)
    bi = np.asarray(b_in)[0]
    A["vecs"] = np.ascontiguousarray(np.concatenate(
        [np.stack([bi[c] for c in cols], 1), tiles(g_mix), tiles(b_out), tiles(g_ffn), tiles(conv_w),
         tiles(conv_b), tiles(b_a), tiles(b_i), tiles(lam), qs], 1))
    A["sinks_p"] = np.ascontiguousarray(np.broadcast_to(sinks, (P, NH)))
    jr = np.arange(P) // DT % JT
    tr = np.arange(P) % DT
    br = np.arange(P) // (DT * JT)
    A["sinks_s"] = np.ascontiguousarray(np.stack([sinks[jr], sinks[JT + jr]], 1))
    A["g_fin"] = np.ascontiguousarray(np.broadcast_to(np.asarray(g_final), (P, DM)))
    A["ident_in"] = np.eye(P, dtype=f)
    FAR = -1e30 * 2.0 ** NH
    i, j = np.arange(P)[:, None], np.arange(2 * P)[None]
    d = P + i - j
    A["dist_in"] = np.stack([np.where((d >= 0) & (d < P), -d, FAR),
                             np.where((d >= 0) & (d < P) & (j >= P), -d, FAR)]).astype(f)
    dc = P + tr[:, None] - np.arange(P)[None]
    tn, bn = np.arange(DB * DT)[None] // DB, np.arange(DB * DT)[None] % DB
    dn = tr[:, None] - tn
    A["dist_s_in"] = np.concatenate([np.where((dc >= 0) & (dc < P), -dc, FAR),
                                     np.where((dn >= 0) & (bn == br[:, None]), -dn, FAR)], 1).astype(f)
    A["per_row"] = np.stack([2.0 ** -(jr + 1.0), 2.0 ** -(JT + jr + 1.0), 0 * jr, 0 * jr], 1).astype(f)

    outs = [("y_p", (1, SEQ, DM)), ("y_s", (DB, DT, DM)), ("nk_p", (1, 1, WINDOW, 2, HEAD)),
            ("nv_p", (1, 1, WINDOW, 2, HEAD)), ("nc_p", (1, 1, CONV_W - 1, LRU)), ("nh_p", (1, 1, LRU)),
            ("nk_s", (1, DB, WINDOW, 2, HEAD)), ("nv_s", (1, DB, WINDOW, 2, HEAD)),
            ("nc_s", (1, DB, CONV_W - 1, LRU)), ("nh_s", (1, DB, LRU))]
    nc = bacc.Bacc("TRN2", target_bir_lowering=False, num_devices=1)
    order = ["x_prompt", "x_sample", "cache_k", "cache_v", "state_conv", "state_h", "units", "vecs", "w_a", "w_i",
             "sinks_p", "sinks_s", "g_fin", "ident_in", "dist_in", "dist_s_in", "per_row"]
    arrays, args = {}, []
    for name in order:
        a = np.ascontiguousarray(A[name])
        arrays[f"in_{name}"] = a
        args.append(nc.dram_tensor(f"in_{name}", a.shape, mybir.dt.from_np(a.dtype), kind="ExternalInput").ap())
    for name, shape in outs:
        args.append(nc.dram_tensor(f"out_{name}", shape, F32, kind="ExternalOutput").ap())
    hymba_layer(nc, *args, FF)
    r = run_bass_kernel_spmd(nc, [arrays], core_ids=[0])
    return tuple(r.results[0][f"out_{name}"] for name, _ in outs)
```
